# Optimizing a Trainium2 kernel written in Bass

```python
import math
import jax
import jax.numpy as jnp
from jax import lax
import numpy as np

D_MODEL = 1024
BATCH = 1
SEQ = 256
DEPTH = 2

GRID_W = 64
CTX_LEN = 256
N_MIXERS = 2
NORM_EPS = 1e-6

MLA_HEADS = 16
Q_LORA = 384
KV_LORA = 256
QK_NOPE = 64
QK_ROPE = 32
V_DIM = 64
ROPE_BASE = 10000.0
Q_BLOCK = 128

HY_ORDER = 2
HY_EMB = 33
HY_BANDS = (HY_EMB - 1) // 2
HY_FFN = 64
HY_SHORT = 3
HY_TARGET = 1e-2
HY_FAST_PCT = 0.3
HY_SLOW_PCT = 1.5

PEER_HEADS = 8
PEER_NK = 128
PEER_EXPERTS = PEER_NK * PEER_NK
PEER_DK = 256
PEER_TOPK = 16
PEER_CHUNK = 512

kernel_name = "hybrid_mla_hyena_peer_diffusion_block"

def rmsnorm(x, g):
    xf = x.astype(jnp.float32)
    y = xf * lax.rsqrt(jnp.mean(xf * xf, axis=-1, keepdims=True) + NORM_EPS)
    return y.astype(x.dtype) * g

def modulate(h, shift, scale):
    return h * (1 + scale) + shift

def axial_rope_tables(n_tokens, dtype):
    t = jnp.arange(n_tokens, dtype=jnp.int32)
    row = (t // GRID_W).astype(jnp.float32)
    col = (t % GRID_W).astype(jnp.float32)
    n_freq = QK_ROPE // 4
    inv = ROPE_BASE ** (-jnp.arange(n_freq, dtype=jnp.float32) / n_freq)
    ar = row[:, None] * inv
    ac = col[:, None] * inv
    ang = jnp.concatenate([ar, ar, ac, ac], axis=-1)[:, None, :]
    return jnp.cos(ang).astype(dtype), jnp.sin(ang).astype(dtype)

def _rotate_half(x):
    x1, x2 = jnp.split(x, 2, axis=-1)
    return jnp.concatenate([-x2, x1], axis=-1)

def apply_axial_rope(x, cos, sin):
    xr, xc = jnp.split(x, 2, axis=-1)
    rot = jnp.concatenate([_rotate_half(xr), _rotate_half(xc)], axis=-1)
    return x * cos + rot * sin

def mla_queries(lat, g_q, w_uq, rope):
    B, L, _ = lat.shape
    cq = rmsnorm(lat[..., :Q_LORA], g_q)
    q = (cq @ w_uq).reshape(B, L, MLA_HEADS, QK_NOPE + QK_ROPE)
    q_nope, q_rope = q[..., :QK_NOPE], q[..., QK_NOPE:]
    if rope is not None:
        q_rope = apply_axial_rope(q_rope, *rope)
    return jnp.concatenate([q_nope, q_rope], axis=-1)

def mla_keys_values(lat, g_kv, w_ukv, rope):
    B, L, _ = lat.shape
    ckv = rmsnorm(lat[..., Q_LORA:Q_LORA + KV_LORA], g_kv)
    kv = (ckv @ w_ukv).reshape(B, L, MLA_HEADS, QK_NOPE + V_DIM)
    k_rope = lat[..., Q_LORA + KV_LORA:][:, :, None, :]
    if rope is not None:
        k_rope = apply_axial_rope(k_rope, *rope)
    k = jnp.concatenate([kv[..., :QK_NOPE], jnp.broadcast_to(k_rope, (B, L, MLA_HEADS, QK_ROPE))], axis=-1)
    return k, kv[..., QK_NOPE:]

def block_attention(q, k, v):
    B, L, H, dq = q.shape
    nb = L // Q_BLOCK
    qb = q.reshape(B, nb, Q_BLOCK, H, dq).transpose(1, 0, 2, 3, 4)
    scale = dq ** -0.5

    def one_block(qi):
        s = jnp.einsum('bqhd,bkhd->bhqk', qi, k).astype(jnp.float32) * scale
        p = jax.nn.softmax(s, axis=-1).astype(v.dtype)
        return jnp.einsum('bhqk,bkhd->bqhd', p, v)

    o = lax.map(one_block, qb)
    return o.transpose(1, 0, 2, 3, 4).reshape(B, L, H * v.shape[-1])

def hyena_filters(L, w1, b1, w2, b2, w3, b3, w4, sin_freq, deltas):
    f32 = jnp.float32
    t = jnp.linspace(0.0, 1.0, L, dtype=f32)[:, None]
    w = (2.0 * math.pi / L) * jnp.arange(L, dtype=f32)[:, None]
    f = jnp.linspace(1e-4, HY_BANDS - 1, HY_BANDS, dtype=f32)[None, :]
    z = jnp.concatenate([t, jnp.cos(f * w), -jnp.sin(f * w)], axis=-1).astype(w1.dtype)
    a = jnp.sin(sin_freq * (z @ w1 + b1))
    a = jnp.sin(sin_freq * (a @ w2 + b2))
    a = jnp.sin(sin_freq * (a @ w3 + b3))
    d = w4.shape[-1] // (2 * HY_ORDER)
    hf = (a @ w4).astype(f32).reshape(L, HY_ORDER, 2, d)
    decay = jnp.exp(-t[:, :, None] * jnp.abs(deltas.astype(f32)))
    hf = hf * decay[:, :, None, :]
    fwd, bwd = hf[:, :, 0], hf[:, :, 1]
    k = jnp.concatenate([fwd, jnp.zeros((1, HY_ORDER, d), f32), bwd[:0:-1]], axis=0)
    k = k / jnp.sum(jnp.abs(k), axis=0, keepdims=True)
    return jnp.fft.rfft(k, axis=0)

def fft_long_conv(u, kf):
    L = u.shape[1]
    U = jnp.fft.rfft(u.astype(jnp.float32), n=2 * L, axis=1)
    y = jnp.fft.irfft(U * kf[None], n=2 * L, axis=1)[:, :L]
    return y.astype(u.dtype)

def hyena_mixer(h, w_in, conv_w, conv_b, w1, b1, w2, b2, w3, b3, w4, sin_freq, deltas, bias, w_out):
    L = h.shape[1]
    p = h @ w_in
    pad = HY_SHORT // 2
    pp = jnp.pad(p, ((0, 0), (pad, pad), (0, 0)))
    acc = conv_b
    for tap in range(HY_SHORT):
        acc = acc + conv_w[tap] * pp[:, tap:tap + L]
    parts = jnp.split(acc, HY_ORDER + 1, axis=-1)
    z = parts[0]
    kf = hyena_filters(L, w1, b1, w2, b2, w3, b3, w4, sin_freq, deltas)
    for n in range(HY_ORDER):
        z = parts[n + 1] * (fft_long_conv(z, kf[:, n]) + bias[n] * z)
    return z @ w_out

def peer(h, wq, keys, u, v):
    shp = h.shape
    D = shp[-1]
    xt = h.reshape(-1, D)
    T = xt.shape[0]
    chunk = math.gcd(T, PEER_CHUNK)

    def one_chunk(xc):
        q = (xc @ wq).reshape(chunk, PEER_HEADS, 2, PEER_DK // 2)
        s = jnp.einsum('thpk,hpnk->thpn', q, keys).astype(jnp.float32)
        sv, si = lax.top_k(s, PEER_TOPK)
        cand = (sv[:, :, 0, :, None] + sv[:, :, 1, None, :]).reshape(chunk, PEER_HEADS, PEER_TOPK * PEER_TOPK)
        cidx = (si[:, :, 0, :, None] * PEER_NK + si[:, :, 1, None, :]).reshape(chunk, PEER_HEADS, PEER_TOPK * PEER_TOPK)
        fs, fi = lax.top_k(cand, PEER_TOPK)
        eidx = jnp.take_along_axis(cidx, fi, axis=-1)
        g = jax.nn.softmax(fs, axis=-1).astype(xc.dtype)
        act = jax.nn.gelu(jnp.einsum('td,thkd->thk', xc, u[eidx]), approximate=False)
        return jnp.einsum('thk,thkd->td', g * act, v[eidx])

    out = lax.map(one_chunk, xt.reshape(T // chunk, chunk, D))
    return out.reshape(shp)

def setup_inputs(seed: int = 0) -> dict:
    key = jax.random.key(seed)
    ks = iter(jax.random.split(key, 48))

    def nrm(shape, scale):
        return jax.random.normal(next(ks), shape, jnp.float32) * scale

    def gain(shape):
        return 1.0 + nrm(shape, 0.02)

    D = D_MODEL
    n_att = (DEPTH + N_MIXERS - 1) // N_MIXERS
    n_hy = DEPTH // N_MIXERS
    decay_lo = -math.log(HY_TARGET) / HY_SLOW_PCT
    decay_hi = -math.log(HY_TARGET) / HY_FAST_PCT
    deltas = jnp.linspace(decay_lo, decay_hi, D, dtype=jnp.float32)
    return {
        "x": nrm((BATCH, SEQ, D), 1.0),
        "c": nrm((BATCH, D), 1.0),
        "ctx": nrm((BATCH, CTX_LEN, D), 1.0),
        "c_ctx": nrm((D,), 1.0),
        "mod_w": nrm((DEPTH, D, 6 * D), 0.5 * D ** -0.5),
        "mod_b": nrm((DEPTH, 6 * D), 0.02),
        "norm_mix_g": gain((DEPTH, D)),
        "norm_ffn_g": gain((DEPTH, D)),
        "final_g": gain((D,)),
        "mla_w_dkv": nrm((n_att, D, Q_LORA + KV_LORA + QK_ROPE), D ** -0.5),
        "mla_q_norm_g": gain((n_att, Q_LORA)),
        "mla_w_uq": nrm((n_att, Q_LORA, MLA_HEADS * (QK_NOPE + QK_ROPE)), Q_LORA ** -0.5),
        "mla_kv_norm_g": gain((n_att, KV_LORA)),
        "mla_w_ukv": nrm((n_att, KV_LORA, MLA_HEADS * (QK_NOPE + V_DIM)), KV_LORA ** -0.5),
        "mla_w_o": nrm((n_att, MLA_HEADS * V_DIM, D), (MLA_HEADS * V_DIM) ** -0.5),
        "hy_w_in": nrm((n_hy, D, (HY_ORDER + 1) * D), D ** -0.5),
        "hy_conv_w": nrm((n_hy, HY_SHORT, (HY_ORDER + 1) * D), HY_SHORT ** -0.5),
        "hy_conv_b": nrm((n_hy, (HY_ORDER + 1) * D), 0.02),
        "hy_w1": nrm((n_hy, HY_EMB, HY_FFN), HY_EMB ** -0.5),
        "hy_b1": nrm((n_hy, HY_FFN), 0.1),
        "hy_w2": nrm((n_hy, HY_FFN, HY_FFN), HY_FFN ** -0.5),
        "hy_b2": nrm((n_hy, HY_FFN), 0.1),
        "hy_w3": nrm((n_hy, HY_FFN, HY_FFN), HY_FFN ** -0.5),
        "hy_b3": nrm((n_hy, HY_FFN), 0.1),
        "hy_w4": nrm((n_hy, HY_FFN, HY_ORDER * 2 * D), HY_FFN ** -0.5),
        "hy_sin_freq": gain((n_hy, HY_FFN)),
        "hy_deltas": deltas * gain((n_hy, HY_ORDER, D)),
        "hy_bias": nrm((n_hy, HY_ORDER, D), 1.0),
        "hy_w_out": nrm((n_hy, D, D), D ** -0.5),
        "peer_wq": nrm((DEPTH, D, PEER_HEADS * PEER_DK), D ** -0.5),
        "peer_keys": nrm((DEPTH, PEER_HEADS, 2, PEER_NK, PEER_DK // 2), (PEER_DK // 2) ** -0.5),
        "peer_u": nrm((DEPTH, PEER_EXPERTS, D), D ** -0.5),
        "peer_v": nrm((DEPTH, PEER_EXPERTS, D), 1.0),
    }

def reference(x, c, ctx, c_ctx, mod_w, mod_b, norm_mix_g, norm_ffn_g, final_g,
              mla_w_dkv, mla_q_norm_g, mla_w_uq, mla_kv_norm_g, mla_w_ukv, mla_w_o,
              hy_w_in, hy_conv_w, hy_conv_b, hy_w1, hy_b1, hy_w2, hy_b2, hy_w3, hy_b3, hy_w4,
              hy_sin_freq, hy_deltas, hy_bias, hy_w_out,
              peer_wq, peer_keys, peer_u, peer_v):
    S = x.shape[1]
    rope = axial_rope_tables(S, x.dtype)
    sc = jax.nn.silu(c)
    sc_ctx = jax.nn.silu(c_ctx)
    for i in range(DEPTH):
        j = i // N_MIXERS
        ctx_read_later = any(l % N_MIXERS == 0 for l in range(i + 1, DEPTH))
        m_lat = jnp.split((sc @ mod_w[i] + mod_b[i])[:, None, :], 6, axis=-1)
        m_ctx = jnp.split(sc_ctx @ mod_w[i] + mod_b[i], 6, axis=-1)

        hl = modulate(rmsnorm(x, norm_mix_g[i]), m_lat[0], m_lat[1])
        if i % N_MIXERS == 0:
            hc = modulate(rmsnorm(ctx, norm_mix_g[i]), m_ctx[0], m_ctx[1])
            lat_l = hl @ mla_w_dkv[j]
            lat_c = hc @ mla_w_dkv[j]
            kl, vl = mla_keys_values(lat_l, mla_kv_norm_g[j], mla_w_ukv[j], rope)
            kc, vc = mla_keys_values(lat_c, mla_kv_norm_g[j], mla_w_ukv[j], None)
            ql = mla_queries(lat_l, mla_q_norm_g[j], mla_w_uq[j], rope)
            k_all = jnp.concatenate([kl, kc], axis=1)
            v_all = jnp.concatenate([vl, vc], axis=1)
            yl = block_attention(ql, k_all, v_all) @ mla_w_o[j]
            if ctx_read_later:
                qc = mla_queries(lat_c, mla_q_norm_g[j], mla_w_uq[j], None)
                yc = block_attention(qc, kc, vc) @ mla_w_o[j]
        else:
            hy = (hy_w_in[j], hy_conv_w[j], hy_conv_b[j], hy_w1[j], hy_b1[j], hy_w2[j], hy_b2[j],
                  hy_w3[j], hy_b3[j], hy_w4[j], hy_sin_freq[j], hy_deltas[j], hy_bias[j], hy_w_out[j])
            yl = hyena_mixer(hl, *hy)
            if ctx_read_later:
                hc = modulate(rmsnorm(ctx, norm_mix_g[i]), m_ctx[0], m_ctx[1])
                yc = hyena_mixer(hc, *hy)
        x = x + m_lat[2] * yl
        if ctx_read_later:
            ctx = ctx + m_ctx[2] * yc

        hl = modulate(rmsnorm(x, norm_ffn_g[i]), m_lat[3], m_lat[4])
        x = x + m_lat[5] * peer(hl, peer_wq[i], peer_keys[i], peer_u[i], peer_v[i])
        if ctx_read_later:
            hc = modulate(rmsnorm(ctx, norm_ffn_g[i]), m_ctx[3], m_ctx[4])
            ctx = ctx + m_ctx[5] * peer(hc, peer_wq[i], peer_keys[i], peer_u[i], peer_v[i])
    return rmsnorm(x, final_g)


_drawn_inputs = setup_inputs


def setup_inputs(seed=0):
    import zlib

    import numpy as np

    out = dict(_drawn_inputs(seed))
    spreads = {}
    factors = {'norm_mix_g': 2.755,
     'final_g': 3.009,
     'mla_q_norm_g': 5.304,
     'mla_kv_norm_g': 3.975,
     'hy_conv_b': 2.879,
     'hy_sin_freq': 8.0}
    for name, (base, spread) in spreads.items():
        noise = np.random.default_rng([zlib.crc32(name.encode()), seed]).standard_normal(out[name].shape)
        drawn = base * np.exp(spread * noise) if base else spread * noise
        out[name] = jnp.asarray(drawn.astype(out[name].dtype))
    for name, factor in factors.items():
        out[name] = (out[name] * factor).astype(out[name].dtype)
    return out
```

```python
from contextlib import ExitStack, contextmanager
import math

import numpy as np
import concourse.bass as bass
from concourse import mybir
from concourse.alu_op_type import AluOpType as ALU

ACT = mybir.ActivationFunctionType
F32 = mybir.dt.float32
F32R = mybir.dt.float32r
U32 = mybir.dt.uint32
AX = mybir.AxisListType

P = 128
D = 1024
DC = D // P
T = 256
TT = T // P
EPS = 1e-6
HEADS, NOPE, ROPE, VD = 16, 64, 32, 64
QK = NOPE + ROPE
QL, KVL = 384, 256
QC, KC = QL // P, KVL // P
DKV = QC + KC + 1
PH, NK, TOPK = 8, 128, 16
HP = 2 * PH
ORDER, FFN, EMB = 2, 64, 33
RAW, WSL = 4, 2
MODS = 6 * DC
SCALE = QK ** -0.5
LOWEST = -3.4028234663852886e38
MAGIC = 12582912.0
TWO_PI_1, TWO_PI_2 = 6.28125, 0.0019340515136718750
TWO_PI_3 = 2 * math.pi - TWO_PI_1 - TWO_PI_2

COLS = {}
_at = 0
for _n, _w in (("mix_g", 2 * DC), ("ffn_g", 2 * DC), ("final_g", DC), ("q_g", QC), ("kv_g", KC), ("conv_w", 9 * DC),
               ("conv_b", 3 * DC), ("hy_bias", ORDER * DC), ("mod_b", 2 * MODS), ("neg_t", TT)):
    COLS[_n] = (_at, _at + _w)
    _at += _w
NCOLS = _at

STREAM = [("dkv", DKV), ("wo", DC), ("wq0", HP), ("u0", NK), ("v0", NK), ("win", 3 * DC), ("wout", DC),
          ("wq1", HP), ("u1", NK), ("v1", NK)]
FIRST = {}
_at = 0
for _n, _w in STREAM:
    FIRST[_n] = _at
    _at += _w

U_BESIDE = 22


class Chain:

    def __init__(self, eng, sem):
        self.eng, self.sem, self.n, self.i, self.per, self.k = eng, sem, 0, None, 0, 0

    def link(self, ins):
        ins.then_inc(self.sem, 1)
        if self.i is None:
            self.n += 1
            self.eng.wait_ge(self.sem, self.n)
        else:
            self.k += 1
            self.eng.wait_ge(self.sem, self.i * self.per + (self.n + self.k))

    @contextmanager
    def loop(self, count, per):
        with self.eng.Fori(0, count) as i:
            self.i, self.per, self.k = i, per, 0
            yield i
            assert self.k == per, (self.k, per)
        self.i = None
        self.n += count * per


def build(nc, a, out):
    with ExitStack() as ctx:
        def sb(name, shape, dt=F32):
            return ctx.enter_context(nc.sbuf_tensor(name, shape, dt))

        sems = {}

        def sem(name):
            if name not in sems:
                sems[name] = ctx.enter_context(nc.semaphore(name))
            return sems[name]

        x = sb("x", [P, DC, T])
        h_hi = sb("h_hi", [P, DC, T], F32R)
        h_lo = sb("h_lo", [P, DC, T], F32R)
        raw = sb("raw", [P, RAW, D])
        w_hi = sb("w_hi", [P, WSL, D], F32R)
        w_lo = sb("w_lo", [P, WSL, D], F32R)
        small = sb("small", [P, 2048])
        silu = sb("silu", [P, D])
        cols = sb("cols", [P, NCOLS])
        mod = sb("mod", [P, 2 * MODS])
        modc = sb("modc", [P, 2 * DC])
        gain = sb("gain", [P, 5 * DC])
        sel_i = sb("sel_i", [P, T])
        sel_j = sb("sel_j", [P, T])
        sel_g = sb("sel_g", [P, T])
        ident = sb("ident", [P, P])
        iota = sb("iota", [P, P])
        ones = sb("ones", [P, P])
        zero = sb("zero", [P, 8])
        rstd = sb("rstd", [P, 512])
        arena_off = (nc.sbuf_base + 31) // 32 * 32
        arena = sb("arena", [P, NK * T])
        ps = ctx.enter_context(nc.psum_tensor("ps", [P, 8, 512], F32))

        def cut(at, *shape):
            n = int(np.prod(shape))
            v = arena[:, at:at + n]
            if len(shape) == 1:
                return v
            names = "abcde"[:len(shape)]
            return v.rearrange(f"p ({' '.join(names)}) -> p {' '.join(names)}", **{k: s for k, s in zip(names[1:], shape[1:])})

        def scut(at, *shape):
            n = int(np.prod(shape))
            v = small[:, at:at + n]
            if len(shape) == 1:
                return v
            names = "abcde"[:len(shape)]
            return v.rearrange(f"p ({' '.join(names)}) -> p {' '.join(names)}", **{k: s for k, s in zip(names[1:], shape[1:])})

        def col(name, k, rows=P):
            return cols[0:rows, COLS[name][0] + k:COLS[name][0] + k + 1]

        at = 0
        def take(*shape):
            nonlocal at
            v = cut(at, *shape)
            at += int(np.prod(shape))
            return v
        cx = take(DC, T)
        tmp = take(DC, T)
        silu_c = take(D)
        junk = take(D)
        q_heads = cut(0, HEADS, T)
        lat = take(DKV, 512)
        w_uq = take(QC, HEADS, P)
        v_keys = w_uq.rearrange("p a b c -> p (a b c)")[:, 0:4 * D].rearrange("p (a b) -> p a b", a=4)
        w_uk = take(KC, HEADS // 2, P)
        w_uv = take(KC, D)
        cq = take(QC, T)
        ckv = take(KC, 512)
        rope = take(T)
        rope_s = take(2, T)
        rope_c = take(2, T)
        k_heads = take(4, 512)
        c_at = at
        probs = take(2, 512)
        probs_t = take(2, 4, T)
        take(2 * DC * T - 1024 - 2048)
        smax = take(64)
        assert at <= NK * T, at
        c_hi = nc.alloc_sbuf_tensor_at("c_hi", [P, DC, T], F32R, offset=arena_off + 4 * c_at)
        c_lo = nc.alloc_sbuf_tensor_at("c_lo", [P, DC, T], F32R, offset=arena_off + 4 * (c_at + DC * T))

        tmp_flat = tmp.rearrange("p a b -> p (a b)")
        squares = probs_t.rearrange("p a b c -> p (a b c)")
        sq_q = squares[:, 0:QC * T].rearrange("p (a b) -> p a b", a=QC)
        sq_k = squares[:, QC * T:QC * T + KC * 512].rearrange("p (a b) -> p a b", a=KC)

        at = 0
        hf = take(TT, ORDER, 2, D)
        conv = cut(0, 3 * DC, T)
        k_re = take(TT, ORDER, D)
        k_im = take(TT, ORDER, D)
        hf_abs = cut(TT * ORDER * 2 * D, TT, ORDER, 2, D)
        w4_at = at
        w4 = take(4 * D)
        delta = take(ORDER, D)
        decay = take(ORDER, D)
        hf_diff = cut(w4_at, TT, ORDER, D)
        u_re = cut(w4_at, TT, D)
        u_im = cut(w4_at + 2 * D, TT, D)
        y_re = cut(w4_at + 4 * D, TT, D)
        y_im = cut(w4_at + 6 * D, TT, D)
        tr_z = take(TT, D)
        zz = take(DC, T)
        dft = take(4, TT, T)
        ctmp = tr_z
        pad = take(2, 258)
        arg = take(3, T)
        zfeat = take(T)
        w1 = take(FFN)
        w23 = take(2, FFN)
        fcol = take(4)
        inv_norm = take(ORDER * DC)
        hrt = cut(3 * DC * T, 2, T)
        assert at <= NK * T, at

        hf_all = cut(0, TT * ORDER * 2 * D)
        hf_abs5 = hf_abs
        hf_abs = cut(TT * ORDER * 2 * D, TT * ORDER * 2 * D)
        hf_sum = hf[:, :, :, 0, :]

        acts = cut(0, NK, T)
        q_all = cut(88 * T, HP, T)
        keys = cut(104 * T, HP, P)
        scores = cut(112 * T, TT, HP, P)
        fs = scut(0, TT, PH * TOPK)
        fi_i = scut(256, TT, PH * TOPK)
        fi_j = scut(512, TT, PH * TOPK)
        sv = scut(768, 2, TOPK)
        si_u = scut(800, 2, TOPK).bitcast(U32)
        si_f = scut(832, 2, TOPK)
        cand = scut(864, TOPK, TOPK)
        cand_flat = scut(864, TOPK * TOPK)
        eq = scut(1120, TOPK, TOPK)
        eq2 = scut(1376, TOPK, TOPK)
        fi_u = scut(1632, TOPK).bitcast(U32)
        fa_u = scut(1648, 2, TOPK).bitcast(U32)
        fa_f = scut(1680, 2, TOPK)
        fsum = scut(1712, TT * PH)
        fs_one = scut(1984, TOPK)
        pair = scut(1728, 2, P)
        oh_i = scut(0, 2, 4, P)
        oh_j = scut(1024, 2, 4, P)
        mod_raw = scut(0, 2, D)
        scores_v = cut(112 * T, TT * PH, 2 * P)
        fs_v = scut(0, TT * PH, TOPK)
        fi_i_v = scut(256, TT * PH, TOPK)
        fi_j_v = scut(512, TT * PH, TOPK)
        got = sb("got", [P, 8])

        block = ctx.enter_context(nc.Block())

        def raw_sem(n):
            return sem(f"raw_landed_{n % RAW}")

        def load_chunk(sp, name, index, n, i=0):
            src = a[name]
            if n >= RAW:
                sp.wait_ge(sem("w_lo_ready"), i * RAW + (n - RAW + 1))
            sp.dma_start(raw[:, n % RAW, :], src[bass.ds(index, 1), :, :].rearrange("o p n -> p (o n)")).then_inc(raw_sem(n), 16)

        def hi_chunk(act, n, i=0):
            act.wait_ge(raw_sem(n), i * 16 + 16 * (n // RAW + 1))
            if n >= WSL:
                act.wait_ge(sem("w_used"), i * RAW + (n - WSL + 1))
            act.activation(w_hi[:, n % WSL, :], raw[:, n % RAW, :], ACT.Copy).then_inc(sem("w_hi_ready"), 1)

        def lo_chunk(dve, n, i=0):
            dve.wait_ge(sem("w_hi_ready"), i * RAW + (n + 1))
            dve.tensor_tensor(w_lo[:, n % WSL, :], raw[:, n % RAW, :], w_hi[:, n % WSL, :], ALU.subtract)\
               .then_inc(sem("w_lo_ready"), 1)

        def product(pe, n, outs, i=0):
            pe.wait_ge(sem("w_lo_ready"), i * RAW + (n + 1))
            s = n % WSL
            for o, rh, rl in outs:
                for c in range(DC):
                    wh, wl = w_hi[:, s, c * P:(c + 1) * P], w_lo[:, s, c * P:(c + 1) * P]
                    pe.matmul(o, wh, rh[:, c, :], start=(c == 0), stop=False)
                    pe.matmul(o, wh, rl[:, c, :], start=False, stop=False)
                    last = pe.matmul(o, wl, rh[:, c, :], start=False, stop=(c == DC - 1))
            last.then_inc(sem("w_used"), 1)

        def multiplied(eng, n, i=0):
            eng.wait_ge(sem("w_used"), i * RAW + (n + 1))

        def mod_col(l, part, c):
            k = l * MODS + part * DC + c
            return mod[:, k:k + 1]

        @block.sync
        def _(sp):
            for name, count in STREAM:
                n0 = FIRST[name]
                if count % RAW or n0 < RAW:
                    for k in range(count):
                        load_chunk(sp, name, k, n0 + k)
                else:
                    with sp.Fori(0, count // RAW) as i:
                        for u in range(RAW):
                            load_chunk(sp, name, i * RAW + u, n0 + u, i)
            sp.wait_ge(sem("result_ready"), 1)
            sp.dma_start(out, x[:, :, :]).then_inc(sem("stored"), 16)
            sp.wait_ge(sem("stored"), 16)

        @block.gpsimd
        def _(pool):
            def load_mod(k):
                if k >= 2:
                    pool.wait_ge(sem("mod_used"), k - 1)
                pool.dma_start(mod_raw[:, k % 2, :], a["mod_w"][k]).then_inc(sem(f"mod_landed_{k % 2}"), 16)

            pool.dma_start(silu[:, :], a["c"]).then_inc(sem("c_landed"), 16)
            pool.dma_start(silu_c, a["c_ctx"]).then_inc(sem("c_landed"), 16)
            pool.dma_start(cols[:, :], a["cols"]).then_inc(sem("cols_landed"), 16)
            pool.dma_start(x[:, :, :], a["x"]).then_inc(sem("x_landed"), 16)
            pool.dma_start(cx, a["ctx"]).then_inc(sem("x_landed"), 16)
            pool.memset(ones[:, :], 1.0).then_inc(sem("ones_ready"), 1)
            pool.dma_start(ident[:, :], a["ident"]).then_inc(sem("table_landed"), 16)
            pool.dma_start(iota[:, :], a["iota"]).then_inc(sem("table_landed"), 16)
            for k in range(2 * DC):
                load_mod(k)
            pool.dma_start(rope, a["rope"]).then_inc(sem("attn_landed"), 16)
            pool.dma_start(w_uq, a["w_uq"]).then_inc(sem("attn_landed"), 16)
            pool.dma_start(w_uk, a["w_uk"]).then_inc(sem("attn_landed"), 16)
            pool.dma_start(w_uv, a["w_uv"]).then_inc(sem("attn_landed"), 16)
            for k in range(2 * DC, MODS):
                load_mod(k)
            for l in range(2):
                pool.wait_ge(sem("x_ready"), 1 + 2 * l)
                pool.dma_start(keys, a["keys"][l]).then_inc(sem("keys_landed"), 16)
                if l == 0:
                    pool.wait_ge(sem("gates_done_0"), 1)
                    for k in range(MODS, 2 * MODS):
                        load_mod(k)
                    pool.wait_ge(sem("x_ready"), 2)
                    for dst, src in ((w4[0:FFN, :], "w4"), (delta, "delta"), (dft, "dft"), (zfeat[0:EMB, :], "zfeat"),
                                     (w1[0:EMB, :], "w1"), (w23[0:FFN, :, :], "w23"), (fcol[0:FFN, :], "fcol")):
                        pool.dma_start(dst, a[src]).then_inc(sem("hyena_landed"), 16)

        @block.scalar
        def _(act):
            def square(k, src, dst):
                act.activation(dst, src, ACT.Square).then_inc(sem("square_ready"), 1)

            def root(k, width, features=D):
                act.wait_ge(sem("sum_ready"), k + 1)
                act.activation(rstd[:, 0:width], ps[:, 0, 0:width], ACT.Sqrt, bias=zero[:, 1:2],
                               scale=1.0 / features).then_inc(sem("root_ready"), 1)

            def split(s, src, hi):
                act.wait_ge(sem("to_split"), s + 1)
                act.activation(hi[:, :, :], src, ACT.Copy).then_inc(sem("h_hi_ready"), 1)

            act.wait_ge(sem("c_landed"), 32)
            act.activation(tmp_flat[:, 0:D], silu[:, :], ACT.Exp, scale=-1.0).then_inc(sem("c_exp"), 1)
            act.activation(tmp_flat[:, D:2 * D], silu_c, ACT.Exp, scale=-1.0).then_inc(sem("c_exp"), 1)

            act.wait_ge(sem("x_landed"), 32)
            act.wait_ge(sem("silu_ready"), 1)
            square(0, x[:, :, :], tmp)
            root(0, T)
            split(0, tmp, h_hi)
            act.wait_ge(sem("h_lo_ready"), 1)
            square(1, cx, tmp)
            root(1, T)
            split(1, tmp, c_hi)

            def lat_copy(m):
                multiplied(act, m)
                w = 512 if m >= QC else T
                act.activation(lat[:, m, 0:w], ps[:, 1 + m % 2, 0:w], ACT.Copy).then_inc(sem("lat_ready"), 1)

            for m in range(DKV):
                hi_chunk(act, m)
                if m:
                    lat_copy(m - 1)
            lat_copy(DKV - 1)
            act.wait_ge(sem("lat_ready"), DKV)
            square(2, lat[:, 0:QC, 0:T], sq_q)
            square(3, lat[:, QC:QC + KC, :], sq_k)
            root(2, T, QL)
            act.wait_ge(sem("cq_ready"), 1)
            root(3, 512, KVL)
            for p in range(HEADS // 2):
                act.wait_ge(sem("q_ready"), p + 1)
                act.activation(q_heads[0:NOPE, 2 * p:2 * p + 2, :], ps[0:NOPE, 1 + p % 2, :].rearrange("p (a b) -> p a b", a=2),
                               ACT.Copy).then_inc(sem("q_nope_ready"), 1)
            for k in range(8):
                act.wait_ge(sem("v_ready"), k + 1)
                act.activation(v_keys[:, k // 2, (k % 2) * 512:(k % 2 + 1) * 512], ps[:, 3 + k % 2, :], ACT.Copy)\
                   .then_inc(sem("v_keys_ready"), 1)
            for p in range(HEADS // 2):
                act.wait_ge(sem("k_ready"), p + 1)
                if p >= 2:
                    act.wait_ge(sem("scores_ready"), 4 * (p - 1))
                for j in range(2):
                    act.activation(k_heads[0:NOPE, (2 * p + j) % 4, :], ps[j * NOPE:(j + 1) * NOPE, 1, :], ACT.Copy)\
                       .then_inc(sem("k_heads_ready"), 1)
                for u in range(4 * p, 4 * p + 4):
                    act.wait_ge(sem("max_ready"), u + 1)
                    if u >= 2:
                        act.wait_ge(sem("turned"), u - 1)
                    act.activation(probs[:, u % 2, :], ps[:, 2 + u % 2, :], ACT.Exp, bias=smax[:, u % 8:u % 8 + 1],
                                   scale=SCALE, accum_out=smax[:, 8 + u % 8:9 + u % 8]).then_inc(sem("exp_ready"), 1)
                for hh in (2 * p, 2 * p + 1):
                    o = (hh % 2) * VD
                    act.wait_ge(sem("o_ready"), hh + 1)
                    act.activation(h_hi[o:o + VD, p, :], ps[0:VD, 6 + hh % 2, 0:T], ACT.Copy).then_inc(sem("o_hi_ready"), 1)
            for m in range(DC):
                hi_chunk(act, FIRST["wo"] + m)

            def input_norm(k, s, residual):
                act.wait_ge(sem("x_ready"), residual)
                square(k, x[:, :, :], tmp)
                root(k, T)
                split(s, tmp, h_hi)

            def retrieval(l):
                n0 = FIRST[f"wq{l}"]

                def q_copy(i, u):
                    multiplied(act, n0 + u, i)
                    act.activation(q_all[:, bass.ds(i * RAW + u, 1), :], ps[:, 4 + u, 0:T].unsqueeze(1), ACT.Copy)\
                       .then_inc(sem(f"q_all_ready_{l}"), 1)

                hi_chunk(act, n0)
                with act.Fori(0, HP // RAW - 1) as i:
                    for u in range(RAW):
                        hi_chunk(act, n0 + u + 1, i)
                        q_copy(i, u)
                for u in range(RAW):
                    if u < RAW - 1:
                        hi_chunk(act, n0 + HP - RAW + u + 1)
                    q_copy(HP // RAW - 1, u)
                for m in range(HP):
                    act.wait_ge(sem(f"key_scores_{l}"), m + 1)
                    act.activation(scores[:, :, m, :], ps[:, 4 + m % 4, 0:T].rearrange("p (a b) -> p a b", a=TT), ACT.Copy)\
                       .then_inc(sem(f"scores_copied_{l}"), 1)
                n0 = FIRST[f"u{l}"]

                def gelu(i, u):
                    multiplied(act, n0 + u, i)
                    act.activation(acts[:, bass.ds(i * RAW + u, 1), :], ps[:, 4 + u, 0:T].unsqueeze(1), ACT.Gelu)\
                       .then_inc(sem(f"acts_ready_{l}"), 1)

                hi_chunk(act, n0)
                with act.Fori(0, U_BESIDE) as i:
                    for u in range(RAW):
                        hi_chunk(act, n0 + u + 1, i)
                        gelu(i, u)
                act.wait_ge(sem(f"topk_done_{l}"), 1)
                with act.Fori(U_BESIDE, NK // RAW - 1) as i:
                    for u in range(RAW):
                        hi_chunk(act, n0 + u + 1, i)
                        gelu(i, u)
                for u in range(RAW):
                    if u < RAW - 1:
                        hi_chunk(act, n0 + NK - RAW + u + 1)
                    gelu(NK // RAW - 1, u)
                act.activation(fs_v, fs_v, ACT.Exp).then_inc(sem(f"fs_exp_{l}"), 1)
                n0 = FIRST[f"v{l}"]
                act.wait_ge(sem(f"gates_done_{l}"), 1)
                with act.Fori(0, NK // RAW) as i:
                    for u in range(RAW):
                        hi_chunk(act, n0 + u, i)
                        act.activation(h_hi[:, u % 2, :], acts[:, bass.ds(i * RAW + u, 1), :].rearrange("p o t -> p (o t)"), ACT.Copy)\
                           .then_inc(sem(f"g_hi_ready_{l}"), 1)

            input_norm(4, 2, 1)
            retrieval(0)

            act.wait_ge(sem("hyena_landed"), 16 * 7)
            for k in range(3):
                act.wait_ge(sem("arg_ready"), k + 1)
                act.activation(arg[0:FFN, 2, :], arg[0:FFN, 0, :], ACT.Sin).then_inc(sem("sin_ready"), 1)
            act.activation(delta, delta, ACT.Abs).then_inc(sem("delta_abs"), 1)
            act.wait_ge(sem("delta_abs"), 1)
            for mt in range(TT):
                if mt:
                    act.wait_ge(sem("hf_ready"), 8)
                act.activation(decay, delta, ACT.Exp, scale=col("neg_t", mt)).then_inc(sem("decay_ready"), 1)
            act.wait_ge(sem("hf_zeroed"), 1)
            act.activation(hf_abs, hf_all, ACT.Abs).then_inc(sem("hf_abs_ready"), 1)
            for k in range(16):
                part, kt, o, half = k // 8, (k // 4) % 2, (k // 2) % 2, k % 2
                act.wait_ge(sem("kf_ready"), k + 1)
                act.activation((k_re, k_im)[part][:, kt, o, half * 512:half * 512 + 512], ps[:, 4 + k % 4, :], ACT.Copy)\
                   .then_inc(sem("kf_copied"), 1)
            input_norm(5, 3, 2)
            n0 = FIRST["win"]

            def p_copy(m):
                multiplied(act, n0 + m)
                if m >= 2:
                    act.wait_ge(sem("conv_done"), m - 1)
                act.activation(pad[:, m % 2, 1:T + 1], ps[:, 4 + m % 4, 0:T], ACT.Copy).then_inc(sem("p_copied"), 1)

            act.wait_ge(sem("pad_ready"), 1)
            for m in range(3 * DC):
                hi_chunk(act, n0 + m)
                if m:
                    p_copy(m - 1)
            p_copy(3 * DC - 1)
            for o in range(ORDER):
                for k in range(4):
                    act.wait_ge(sem("z_turned"), 4 * o + k + 1)
                    act.activation(tr_z[:, k // 2, (k % 2) * 512:(k % 2) * 512 + 512], ps[:, 4 + k % 4, :], ACT.Copy)\
                       .then_inc(sem("tr_z_ready"), 1)
                if o:
                    act.wait_ge(sem("yf_ready"), o)
                for k in range(8):
                    part, kt, half = k // 4, (k // 2) % 2, k % 2
                    act.wait_ge(sem("uf_ready"), 8 * o + k + 1)
                    act.activation((u_re, u_im)[part][:, kt, half * 512:half * 512 + 512], ps[:, k % 4, :], ACT.Copy)\
                       .then_inc(sem("uf_copied"), 1)
            split(4, zz, h_hi)
            for m in range(DC):
                hi_chunk(act, FIRST["wout"] + m)
            input_norm(6, 5, 3)
            retrieval(1)
            act.wait_ge(sem("x_ready"), 4)
            square(7, x[:, :, :], tmp)
            root(7, T)

        @block.tensor
        def _(pe):
            def sums(k, src, chunks, width):
                pe.wait_ge(sem("square_ready"), k + 1)
                if k:
                    pe.wait_ge(sem("root_ready"), k)
                for c in range(chunks):
                    last = pe.matmul(ps[:, 0, 0:width], ones[:, :], src[:, c, :], start=(c == 0), stop=(c == chunks - 1))
                last.then_inc(sem("sum_ready"), 1)

            pe.wait_ge(sem("ones_ready"), 1)
            sums(0, tmp, DC, T)
            sums(1, tmp, DC, T)
            pe.wait_ge(sem("h_lo_ready"), 2)
            for m in range(DKV):
                if m >= 2:
                    pe.wait_ge(sem("lat_ready"), m - 1)
                bank = ps[:, 1 + m % 2, :]
                outs = [(bank[:, 0:T], h_hi, h_lo)]
                if m >= QC:
                    outs.append((bank[:, T:2 * T], c_hi, c_lo))
                product(pe, m, outs)
            sums(2, sq_q, QC, T)
            sums(3, sq_k, KC, 512)
            pe.wait_ge(sem("attn_landed"), 64)
            pe.wait_ge(sem("cq_ready"), 1)
            for p in range(HEADS // 2):
                if p >= 2:
                    pe.wait_ge(sem("q_nope_ready"), p - 1)
                    pe.wait_ge(sem("q_rope_ready"), p - 1)
                for j in range(2):
                    for c in range(QC):
                        last = pe.matmul(ps[:, 1 + p % 2, j * T:(j + 1) * T], w_uq[:, c, 2 * p + j, :], cq[:, c, :],
                                         start=(c == 0), stop=(c == QC - 1))
                last.then_inc(sem("q_ready"), 1)
            pe.wait_ge(sem("ckv_ready"), 1)
            for k in range(8):
                if k >= 2:
                    pe.wait_ge(sem("v_keys_ready"), k - 1)
                for c in range(KC):
                    last = pe.matmul(ps[:, 3 + k % 2, :], ckv[:, c, (k // 2) * P:(k // 2 + 1) * P],
                                     w_uv[:, c, (k % 2) * 512:(k % 2 + 1) * 512], start=(c == 0), stop=(c == KC - 1))
                last.then_inc(sem("v_ready"), 1)
            pe.wait_ge(sem("v_keys_ready"), 8)
            pe.wait_ge(sem("q_nope_ready"), 8)
            pe.wait_ge(sem("q_rope_ready"), 8)
            pe.wait_ge(sem("k_rope_ready"), 1)

            def score(u):
                hh, qt = u // 2, u % 2
                pe.wait_ge(sem("k_heads_ready"), hh + 1)
                if u >= 2:
                    pe.wait_ge(sem("exp_ready"), u - 1)
                pe.matmul(ps[:, 2 + u % 2, :], q_heads[0:QK, hh, qt * P:(qt + 1) * P], k_heads[0:QK, hh % 4, :], start=True, stop=True)\
                  .then_inc(sem("scores_ready"), 1)

            def turn(u):
                pe.wait_ge(sem("probs_ready"), u + 1)
                if u >= 2:
                    pe.wait_ge(sem("probs_t_ready"), u - 1)
                for k in range(4):
                    last = pe.transpose(ps[:, 4 + u % 2, k * P:(k + 1) * P], probs[:, u % 2, k * P:(k + 1) * P], ident[:, :])
                last.then_inc(sem("turned"), 1)

            def mix(hh):
                pe.wait_ge(sem("probs_t_ready"), 2 * hh + 2)
                if hh >= 2:
                    pe.wait_ge(sem("o_lo_ready"), hh - 1)
                for k in range(4):
                    last = pe.matmul(ps[0:VD, 6 + hh % 2, 0:T], v_keys[:, k, hh * VD:(hh + 1) * VD], probs_t[:, hh % 2, k, :],
                                     start=(k == 0), stop=(k == 3))
                last.then_inc(sem("o_ready"), 1)

            pe.wait_ge(sem("table_landed"), 32)
            for p in range(HEADS // 2):
                if p:
                    pe.wait_ge(sem("k_heads_ready"), 2 * p)
                for c in range(KC):
                    last = pe.matmul(ps[:, 1, :], w_uk[:, c, p, :], ckv[:, c, :], start=(c == 0), stop=(c == KC - 1))
                last.then_inc(sem("k_ready"), 1)
                u = 4 * p
                score(u)
                score(u + 1)
                turn(u)
                score(u + 2)
                turn(u + 1)
                mix(2 * p)
                score(u + 3)
                turn(u + 2)
                turn(u + 3)
                mix(2 * p + 1)

            def residual_products(name):
                for m in range(DC):
                    if m >= 2:
                        pe.wait_ge(sem(f"{name}_added"), m - 1)
                    product(pe, FIRST[name] + m, [(ps[:, 1 + m % 2, 0:T], h_hi, h_lo)])

            pe.wait_ge(sem("o_lo_ready"), HEADS)
            residual_products("wo")

            def retrieval(l):
                n0 = FIRST[f"wq{l}"]
                for u in range(RAW):
                    product(pe, n0 + u, [(ps[:, 4 + u, 0:T], h_hi, h_lo)])
                with pe.Fori(1, HP // RAW) as i:
                    for u in range(RAW):
                        pe.wait_ge(sem(f"q_all_ready_{l}"), i * RAW + (u + 1 - RAW))
                        product(pe, n0 + u, [(ps[:, 4 + u, 0:T], h_hi, h_lo)], i)
                pe.wait_ge(sem("keys_landed"), 16 * (l + 1))
                pe.wait_ge(sem(f"q_all_ready_{l}"), HP)
                for m in range(HP):
                    if m >= 4:
                        pe.wait_ge(sem(f"scores_copied_{l}"), m - 3)
                    for tt in range(TT):
                        last = pe.matmul(ps[:, 4 + m % 4, tt * P:(tt + 1) * P], q_all[:, m, tt * P:(tt + 1) * P], keys[:, m, :],
                                         start=True, stop=True)
                    last.then_inc(sem(f"key_scores_{l}"), 1)
                n0 = FIRST[f"u{l}"]
                pe.wait_ge(sem(f"scores_copied_{l}"), HP)
                for u in range(RAW):
                    product(pe, n0 + u, [(ps[:, 4 + u, 0:T], h_hi, h_lo)])
                with pe.Fori(1, NK // RAW) as i:
                    for u in range(RAW):
                        pe.wait_ge(sem(f"acts_ready_{l}"), i * RAW + (u + 1 - RAW))
                        product(pe, n0 + u, [(ps[:, 4 + u, 0:T], h_hi, h_lo)], i)
                pe.wait_ge(sem(f"sel_ready_{l}"), 1)
                pe.wait_ge(sem(f"acts_ready_{l}"), NK)
                for k, src in enumerate((fi_i, fi_j, fs)):
                    for tt in range(TT):
                        last = pe.transpose(ps[:, 4 + k, tt * P:(tt + 1) * P], src[:, tt, :], ident[:, :])
                last.then_inc(sem(f"sel_turned_{l}"), 1)
                with pe.Fori(0, T // 8) as i:
                    for b in range(2):
                        pe.wait_ge(sem(f"onehot_ready_{l}"), i * 2 + (b + 1))
                        for t in range(4):
                            last = pe.matmul(ps[:, 4 + b, t * P:(t + 1) * P], oh_i[:, b, t, :], oh_j[:, b, t, :], start=True, stop=True)
                        last.then_inc(sem(f"gate_ready_{l}"), 1)
                pe.wait_ge(sem(f"zeros_ready_{l}"), 1)
                for b in range(4):
                    pe.matmul(ps[:, b, :], ones[:, :], rstd[:, :], start=True, stop=False, skip_group_check=True)
                n0 = FIRST[f"v{l}"]
                with pe.Fori(0, NK // RAW) as i:
                    for u in range(RAW):
                        n = n0 + u
                        s = n % WSL
                        pe.wait_ge(sem("w_lo_ready"), i * RAW + (n + 1))
                        pe.wait_ge(sem(f"g_lo_ready_{l}"), i * RAW + (u + 1))
                        for c in range(DC):
                            o = ps[:, c // 2, (c % 2) * T:(c % 2 + 1) * T]
                            wh, wl = w_hi[:, s, c * P:(c + 1) * P], w_lo[:, s, c * P:(c + 1) * P]
                            pe.matmul(o, wh, h_hi[:, u % 2, :], start=False, stop=False, skip_group_check=True)
                            pe.matmul(o, wh, h_lo[:, u % 2, :], start=False, stop=False, skip_group_check=True)
                            last = pe.matmul(o, wl, h_hi[:, u % 2, :], start=False, stop=False, skip_group_check=True)
                        last.then_inc(sem("w_used"), 1)

            sums(4, tmp, DC, T)
            pe.wait_ge(sem("h_lo_ready"), 3)
            retrieval(0)

            pe.wait_ge(sem("hyena_landed"), 16 * 7)
            pe.wait_ge(sem("x_ready"), 2)
            pe.matmul(ps[0:FFN, 4, 0:T], w1[0:EMB, :], zfeat[0:EMB, :], start=True, stop=True).then_inc(sem("ffn_ready"), 1)
            for k in range(2):
                pe.wait_ge(sem("sin_ready"), k + 1)
                pe.matmul(ps[0:FFN, 5 + k, 0:T], w23[0:FFN, k, :], arg[0:FFN, 2, :], start=True, stop=True).then_inc(sem("ffn_ready"), 1)
            pe.wait_ge(sem("sin_ready"), 3)
            for k in range(16):
                mt, blk = k // 8, k % 8
                if k >= 4:
                    pe.wait_ge(sem("hf_ready"), k - 3)
                pe.matmul(ps[:, 4 + k % 4, :], arg[0:FFN, 2, mt * P:(mt + 1) * P], w4[0:FFN, blk * 512:(blk + 1) * 512], start=True, stop=True)\
                  .then_inc(sem("hf_prod"), 1)
            pe.wait_ge(sem("hf_abs_ready"), 1)
            for o in range(ORDER):
                for c in range(DC):
                    for k in range(4):
                        last = pe.matmul(ps[:, 0, o * DC + c:o * DC + c + 1], hf_abs5[:, k // 2, o, k % 2, c * P:(c + 1) * P], ones[:, 0:1],
                                         start=(k == 0), stop=(k == 3))
            last.then_inc(sem("norm_sum"), 1)
            pe.wait_ge(sem("hf_mixed"), 1)
            for k in range(16):
                part, kt, o, half = k // 8, (k // 4) % 2, (k // 2) % 2, k % 2
                if k >= 4:
                    pe.wait_ge(sem("kf_copied"), k - 3)
                src = hf_diff if part else hf_sum
                for mt in range(TT):
                    last = pe.matmul(ps[:, 4 + k % 4, :], dft[:, part, mt, kt * P:(kt + 1) * P], src[:, mt, o, half * 512:half * 512 + 512],
                                     start=(mt == 0), stop=(mt == TT - 1))
                last.then_inc(sem("kf_ready"), 1)
            pe.wait_ge(sem("inv_norm_ready"), 1)
            sums(5, tmp, DC, T)
            pe.wait_ge(sem("h_lo_ready"), 4)
            for m in range(3 * DC):
                if m >= 4:
                    pe.wait_ge(sem("p_copied"), m - 3)
                product(pe, FIRST["win"] + m, [(ps[:, 4 + m % 4, 0:T], h_hi, h_lo)])
            for o in range(ORDER):
                if o == 0:
                    pe.wait_ge(sem("conv_done"), DC)
                    pe.wait_ge(sem("p_copied"), 3 * DC)
                    src = conv
                else:
                    pe.wait_ge(sem("z_ready"), DC)
                    src = zz
                for k in range(4):
                    for j in range(4):
                        last = pe.transpose(ps[:, 4 + k, j * P:(j + 1) * P], src[:, (k % 2) * 4 + j, (k // 2) * P:(k // 2 + 1) * P], ident[:, :])
                    last.then_inc(sem("z_turned"), 1)
                pe.wait_ge(sem("tr_z_ready"), 4 * (o + 1))
                for k in range(8):
                    part, kt, half = k // 4, (k // 2) % 2, k % 2
                    if k >= 4:
                        pe.wait_ge(sem("uf_copied"), 8 * o + k - 3)
                    for mt in range(TT):
                        last = pe.matmul(ps[:, k % 4, :], dft[:, part, mt, kt * P:(kt + 1) * P], tr_z[:, mt, half * 512:half * 512 + 512],
                                         start=(mt == 0), stop=(mt == TT - 1))
                    last.then_inc(sem("uf_ready"), 1)
                pe.wait_ge(sem("yf_ready"), o + 1)
                for c in range(DC):
                    if c >= 4:
                        pe.wait_ge(sem("z_ready"), DC * o + c - 3)
                    for k in range(4):
                        part, kt = k // 2, k % 2
                        last = pe.matmul(ps[:, 4 + c % 4, 0:T], (y_re, y_im)[part][:, kt, c * P:(c + 1) * P], dft[:, 2 + part, kt, :],
                                         start=(k == 0), stop=(k == 3))
                    last.then_inc(sem("yt_ready"), 1)
            pe.wait_ge(sem("h_lo_ready"), 5)
            residual_products("wout")
            sums(6, tmp, DC, T)
            pe.wait_ge(sem("h_lo_ready"), 6)
            retrieval(1)
            sums(7, tmp, DC, T)

        @block.vector
        def _(dve):
            ch = Chain(dve, sem("dve_chain"))
            link = ch.link

            def b_cols(name, k, n):
                return cols[:, COLS[name][0] + k:COLS[name][0] + k + n]

            def gain_of(g, m, name, k):
                link(dve.scalar_tensor_tensor(out=gain[:, g * DC:(g + 1) * DC], in0=m, scalar=1.0, in1=b_cols(name, k, DC),
                                              op0=ALU.add, op1=ALU.mult))

            def normalise(k, src, dst, width, chunks):
                dve.wait_ge(sem("root_ready"), k + 1)
                link(dve.reciprocal(rstd[:, 0:width], rstd[:, 0:width]))
                link(dve.tensor_tensor(dst, src, rstd[:, 0:width].unsqueeze(1).broadcast_to([P, chunks, width]), ALU.mult))

            def modulated(k, s, src, g, shift, hi, lo):
                normalise(k, src, tmp, T, DC)
                for c in range(DC):
                    last = dve.tensor_scalar(tmp[:, c, :], tmp[:, c, :], gain[:, g * DC + c:g * DC + c + 1], shift(c), ALU.mult, ALU.add)
                last.then_inc(sem("to_split"), 1)
                dve.wait_ge(sem("to_split"), s + 1)
                low(s, tmp, hi, lo)

            def low(s, src, hi, lo):
                dve.wait_ge(sem("h_hi_ready"), s + 1)
                dve.tensor_tensor(lo[:, :, :], src, hi[:, :, :], ALU.subtract).then_inc(sem("h_lo_ready"), 1)

            link(dve.memset(zero[:, :], 0.0))
            link(dve.memset(zero[:, 1:2], EPS))
            dve.wait_ge(sem("c_exp"), 2)
            link(dve.tensor_scalar(tmp_flat, tmp_flat, 1.0, None, ALU.add))
            link(dve.reciprocal(tmp_flat, tmp_flat))
            link(dve.tensor_tensor(silu[:, :], silu[:, :], tmp_flat[:, 0:D], ALU.mult))
            dve.tensor_tensor(silu_c, silu_c, tmp_flat[:, D:2 * D], ALU.mult).then_inc(sem("silu_ready"), 1)
            dve.wait_ge(sem("silu_ready"), 1)
            dve.wait_ge(sem("cols_landed"), 16)

            def dot(k, slot, dst):
                dve.tensor_tensor_reduce(mod_raw[:, slot, :], mod_raw[:, slot, :], silu[:, :], 1.0, 0.0, ALU.mult, ALU.add, dst)\
                   .then_inc(sem("mod_used"), 1)

            for k in range(2 * DC):
                dve.wait_ge(sem(f"mod_landed_{k % 2}"), 16 * (k // 2 + 1))
                link(dve.tensor_tensor_reduce(junk, mod_raw[:, k % 2, :], silu_c, 1.0, 0.0, ALU.mult, ALU.add, modc[:, k:k + 1]))
                dot(k, k % 2, mod[:, k:k + 1])
            dve.wait_ge(sem("mod_used"), 2 * DC)
            link(dve.tensor_tensor(mod[:, 0:2 * DC], mod[:, 0:2 * DC], b_cols("mod_b", 0, 2 * DC), ALU.add))
            link(dve.tensor_tensor(modc[:, :], modc[:, :], b_cols("mod_b", 0, 2 * DC), ALU.add))
            gain_of(0, mod[:, DC:2 * DC], "mix_g", 0)
            gain_of(1, modc[:, DC:2 * DC], "mix_g", 0)
            modulated(0, 0, x[:, :, :], 0, lambda c: mod[:, c:c + 1], h_hi, h_lo)
            modulated(1, 1, cx, 1, lambda c: modc[:, c:c + 1], c_hi, c_lo)
            for m in range(DKV):
                lo_chunk(dve, m)
            normalise(2, lat[:, 0:QC, 0:T], cq, T, QC)
            for c in range(QC):
                last = dve.tensor_scalar(cq[:, c, :], cq[:, c, :], col("q_g", c), None, ALU.mult)
            last.then_inc(sem("cq_ready"), 1)
            normalise(3, lat[:, QC:QC + KC, :], ckv, 512, KC)
            for c in range(KC):
                last = dve.tensor_scalar(ckv[:, c, :], ckv[:, c, :], col("kv_g", c), None, ALU.mult)
            last.then_inc(sem("ckv_ready"), 1)
            dve.wait_ge(sem("attn_landed"), 64)
            lr = lat[:, DKV - 1, :]
            link(dve.tensor_tensor(rope_s[NOPE:QK, 0, :], lr[QK:P, 0:T], rope[QK:P, :], ALU.mult))
            link(dve.tensor_tensor(rope_c[NOPE:QK, 0, :], lr[NOPE:QK, 0:T], rope[NOPE:QK, :], ALU.mult))
            for s in range(4):
                dve.tensor_tensor(k_heads[NOPE:QK, s, 0:T], rope_s[NOPE:QK, 0, :], rope_c[NOPE:QK, 0, :], ALU.add)
                last = dve.tensor_copy(k_heads[NOPE:QK, s, T:2 * T], lr[NOPE:QK, T:2 * T])
            last.then_inc(sem("k_rope_ready"), 1)
            dve.wait_ge(sem("k_rope_ready"), 1)
            for p in range(HEADS // 2):
                dve.wait_ge(sem("q_ready"), p + 1)
                bank = ps[:, 1 + p % 2, :].rearrange("p (a b) -> p a b", a=2)
                link(dve.tensor_tensor(rope_s[NOPE:QK, :, :], bank[QK:P, :, :], rope[QK:P, :].unsqueeze(1).broadcast_to([ROPE, 2, T]), ALU.mult))
                link(dve.tensor_tensor(rope_c[NOPE:QK, :, :], bank[NOPE:QK, :, :], rope[NOPE:QK, :].unsqueeze(1).broadcast_to([ROPE, 2, T]), ALU.mult))
                dve.tensor_tensor(q_heads[NOPE:QK, 2 * p:2 * p + 2, :], rope_s[NOPE:QK, :, :], rope_c[NOPE:QK, :, :], ALU.add)\
                   .then_inc(sem("q_rope_ready"), 1)
                dve.wait_ge(sem("q_rope_ready"), p + 1)

            def row_max(u):
                dve.wait_ge(sem("scores_ready"), u + 1)
                k = u % 8
                if u >= 8:
                    dve.wait_ge(sem("exp_ready"), u - 7)
                link(dve.tensor_reduce(smax[:, 24 + k:25 + k], ps[:, 2 + u % 2, :], AX.X, ALU.max))
                dve.tensor_scalar(smax[:, k:k + 1], smax[:, 24 + k:25 + k], -SCALE, None, ALU.mult).then_inc(sem("max_ready"), 1)

            def norm_probs(u):
                dve.wait_ge(sem("exp_ready"), u + 1)
                k = u % 8
                link(dve.reciprocal(smax[:, 16 + k:17 + k], smax[:, 8 + k:9 + k]))
                dve.tensor_scalar(probs[:, u % 2, :], probs[:, u % 2, :], smax[:, 16 + k:17 + k], None, ALU.mult).then_inc(sem("probs_ready"), 1)

            def copy_turned(u):
                dve.wait_ge(sem("turned"), u + 1)
                hh = u // 2
                if hh >= 2:
                    dve.wait_ge(sem("o_ready"), hh - 1)
                dve.tensor_copy(probs_t[:, hh % 2, :, (u % 2) * P:(u % 2 + 1) * P], ps[:, 4 + u % 2, :].rearrange("p (a b) -> p a b", a=4))\
                   .then_inc(sem("probs_t_ready"), 1)

            for p in range(HEADS // 2):
                u = 4 * p
                row_max(u)
                row_max(u + 1)
                norm_probs(u)
                copy_turned(u)
                row_max(u + 2)
                norm_probs(u + 1)
                copy_turned(u + 1)
                row_max(u + 3)
                norm_probs(u + 2)
                copy_turned(u + 2)
                norm_probs(u + 3)
                copy_turned(u + 3)
                for hh in (2 * p, 2 * p + 1):
                    o = (hh % 2) * VD
                    dve.wait_ge(sem("o_hi_ready"), hh + 1)
                    dve.tensor_tensor(h_lo[o:o + VD, p, :], ps[0:VD, 6 + hh % 2, 0:T], h_hi[o:o + VD, p, :], ALU.subtract)\
                       .then_inc(sem("o_lo_ready"), 1)
                for k in range(2 * DC + 4 * p, 2 * DC + 4 * p + 4):
                    dve.wait_ge(sem(f"mod_landed_{k % 2}"), 16 * (k // 2 + 1))
                    dot(k, k % 2, mod[:, k:k + 1])
            dve.wait_ge(sem("mod_used"), MODS)
            link(dve.tensor_tensor(mod[:, 2 * DC:MODS], mod[:, 2 * DC:MODS], b_cols("mod_b", 2 * DC, MODS - 2 * DC), ALU.add))
            gain_of(2, mod[:, 4 * DC:5 * DC], "ffn_g", 0)

            def add_residual(m, bank, l, part):
                return dve.scalar_tensor_tensor(out=x[:, m, :], in0=bank, scalar=mod_col(l, part, m), in1=x[:, m, :], op0=ALU.mult, op1=ALU.add)

            def residual(name, l):
                for m in range(DC):
                    lo_chunk(dve, FIRST[name] + m)
                    if m:
                        multiplied(dve, FIRST[name] + m - 1)
                        add_residual(m - 1, ps[:, 1 + (m - 1) % 2, 0:T], l, 2).then_inc(sem(f"{name}_added"), 1)
                multiplied(dve, FIRST[name] + DC - 1)
                add_residual(DC - 1, ps[:, 1 + (DC - 1) % 2, 0:T], l, 2).then_inc(sem("x_ready"), 1)

            residual("wo", 0)
            dve.wait_ge(sem("x_ready"), 1)
            modulated(4, 2, x[:, :, :], 2, lambda c: mod_col(0, 3, c), h_hi, h_lo)

            def top16(values, out16, index16):
                dve.drain()
                dve.max(out16[:, 0:8], values)
                dve.drain()
                dve.max_index(index16[:, 0:8], out16[:, 0:8], values)
                dve.drain()
                dve.match_replace(values, out16[:, 0:8], values, LOWEST)
                dve.drain()
                dve.max(out16[:, 8:16], values)
                dve.drain()
                dve.max_index(index16[:, 8:16], out16[:, 8:16], values)
                dve.drain()

            iota16 = iota[:, 0:TOPK].unsqueeze(1).broadcast_to([P, TOPK, TOPK])

            def retrieval(l):
                n0 = FIRST[f"wq{l}"]
                with dve.Fori(0, HP // RAW) as i:
                    for u in range(RAW):
                        lo_chunk(dve, n0 + u, i)
                n0 = FIRST[f"u{l}"]
                lo_chunk(dve, n0)
                dve.wait_ge(sem(f"scores_copied_{l}"), HP)
                with ch.loop(TT * PH, 11) as i:
                    lo_chunk(dve, n0 + 1, i)
                    dve.tensor_copy(pair, scores_v[:, bass.ds(i, 1), :].rearrange("p o (a b) -> p (o a) b", a=2))
                    top16(pair[:, 0, :], sv[:, 0, :], si_u[:, 0, :])
                    lo_chunk(dve, n0 + 2, i)
                    top16(pair[:, 1, :], sv[:, 1, :], si_u[:, 1, :])
                    lo_chunk(dve, n0 + 3, i)
                    link(dve.tensor_copy(si_f, si_u))
                    dve.tensor_tensor(cand, sv[:, 0, :].unsqueeze(2).broadcast_to([P, TOPK, TOPK]),
                                      sv[:, 1, :].unsqueeze(1).broadcast_to([P, TOPK, TOPK]), ALU.add)
                    top16(cand_flat, fs_one, fi_u)
                    lo_chunk(dve, n0 + 4, i)
                    link(dve.tensor_scalar(fa_u[:, 0, :], fi_u, 4, None, ALU.logical_shift_right))
                    link(dve.tensor_scalar(fa_u[:, 1, :], fi_u, TOPK - 1, None, ALU.bitwise_and))
                    link(dve.tensor_copy(fa_f, fa_u))
                    for p, dst in ((0, fi_i_v), (1, fi_j_v)):
                        link(dve.tensor_tensor(eq, fa_f[:, p, :].unsqueeze(2).broadcast_to([P, TOPK, TOPK]), iota16, ALU.is_equal))
                        link(dve.tensor_tensor(eq, eq, si_f[:, p, :].unsqueeze(1).broadcast_to([P, TOPK, TOPK]), ALU.mult))
                        link(dve.tensor_reduce(dst[:, bass.ds(i, 1), :], eq, AX.X, ALU.add))
                    link(dve.tensor_scalar(fs_v[:, bass.ds(i, 1), :].rearrange("p o k -> p (o k)"), fs_one, fs_one[:, 0:1], None, ALU.subtract))
                dve.tensor_copy(got[:, 0:1], fs_one[:, 0:1]).then_inc(sem(f"topk_done_{l}"), 1)
                with dve.Fori(TT * PH, NK // RAW - 1) as i:
                    for u in range(RAW):
                        lo_chunk(dve, n0 + u + 1, i)
                for u in range(RAW - 1):
                    lo_chunk(dve, n0 + NK - RAW + 1 + u)
                dve.wait_ge(sem(f"fs_exp_{l}"), 1)
                link(dve.tensor_reduce(fsum, fs_v, AX.X, ALU.add))
                link(dve.reciprocal(fsum, fsum))
                dve.tensor_tensor(fs_v, fs_v, fsum.unsqueeze(2).broadcast_to([P, TT * PH, TOPK]), ALU.mult).then_inc(sem(f"sel_ready_{l}"), 1)
                dve.wait_ge(sem(f"sel_turned_{l}"), 1)
                for k, dst in enumerate((sel_i, sel_j, sel_g)):
                    last = dve.tensor_copy(dst[:, :], ps[:, 4 + k, 0:T])
                link(last)

                def onehots(b, t0):
                    for t in range(4):
                        c = bass.ds(t0 + t, 1)
                        dve.tensor_scalar(oh_i[:, b, t, :], iota[:, :], sel_i[:, c], None, ALU.is_equal)
                        last = dve.tensor_scalar(oh_j[:, b, t, :], iota[:, :], sel_j[:, c], sel_g[:, c], ALU.is_equal, ALU.mult)
                    last.then_inc(sem(f"onehot_ready_{l}"), 1)

                def apply_gates(b, t0, count):
                    dve.wait_ge(sem(f"gate_ready_{l}"), count)
                    some = acts[:, :, bass.ds(t0, 4)]
                    return dve.tensor_tensor(some, ps[:, 4 + b, :].rearrange("p (t j) -> p j t", t=4), some, ALU.mult)

                onehots(0, 0)
                with dve.Fori(0, T // 8 - 1) as i:
                    onehots(1, i * 8 + 4)
                    apply_gates(0, i * 8, i * 2 + 1)
                    onehots(0, i * 8 + 8)
                    apply_gates(1, i * 8 + 4, i * 2 + 2)
                onehots(1, T - 4)
                apply_gates(0, T - 8, T // 4 - 1)
                apply_gates(1, T - 4, T // 4).then_inc(sem(f"gates_done_{l}"), 1)
                dve.memset(rstd[:, :], 0.0).then_inc(sem(f"zeros_ready_{l}"), 1)
                n0 = FIRST[f"v{l}"]

                def g_low(i, u, step):
                    dve.wait_ge(sem(f"g_hi_ready_{l}"), i * step + (u + 1))
                    dve.tensor_tensor(h_lo[:, u % 2, :], acts[:, bass.ds(i * step + u, 1), :].rearrange("p o t -> p (o t)"), h_hi[:, u % 2, :], ALU.subtract)\
                       .then_inc(sem(f"g_lo_ready_{l}"), 1)

                if l == 0:
                    with dve.Fori(0, 8) as i:
                        for u in range(16):
                            dve.wait_ge(sem("w_hi_ready"), i * 16 + (n0 + u + 1))
                            dve.tensor_tensor(w_lo[:, (n0 + u) % WSL, :], raw[:, (n0 + u) % RAW, :], w_hi[:, (n0 + u) % WSL, :], ALU.subtract)\
                               .then_inc(sem("w_lo_ready"), 1)
                            g_low(i, u, 16)
                            if u % 8 in (1, 4, 6):
                                m = (u // 8) * 3 + (1, 4, 6).index(u % 8)
                                dve.wait_ge(sem(f"mod_landed_{m % 2}"), i * 48 + 16 * ((MODS + m) // 2 + 1))
                                dot(m, m % 2, got[:, m:m + 1])
                        dve.wait_ge(sem("mod_used"), i * 6 + (MODS + 6))
                        dve.tensor_copy(mod[:, bass.ds(i * 6 + MODS, 6)], got[:, 0:6]).then_inc(sem("mod_copied"), 1)
                        dve.wait_ge(sem("mod_copied"), i + 1)
                else:
                    with dve.Fori(0, NK // RAW) as i:
                        for u in range(RAW):
                            lo_chunk(dve, n0 + u, i)
                            g_low(i, u, RAW)
                multiplied(dve, n0 + NK - 1)
                for c in range(DC):
                    last = add_residual(c, ps[:, c // 2, (c % 2) * T:(c % 2 + 1) * T], l, 5)
                last.then_inc(sem("x_ready"), 1)
                dve.wait_ge(sem("x_ready"), 2 + 2 * l)

            retrieval(0)
            link(dve.tensor_tensor(mod[:, MODS:2 * MODS], mod[:, MODS:2 * MODS], b_cols("mod_b", MODS, MODS), ALU.add))
            gain_of(3, mod[:, MODS + DC:MODS + 2 * DC], "mix_g", DC)
            gain_of(4, mod[:, MODS + 4 * DC:MODS + 5 * DC], "ffn_g", DC)

            dve.wait_ge(sem("hyena_landed"), 16 * 7)
            dve.memset(pad[:, :, :], 0.0).then_inc(sem("pad_ready"), 1)
            r, t1 = arg[0:FFN, 0, :], arg[0:FFN, 1, :]
            for k in range(3):
                dve.wait_ge(sem("ffn_ready"), k + 1)
                link(dve.tensor_scalar(r, ps[0:FFN, 4 + k, 0:T], fcol[0:FFN, k:k + 1], fcol[0:FFN, 3:4], ALU.add, ALU.mult))
                link(dve.tensor_scalar(t1, r, 1 / (2 * math.pi), MAGIC, ALU.mult, ALU.add))
                link(dve.tensor_scalar(t1, t1, MAGIC, None, ALU.subtract))
                for part in (TWO_PI_1, TWO_PI_2, TWO_PI_3):
                    link(dve.scalar_tensor_tensor(out=r, in0=t1, scalar=-part, in1=r, op0=ALU.mult, op1=ALU.add))
                dve.tensor_scalar(r, r, 3.1415925, -3.1415925, ALU.min, ALU.max).then_inc(sem("arg_ready"), 1)
            for k in range(16):
                mt, blk = k // 8, k % 8
                dve.wait_ge(sem("decay_ready"), mt + 1)
                dve.wait_ge(sem("hf_prod"), k + 1)
                o, fb, half = blk // 4, (blk // 2) % 2, blk % 2
                dve.tensor_tensor(hf[:, mt, o, fb, half * 512:half * 512 + 512], ps[:, 4 + k % 4, :], decay[:, o, half * 512:half * 512 + 512], ALU.mult)\
                   .then_inc(sem("hf_ready"), 1)
            dve.wait_ge(sem("hf_ready"), 16)
            for o in range(ORDER):
                last = dve.memset(hf[0:1, 0, o, 1, :], 0.0)
            last.then_inc(sem("hf_zeroed"), 1)
            dve.wait_ge(sem("hf_zeroed"), 1)
            dve.wait_ge(sem("hf_abs_ready"), 1)
            for mt in range(TT):
                dve.tensor_tensor(hf_diff[:, mt, :, :], hf[:, mt, :, 0, :], hf[:, mt, :, 1, :], ALU.subtract)
            for mt in range(TT):
                last = dve.tensor_tensor(hf_sum[:, mt, :, :], hf[:, mt, :, 0, :], hf[:, mt, :, 1, :], ALU.add)
            last.then_inc(sem("hf_mixed"), 1)
            dve.wait_ge(sem("norm_sum"), 1)
            dve.reciprocal(inv_norm, ps[:, 0, 0:ORDER * DC]).then_inc(sem("inv_norm_ready"), 1)
            modulated(5, 3, x[:, :, :], 3, lambda c: mod_col(1, 0, c), h_hi, h_lo)
            n0 = FIRST["win"]

            def short_conv(m):
                dve.wait_ge(sem("p_copied"), m + 1)
                b = pad[:, m % 2, :]
                link(dve.tensor_scalar(conv[:, m, :], b[:, 0:T], col("conv_w", m), col("conv_b", m), ALU.mult, ALU.add))
                link(dve.scalar_tensor_tensor(out=conv[:, m, :], in0=b[:, 1:T + 1], scalar=col("conv_w", 3 * DC + m), in1=conv[:, m, :], op0=ALU.mult, op1=ALU.add))
                dve.scalar_tensor_tensor(out=conv[:, m, :], in0=b[:, 2:T + 2], scalar=col("conv_w", 6 * DC + m), in1=conv[:, m, :], op0=ALU.mult, op1=ALU.add)\
                   .then_inc(sem("conv_done"), 1)

            for m in range(3 * DC):
                lo_chunk(dve, n0 + m)
                if m >= 2:
                    short_conv(m - 2)
            short_conv(3 * DC - 2)
            short_conv(3 * DC - 1)
            dve.wait_ge(sem("conv_done"), 3 * DC)
            for o in range(ORDER):
                dve.wait_ge(sem("uf_copied"), 8 * (o + 1))
                for sign, ka, kb, dst in ((ALU.subtract, k_re, k_im, y_re), (ALU.add, k_im, k_re, y_im)):
                    link(dve.tensor_tensor(ctmp, u_im, kb[:, :, o, :], ALU.mult))
                    link(dve.tensor_tensor(dst, u_re, ka[:, :, o, :], ALU.mult))
                    last = dve.tensor_tensor(dst, dst, ctmp, sign)
                    if dst is y_re:
                        link(last)
                last.then_inc(sem("yf_ready"), 1)
                z = conv if o == 0 else zz
                for c in range(DC):
                    dve.wait_ge(sem("yt_ready"), DC * o + c + 1)
                    t = hrt[:, c % 2, :]
                    link(dve.tensor_scalar(t, z[:, c, :], col("hy_bias", o * DC + c), None, ALU.mult))
                    link(dve.scalar_tensor_tensor(out=t, in0=ps[:, 4 + c % 4, 0:T], scalar=inv_norm[:, o * DC + c:o * DC + c + 1], in1=t, op0=ALU.mult, op1=ALU.add))
                    dve.tensor_tensor(zz[:, c, :], t, conv[:, DC * (o + 1) + c, :], ALU.mult).then_inc(sem("z_ready"), 1)
                dve.wait_ge(sem("z_ready"), DC * (o + 1))
            dve.tensor_copy(got[:, 0:1], zz[:, 0, 0:1]).then_inc(sem("to_split"), 1)
            low(4, zz, h_hi, h_lo)
            residual("wout", 1)
            dve.wait_ge(sem("x_ready"), 3)
            modulated(6, 5, x[:, :, :], 4, lambda c: mod_col(1, 3, c), h_hi, h_lo)
            retrieval(1)
            normalise(7, x[:, :, :], x[:, :, :], T, DC)
            for c in range(DC):
                last = dve.tensor_scalar(x[:, c, :], x[:, c, :], col("final_g", c), None, ALU.mult)
            last.then_inc(sem("result_ready"), 1)


def tables():
    f = np.float32
    inv = (10000.0 ** (-np.arange(ROPE // 4, dtype=f) / f(ROPE // 4))).astype(f)
    t = np.arange(T)
    row, colu = (t // 64).astype(f), (t % 64).astype(f)
    ang = np.concatenate([row[:, None] * inv, row[:, None] * inv, colu[:, None] * inv, colu[:, None] * inv], 1).T
    sign = np.where(np.arange(ROPE) % 16 < 8, -1.0, 1.0)[:, None]
    rope = np.zeros((P, T), f)
    rope[NOPE:QK] = np.cos(ang)
    rope[QK:] = np.sin(ang) * sign
    k = np.arange(T)
    ang = 2 * np.pi * np.outer(k, k + 0.5) / (2 * T)
    def tiles(m):
        return m.reshape(TT, P, T).transpose(1, 0, 2)
    dft = np.stack([tiles(np.cos(ang)), tiles(np.sin(ang)), tiles(np.cos(ang).T / T), tiles(np.sin(ang).T / T)], 1).astype(f)
    bands = (EMB - 1) // 2
    lin = np.linspace(0.0, 1.0, T, dtype=f)
    w = (f(2.0 * math.pi / T) * np.arange(T, dtype=f))[None, :]
    fr = np.linspace(1e-4, bands - 1, bands, dtype=f)[:, None]
    zfeat = np.concatenate([lin[None, :], np.cos(fr * w), -np.sin(fr * w)], 0).astype(f)
    return dict(rope=rope, dft=dft, zfeat=zfeat, ident=np.eye(P, dtype=f), iota=np.broadcast_to(np.arange(P, dtype=f), (P, P)),
                neg_t=-lin.reshape(TT, P).T)


def kernel(**inputs):
    import concourse.bacc as _bacc
    from concourse.bass_utils import run_bass_kernel_spmd as _run

    g = {k: np.asarray(v) for k, v in inputs.items()}
    tab = tables()

    def by_feature(v):
        return v.reshape(-1, P).T

    def by_chunk(w):
        return w.reshape(DC, P, -1, P).transpose(2, 1, 0, 3).reshape(-1, P, D)

    swap = np.concatenate([np.arange(8, 16), np.arange(0, 8), np.arange(24, 32), np.arange(16, 24)])
    ar = {}
    for name in ("x", "ctx"):
        ar[name] = g[name][0].T.reshape(DC, P, T).transpose(1, 0, 2)
    ar["c"] = np.broadcast_to(g["c"][0], (P, D))
    ar["c_ctx"] = np.broadcast_to(g["c_ctx"], (P, D))
    ar["mod_w"] = g["mod_w"].reshape(2, D, MODS, P).transpose(0, 2, 3, 1).reshape(2 * MODS, P, D)
    parts = {"mix_g": g["norm_mix_g"], "ffn_g": g["norm_ffn_g"], "final_g": g["final_g"], "q_g": g["mla_q_norm_g"][0],
             "kv_g": g["mla_kv_norm_g"][0], "conv_w": g["hy_conv_w"][0], "conv_b": g["hy_conv_b"][0], "hy_bias": g["hy_bias"][0],
             "mod_b": g["mod_b"]}
    ar["cols"] = np.concatenate([by_feature(parts[n]) if n in parts else tab[n] for n in COLS], 1)
    dkv = g["mla_w_dkv"][0]
    key = dkv[:, QL + KVL:]
    dkv = np.concatenate([dkv[:, :QL + KVL], np.zeros((D, NOPE), np.float32), key, key[:, swap]], 1)
    ar["dkv"] = by_chunk(dkv)
    uq = g["mla_w_uq"][0].reshape(QL, HEADS, QK)
    uq = np.concatenate([uq, uq[:, :, NOPE + swap]], 2)
    ar["w_uq"] = uq.reshape(QC, P, HEADS, P).transpose(1, 0, 2, 3)
    ukv = g["mla_w_ukv"][0].reshape(KC, P, HEADS, NOPE + VD).transpose(1, 0, 2, 3)
    ar["w_uk"] = ukv[..., :NOPE].reshape(P, KC, HEADS // 2, P)
    ar["w_uv"] = ukv[..., NOPE:].reshape(P, KC, D)
    ar["wo"], ar["win"], ar["wout"] = by_chunk(g["mla_w_o"][0]), by_chunk(g["hy_w_in"][0]), by_chunk(g["hy_w_out"][0])
    for l in range(2):
        ar[f"wq{l}"] = by_chunk(g["peer_wq"][l])
        ar[f"u{l}"] = g["peer_u"][l].reshape(NK, NK, DC, P).transpose(1, 3, 2, 0).reshape(NK, P, D)
        ar[f"v{l}"] = g["peer_v"][l].reshape(NK, NK, D).transpose(1, 0, 2)
    ar["keys"] = g["peer_keys"].reshape(2, HP, NK, P).transpose(0, 3, 1, 2)
    ar["w4"] = g["hy_w4"][0]
    ar["delta"] = np.broadcast_to(g["hy_deltas"][0], (P, ORDER, D))
    ar["w1"] = g["hy_w1"][0]
    ar["w23"] = np.stack([g["hy_w2"][0], g["hy_w3"][0]], 1)
    ar["fcol"] = np.stack([g["hy_b1"][0], g["hy_b2"][0], g["hy_b3"][0], g["hy_sin_freq"][0]], 1)
    for n in ("rope", "dft", "zfeat", "ident", "iota"):
        ar[n] = tab[n]

    nc = _bacc.Bacc("TRN2", target_bir_lowering=False, num_devices=1)
    arrays, aps = {}, {}
    for name, v in ar.items():
        arrays[f"in_{name}"] = np.ascontiguousarray(v)
        aps[name] = nc.dram_tensor(f"in_{name}", v.shape, F32, kind="ExternalInput").ap()
    out = nc.dram_tensor("out_x", (P, DC, T), F32, kind="ExternalOutput").ap()
    build(nc, aps, out)
    r = _run(nc, [arrays], core_ids=[0])
    y = r.results[0]["out_x"]
    return np.ascontiguousarray(np.asarray(y).transpose(2, 1, 0).reshape(1, T, D))
```

```python
from contextlib import ExitStack, contextmanager
import math

import numpy as np
import concourse.bass as bass
from concourse import mybir
from concourse.alu_op_type import AluOpType as ALU

ACT = mybir.ActivationFunctionType
F32 = mybir.dt.float32
F32R = mybir.dt.float32r
U32 = mybir.dt.uint32
AX = mybir.AxisListType

P = 128
D = 1024
DC = D // P
T = 256
TT = T // P
EPS = 1e-6
HEADS, NOPE, ROPE, VD = 16, 64, 32, 64
QK = NOPE + ROPE
QL, KVL = 384, 256
QC, KC = QL // P, KVL // P
DKV = QC + KC + 1
PH, NK, TOPK = 8, 128, 16
HP = 2 * PH
ORDER, FFN, EMB = 2, 64, 33
RAW, SPLIT = 4, 4
MODS = 6 * DC
SCALE = QK ** -0.5
LOWEST = -3.4028234663852886e38
MAGIC = 12582912.0
TWO_PI_1, TWO_PI_2 = 6.28125, 0.0019340515136718750
TWO_PI_3 = 2 * math.pi - TWO_PI_1 - TWO_PI_2

COLS = {}
_at = 0
for _n, _w in (("mix_g", 2 * DC), ("ffn_g", 2 * DC), ("final_g", DC), ("q_g", QC), ("kv_g", KC), ("conv_w", 9 * DC),
               ("conv_b", 3 * DC), ("hy_bias", ORDER * DC), ("mod_b", 2 * MODS), ("neg_t", TT)):
    COLS[_n] = (_at, _at + _w)
    _at += _w
NCOLS = _at

STREAM = [("dkv", DKV), ("wo", DC), ("wq0", HP), ("u0", NK), ("v0", NK), ("win", 3 * DC), ("wout", DC),
          ("wq1", HP), ("u1", NK), ("v1", NK)]
FIRST = {}
_at = 0
for _n, _w in STREAM:
    FIRST[_n] = _at
    _at += _w

MOD_BESIDE = (1, 4, 6, 9, 12, 14)
U_TOPK = TT * PH * RAW
U_GATED = U_TOPK + RAW
GROUPS = T // 4
GATE_STEPS = (NK - U_GATED) // RAW


class Chain:

    def __init__(self, eng, sem):
        self.eng, self.sem, self.n, self.i, self.per, self.k = eng, sem, 0, None, 0, 0

    def link(self, ins):
        ins.then_inc(self.sem, 1)
        if self.i is None:
            self.n += 1
            self.eng.wait_ge(self.sem, self.n)
        else:
            self.k += 1
            self.eng.wait_ge(self.sem, self.i * self.per + (self.n + self.k))

    @contextmanager
    def loop(self, count, per):
        with self.eng.Fori(0, count) as i:
            self.i, self.per, self.k = i, per, 0
            yield i
            assert self.k == per, (self.k, per)
        self.i = None
        self.n += count * per


def build(nc, a, out):
    with ExitStack() as ctx:
        def sb(name, shape, dt=F32):
            return ctx.enter_context(nc.sbuf_tensor(name, shape, dt))

        sems = {}

        def sem(name):
            if name not in sems:
                sems[name] = ctx.enter_context(nc.semaphore(name))
            return sems[name]

        x = sb("x", [P, DC, T])
        h_hi = sb("h_hi", [P, DC, T], F32R)
        h_lo = sb("h_lo", [P, DC, T], F32R)
        raw = sb("raw", [P, RAW, D])
        w_hi = sb("w_hi", [P, SPLIT, D // 2], F32R)
        w_lo = sb("w_lo", [P, SPLIT, D // 2], F32R)
        small = sb("small", [P, 2048])
        silu = sb("silu", [P, D])
        cols = sb("cols", [P, NCOLS])
        mod = sb("mod", [P, 2 * MODS])
        modc = sb("modc", [P, 2 * DC])
        gain = sb("gain", [P, 5 * DC])
        sel_i = sb("sel_i", [P, T])
        sel_j = sb("sel_j", [P, T])
        sel_g = sb("sel_g", [P, T])
        ident = sb("ident", [P, P])
        iota = sb("iota", [P, P])
        ones = sb("ones", [P, P])
        zero = sb("zero", [P, 8])
        rstd = sb("rstd", [P, 512])
        arena_off = (nc.sbuf_base + 31) // 32 * 32
        arena = sb("arena", [P, NK * T])
        ps = ctx.enter_context(nc.psum_tensor("ps", [P, 8, 512], F32))

        def cut(at, *shape):
            n = int(np.prod(shape))
            v = arena[:, at:at + n]
            if len(shape) == 1:
                return v
            names = "abcde"[:len(shape)]
            return v.rearrange(f"p ({' '.join(names)}) -> p {' '.join(names)}", **{k: s for k, s in zip(names[1:], shape[1:])})

        def scut(at, *shape):
            n = int(np.prod(shape))
            v = small[:, at:at + n]
            if len(shape) == 1:
                return v
            names = "abcde"[:len(shape)]
            return v.rearrange(f"p ({' '.join(names)}) -> p {' '.join(names)}", **{k: s for k, s in zip(names[1:], shape[1:])})

        def col(name, k, rows=P):
            return cols[0:rows, COLS[name][0] + k:COLS[name][0] + k + 1]

        at = 0
        def take(*shape):
            nonlocal at
            v = cut(at, *shape)
            at += int(np.prod(shape))
            return v
        cx = take(DC, T)
        tmp = take(DC, T)
        silu_c = take(D)
        junk = take(D)
        q_heads = cut(0, HEADS, T)
        lat = take(DKV, 512)
        w_uq = take(QC, HEADS, P)
        v_keys = w_uq.rearrange("p a b c -> p (a b c)")[:, 0:4 * D].rearrange("p (a b) -> p a b", a=4)
        w_uk = take(KC, HEADS // 2, P)
        w_uv = take(KC, D)
        cq = take(QC, T)
        ckv = take(KC, 512)
        rope = take(T)
        rope_s = take(2, T)
        rope_c = take(2, T)
        k_heads = take(4, 512)
        c_at = at
        probs = take(2, 512)
        probs_t = take(2, 4, T)
        take(2 * DC * T - 1024 - 2048)
        smax = take(64)
        assert at <= NK * T, at
        c_hi = nc.alloc_sbuf_tensor_at("c_hi", [P, DC, T], F32R, offset=arena_off + 4 * c_at)
        c_lo = nc.alloc_sbuf_tensor_at("c_lo", [P, DC, T], F32R, offset=arena_off + 4 * (c_at + DC * T))

        tmp_flat = tmp.rearrange("p a b -> p (a b)")
        squares = probs_t.rearrange("p a b c -> p (a b c)")
        sq_q = squares[:, 0:QC * T].rearrange("p (a b) -> p a b", a=QC)
        sq_k = squares[:, QC * T:QC * T + KC * 512].rearrange("p (a b) -> p a b", a=KC)

        at = 0
        hf = take(TT, ORDER, 2, D)
        conv = cut(0, 3 * DC, T)
        k_re = take(TT, ORDER, D)
        k_im = take(TT, ORDER, D)
        hf_abs = cut(TT * ORDER * 2 * D, TT, ORDER, 2, D)
        w4_at = at
        w4 = take(4 * D)
        delta = take(ORDER, D)
        decay = take(ORDER, D)
        hf_diff = cut(w4_at, TT, ORDER, D)
        u_re = cut(w4_at, TT, D)
        u_im = cut(w4_at + 2 * D, TT, D)
        y_re = cut(w4_at + 4 * D, TT, D)
        y_im = cut(w4_at + 6 * D, TT, D)
        tr_z = take(TT, D)
        zz = take(DC, T)
        dft = take(4, TT, T)
        ctmp = tr_z
        pad = take(2, 258)
        arg = take(3, T)
        zfeat = take(T)
        w1 = take(FFN)
        w23 = take(2, FFN)
        fcol = take(4)
        inv_norm = take(ORDER * DC)
        hrt = cut(3 * DC * T, 2, T)
        assert at <= NK * T, at

        hf_all = cut(0, TT * ORDER * 2 * D)
        hf_abs5 = hf_abs
        hf_abs = cut(TT * ORDER * 2 * D, TT * ORDER * 2 * D)
        hf_sum = hf[:, :, :, 0, :]

        acts = cut(0, NK, T)
        q_all = cut(86 * T, HP, T)
        keys = cut(102 * T, HP, P)
        scores = cut(112 * T, TT, HP, P)
        newton = sb("newton", [P, 2 * T])
        eq = newton[:, :].rearrange("p (a b c) -> p a b c", a=2, b=TOPK)
        gelu_out = newton[:, :].rearrange("p (a b) -> p a b", a=2)
        fs = scut(0, TT, PH * TOPK)
        fi_i = scut(256, TT, PH * TOPK)
        fi_j = scut(512, TT, PH * TOPK)
        sv = scut(768, 2, TOPK)
        si_u = scut(800, 2, TOPK).bitcast(U32)
        si_f = scut(832, 2, TOPK)
        cand = scut(864, TOPK, TOPK)
        cand_flat = scut(864, TOPK * TOPK)
        rest = scut(1120, 2, P)
        rest_flat = scut(1120, TOPK * TOPK)
        keys_of = scut(1376, 2, TOPK)
        fi_u = scut(1632, TOPK).bitcast(U32)
        fa_u = scut(1648, 2, TOPK).bitcast(U32)
        fa_f = scut(1680, 2, TOPK)
        fsum = scut(1712, TT * PH)
        fs_one = scut(1984, TOPK)
        pair = scut(1728, 2, P)
        oh_i = scut(0, 2, 4, P)
        oh_j = scut(1024, 2, 4, P)
        mod_raw = scut(0, 2, D)
        scores_v = cut(112 * T, TT * PH, 2 * P)
        fs_v = scut(0, TT * PH, TOPK)
        fi_i_v = scut(256, TT * PH, TOPK)
        fi_j_v = scut(512, TT * PH, TOPK)
        got = sb("got", [P, 8])

        block = ctx.enter_context(nc.Block())

        def raw_sem(n):
            return sem(f"raw_landed_{n % RAW}")

        def load_chunk(sp, name, index, n, i=0):
            if n >= RAW:
                sp.wait_ge(sem("w_lo_a_ready"), i * RAW + (n - RAW + 1))
                sp.wait_ge(sem("w_lo_b_ready"), i * RAW + (n - RAW + 1))
            sp.dma_start(raw[:, n % RAW, :], a[name][bass.ds(index, 1), :, :].rearrange("o p n -> p (o n)")).then_inc(raw_sem(n), 16)

        def half_of(n, k):
            return (2 * n + k) % SPLIT, slice(k * D // 2, (k + 1) * D // 2)

        def hi_chunk(act, n, i=0):
            act.wait_ge(raw_sem(n), i * 16 + 16 * (n // RAW + 1))
            for k in range(2):
                s, part = half_of(n, k)
                if 2 * n + k >= SPLIT:
                    act.wait_ge(sem("w_used"), i * 2 * RAW + (2 * n + k - SPLIT + 1))
                act.activation(w_hi[:, s, :], raw[:, n % RAW, part], ACT.Copy).then_inc(sem("w_hi_ready"), 1)

        def lo_chunk(dve, n, i=0):
            s, part = half_of(n, 0)
            dve.wait_ge(sem("w_hi_ready"), i * 2 * RAW + (2 * n + 1))
            dve.tensor_tensor(w_lo[:, s, :], raw[:, n % RAW, part], w_hi[:, s, :], ALU.subtract).then_inc(sem("w_lo_a_ready"), 1)

        def lo_chunk_b(pool, n, i=0):
            s, part = half_of(n, 1)
            pool.wait_ge(sem("w_hi_ready"), i * 2 * RAW + (2 * n + 2))
            pool.tensor_tensor(w_lo[:, s, :], raw[:, n % RAW, part], w_hi[:, s, :], ALU.subtract).then_inc(sem("w_lo_b_ready"), 1)

        def block_of(n, c):
            s = (2 * n + c // 4) % SPLIT
            return w_hi[:, s, (c % 4) * P:(c % 4 + 1) * P], w_lo[:, s, (c % 4) * P:(c % 4 + 1) * P]

        def product(pe, n, outs, i=0):
            for k in range(2):
                pe.wait_ge(sem("w_lo_b_ready" if k else "w_lo_a_ready"), i * RAW + (n + 1))
                for o, rh, rl in outs:
                    for c in range(4 * k, 4 * k + 4):
                        wh, wl = block_of(n, c)
                        pe.matmul(o, wh, rh[:, c, :], start=(c == 0), stop=False)
                        pe.matmul(o, wh, rl[:, c, :], start=False, stop=False)
                        last = pe.matmul(o, wl, rh[:, c, :], start=False, stop=(c == DC - 1))
                last.then_inc(sem("w_used"), 1)

        def multiplied(eng, n, i=0):
            eng.wait_ge(sem("w_used"), i * 2 * RAW + (2 * n + 2))

        def sum_bank(k):
            return ps[:, 5 if k == 3 else 0, :]

        def mod_col(l, part, c):
            k = l * MODS + part * DC + c
            return mod[:, k:k + 1]

        @block.sync
        def _(sp):
            def load_mod(k, slot=None, i=None):
                if i is None:
                    if k >= 2:
                        sp.wait_ge(sem("mod_used"), k - 1)
                    src = a["mod_w"][k]
                else:
                    sp.wait_ge(sem("mod_used"), i * 6 + (k - 1))
                    src = a["mod_w"][bass.ds(i * 6 + k, 1), :, :].rearrange("o p n -> p (o n)")
                sp.dma_start(mod_raw[:, k % 2, :], src).then_inc(sem(f"mod_landed_{k % 2}"), 16)

            def load_all(name, first=0):
                count, n0 = dict(STREAM)[name], FIRST[name]
                with sp.Fori(0, (count - first) // RAW) as i:
                    for u in range(RAW):
                        load_chunk(sp, name, i * RAW + (first + u), n0 + first + u, i)

            for k in range(2 * DC):
                load_mod(k)
            for k in range(DKV):
                load_chunk(sp, "dkv", k, k)
            load_mod(2 * DC)
            load_mod(2 * DC + 1)
            for k in range(RAW):
                load_chunk(sp, "wo", k, FIRST["wo"] + k)
            for k in range(2 * DC + 2, MODS):
                load_mod(k)
            load_all("wo", RAW)
            for l in range(2):
                load_all(f"wq{l}", 0)
                load_all(f"u{l}")
                if l == 1:
                    load_all("v1")
                    break
                n0 = FIRST["v0"]
                sp.wait_ge(sem("gates_done_0"), 1)
                with sp.Fori(0, NK // 16) as i:
                    for u in range(16):
                        n = n0 + u
                        sp.wait_ge(sem("w_lo_a_ready"), i * 16 + (n - RAW + 1))
                        sp.wait_ge(sem("w_lo_b_ready"), i * 16 + (n - RAW + 1))
                        sp.dma_start(raw[:, n % RAW, :], a["v0"][bass.ds(i * 16 + u, 1), :, :].rearrange("o p n -> p (o n)"))\
                          .then_inc(raw_sem(n), 16)
                        if u in MOD_BESIDE:
                            load_mod(MODS + MOD_BESIDE.index(u), i=i)
                for k in range(RAW):
                    load_chunk(sp, "win", k, FIRST["win"] + k)
                sp.wait_ge(sem("x_ready"), 2)
                for dst, src in ((w4[0:FFN, :], "w4"), (delta, "delta"), (dft, "dft"), (zfeat[0:EMB, :], "zfeat"),
                                 (w1[0:EMB, :], "w1"), (w23[0:FFN, :, :], "w23"), (fcol[0:FFN, :], "fcol")):
                    sp.dma_start(dst, a[src]).then_inc(sem("hyena_landed"), 16)
                load_all("win", RAW)
                load_all("wout")
            sp.wait_ge(sem("result_ready"), 1)
            sp.dma_start(out, x[:, :, :]).then_inc(sem("stored"), 16)
            sp.wait_ge(sem("stored"), 16)

        @block.gpsimd
        def _(pool):
            pool.dma_start(silu[:, :], a["c"]).then_inc(sem("c_landed"), 16)
            pool.dma_start(silu_c, a["c_ctx"]).then_inc(sem("c_landed"), 16)
            pool.dma_start(cols[:, :], a["cols"]).then_inc(sem("cols_landed"), 16)
            pool.dma_start(x[:, :, :], a["x"]).then_inc(sem("x_landed"), 16)
            pool.dma_start(cx, a["ctx"]).then_inc(sem("x_landed"), 16)
            pool.memset(ones[:, :], 1.0).then_inc(sem("ones_ready"), 1)
            pool.dma_start(ident[:, :], a["ident"]).then_inc(sem("table_landed"), 16)
            pool.dma_start(iota[:, :], a["iota"]).then_inc(sem("table_landed"), 16)
            pool.dma_start(rope, a["rope"]).then_inc(sem("attn_landed"), 16)
            pool.dma_start(w_uq, a["w_uq"]).then_inc(sem("attn_landed"), 16)
            pool.dma_start(w_uk, a["w_uk"]).then_inc(sem("attn_landed"), 16)
            pool.dma_start(w_uv, a["w_uv"]).then_inc(sem("attn_landed"), 16)
            for name, count in STREAM:
                n0 = FIRST[name]
                if name[0] == "u":
                    l = name[1]
                    with pool.Fori(0, U_TOPK // RAW) as i:
                        for u in range(RAW):
                            lo_chunk_b(pool, n0 + u, i)
                    pool.wait_ge(sem(f"scores_copied_{l}"), HP)
                    for u in range(RAW):
                        lo_chunk_b(pool, n0 + U_TOPK + u)
                        if u == 0:
                            pool.wait_ge(sem(f"topk_done_{l}"), 1)
                        step = (NK - U_GATED) // RAW
                        j = U_GATED + u * step
                        pool.memset(acts[:, j:j + step, :], 1.0).then_inc(sem(f"ones_in_place_{l}"), 1)
                    with pool.Fori(0, GATE_STEPS) as i:
                        for u in range(RAW):
                            lo_chunk_b(pool, n0 + U_GATED + u, i)
                elif count % RAW:
                    for k in range(count):
                        lo_chunk_b(pool, n0 + k)
                else:
                    with pool.Fori(0, count // RAW) as i:
                        for u in range(RAW):
                            lo_chunk_b(pool, n0 + u, i)

        @block.scalar
        def _(act):
            def square(k, src, dst):
                act.activation(dst, src, ACT.Square).then_inc(sem("square_ready"), 1)

            def root(k, width, features=D):
                act.wait_ge(sem("sum_ready"), k + 1)
                act.activation(rstd[:, 0:width], sum_bank(k)[:, 0:width], ACT.Sqrt, bias=zero[:, 1:2],
                               scale=1.0 / features).then_inc(sem("root_ready"), 1)

            def split(s, src, hi):
                act.wait_ge(sem("to_split"), s + 1)
                act.activation(hi[:, :, :], src, ACT.Copy).then_inc(sem("h_hi_ready"), 1)

            act.wait_ge(sem("c_landed"), 32)
            act.activation(tmp_flat[:, 0:D], silu[:, :], ACT.Exp, scale=-1.0).then_inc(sem("c_exp"), 1)
            act.activation(tmp_flat[:, D:2 * D], silu_c, ACT.Exp, scale=-1.0).then_inc(sem("c_exp"), 1)

            act.wait_ge(sem("x_landed"), 32)
            act.wait_ge(sem("silu_ready"), 1)
            square(0, x[:, :, :], tmp)
            root(0, T)
            split(0, tmp, h_hi)
            act.wait_ge(sem("h_lo_ready"), 1)
            square(1, cx, tmp)
            root(1, T)
            split(1, tmp, c_hi)

            def lat_copy(m):
                multiplied(act, m)
                last = act.activation(lat[:, m, 0:T], ps[:, 1 + m % 2, 0:T], ACT.Copy)
                if m >= QC:
                    last = act.activation(lat[:, m, T:2 * T], ps[:, 3 + m % 2, 0:T], ACT.Copy)
                last.then_inc(sem("lat_ready"), 1)

            for m in range(DKV):
                hi_chunk(act, m)
                if m:
                    lat_copy(m - 1)
            lat_copy(DKV - 1)
            act.wait_ge(sem("lat_ready"), DKV)
            square(2, lat[:, 0:QC, 0:T], sq_q)
            square(3, lat[:, QC:QC + KC, :], sq_k)
            root(2, T, QL)
            act.wait_ge(sem("cq_ready"), 1)
            root(3, 512, KVL)
            for p in range(HEADS // 2):
                act.wait_ge(sem("q_ready"), p + 1)
                act.activation(q_heads[0:NOPE, 2 * p:2 * p + 2, :], ps[0:NOPE, 1 + p % 2, :].rearrange("p (a b) -> p a b", a=2),
                               ACT.Copy).then_inc(sem("q_nope_ready"), 1)
            for k in range(8):
                act.wait_ge(sem("v_ready"), k + 1)
                act.activation(v_keys[:, k // 2, (k % 2) * 512:(k % 2 + 1) * 512], ps[:, 3 + k % 2, :], ACT.Copy)\
                   .then_inc(sem("v_keys_ready"), 1)
            for p in range(HEADS // 2):
                act.wait_ge(sem("k_ready"), p + 1)
                if p >= 2:
                    act.wait_ge(sem("scores_ready"), 4 * (p - 1))
                for j in range(2):
                    act.activation(k_heads[0:NOPE, (2 * p + j) % 4, :], ps[j * NOPE:(j + 1) * NOPE, 1, :], ACT.Copy)\
                       .then_inc(sem("k_heads_ready"), 1)
                for u in range(4 * p, 4 * p + 4):
                    act.wait_ge(sem("max_ready"), u + 1)
                    if u >= 2:
                        act.wait_ge(sem("turned"), u - 1)
                    act.activation(probs[:, u % 2, :], ps[:, 2 + u % 2, :], ACT.Exp, bias=smax[:, u % 8:u % 8 + 1],
                                   scale=SCALE, accum_out=smax[:, 8 + u % 8:9 + u % 8]).then_inc(sem("exp_ready"), 1)
                for hh in (2 * p, 2 * p + 1):
                    o = (hh % 2) * VD
                    act.wait_ge(sem("o_ready"), hh + 1)
                    act.activation(h_hi[o:o + VD, p, :], ps[0:VD, 6 + hh % 2, 0:T], ACT.Copy).then_inc(sem("o_hi_ready"), 1)
            for m in range(DC):
                hi_chunk(act, FIRST["wo"] + m)

            def input_norm(k, s, residual):
                act.wait_ge(sem("x_ready"), residual)
                square(k, x[:, :, :], tmp)
                root(k, T)
                split(s, tmp, h_hi)

            def retrieval(l):
                n0 = FIRST[f"wq{l}"]

                def q_copy(i, u):
                    multiplied(act, n0 + u, i)
                    act.activation(q_all[:, bass.ds(i * RAW + u, 1), :], ps[:, 4 + u, 0:T].unsqueeze(1), ACT.Copy)\
                       .then_inc(sem(f"q_all_ready_{l}"), 1)

                hi_chunk(act, n0)
                with act.Fori(0, HP // RAW - 1) as i:
                    for u in range(RAW):
                        hi_chunk(act, n0 + u + 1, i)
                        q_copy(i, u)
                for u in range(RAW):
                    if u < RAW - 1:
                        hi_chunk(act, n0 + HP - RAW + u + 1)
                    q_copy(HP // RAW - 1, u)
                for m in range(HP):
                    act.wait_ge(sem(f"key_scores_{l}"), m + 1)
                    act.activation(scores[:, :, m, :], ps[:, 4 + m % 4, 0:T].rearrange("p (a b) -> p a b", a=TT), ACT.Copy)\
                       .then_inc(sem(f"scores_copied_{l}"), 1)
                n0 = FIRST[f"u{l}"]

                def gelu(i, u):
                    multiplied(act, n0 + u, i)
                    act.activation(acts[:, bass.ds(i * RAW + u, 1), :], ps[:, 4 + u, 0:T].unsqueeze(1), ACT.Gelu)\
                       .then_inc(sem(f"acts_ready_{l}"), 1)

                def gelu_beside(i, u):
                    act.wait_ge(sem(f"gelu_slots_{l}"), i * RAW + (u + 1))
                    multiplied(act, n0 + U_GATED + u, i)
                    act.activation(gelu_out[:, u % 2, :], ps[:, 4 + u, 0:T], ACT.Gelu).then_inc(sem(f"acts_ready_{l}"), 1)

                hi_chunk(act, n0)
                with act.Fori(0, U_TOPK // RAW) as i:
                    for u in range(RAW):
                        hi_chunk(act, n0 + u + 1, i)
                        gelu(i, u)
                for u in range(RAW):
                    hi_chunk(act, n0 + U_TOPK + u + 1)
                    gelu(U_TOPK // RAW, u)
                    if u == 0:
                        act.wait_ge(sem(f"topk_done_{l}"), 1)
                        act.activation(fs_v, fs_v, ACT.Exp).then_inc(sem(f"fs_exp_{l}"), 1)
                with act.Fori(0, GATE_STEPS - 1) as i:
                    for u in range(RAW):
                        hi_chunk(act, n0 + U_GATED + u + 1, i)
                        gelu_beside(i, u)
                for u in range(RAW):
                    if u < RAW - 1:
                        hi_chunk(act, n0 + NK - RAW + u + 1)
                    gelu_beside(GATE_STEPS - 1, u)
                n0 = FIRST[f"v{l}"]
                act.wait_ge(sem(f"gates_done_{l}"), 1)
                with act.Fori(0, NK // RAW) as i:
                    for u in range(RAW):
                        hi_chunk(act, n0 + u, i)
                        act.activation(h_hi[:, u, :], acts[:, bass.ds(i * RAW + u, 1), :].rearrange("p o t -> p (o t)"), ACT.Copy)\
                           .then_inc(sem(f"g_hi_ready_{l}"), 1)

            def load_keys(l):
                act.dma_start(keys, a["keys"][l]).then_inc(sem("keys_landed"), 16)

            input_norm(4, 2, 1)
            load_keys(0)
            retrieval(0)

            act.wait_ge(sem("hyena_landed"), 16 * 7)
            for k in range(3):
                act.wait_ge(sem("arg_ready"), k + 1)
                act.activation(arg[0:FFN, 2, :], arg[0:FFN, 0, :], ACT.Sin).then_inc(sem("sin_ready"), 1)
            act.activation(delta, delta, ACT.Abs).then_inc(sem("delta_abs"), 1)
            act.wait_ge(sem("delta_abs"), 1)
            for mt in range(TT):
                if mt:
                    act.wait_ge(sem("hf_ready"), 8)
                act.activation(decay, delta, ACT.Exp, scale=col("neg_t", mt)).then_inc(sem("decay_ready"), 1)
            act.wait_ge(sem("hf_zeroed"), 1)
            act.activation(hf_abs, hf_all, ACT.Abs).then_inc(sem("hf_abs_ready"), 1)
            for k in range(16):
                part, kt, o, half = k // 8, (k // 4) % 2, (k // 2) % 2, k % 2
                act.wait_ge(sem("kf_ready"), k + 1)
                act.activation((k_re, k_im)[part][:, kt, o, half * 512:half * 512 + 512], ps[:, 4 + k % 4, :], ACT.Copy)\
                   .then_inc(sem("kf_copied"), 1)
            input_norm(5, 3, 2)
            n0 = FIRST["win"]

            def p_copy(m):
                multiplied(act, n0 + m)
                if m >= 2:
                    act.wait_ge(sem("conv_done"), m - 1)
                act.activation(pad[:, m % 2, 1:T + 1], ps[:, 4 + m % 4, 0:T], ACT.Copy).then_inc(sem("p_copied"), 1)

            act.wait_ge(sem("pad_ready"), 1)
            for m in range(3 * DC):
                hi_chunk(act, n0 + m)
                if m:
                    p_copy(m - 1)
            p_copy(3 * DC - 1)
            for o in range(ORDER):
                for k in range(4):
                    act.wait_ge(sem("z_turned"), 4 * o + k + 1)
                    act.activation(tr_z[:, k // 2, (k % 2) * 512:(k % 2) * 512 + 512], ps[:, 4 + k % 4, :], ACT.Copy)\
                       .then_inc(sem("tr_z_ready"), 1)
                if o:
                    act.wait_ge(sem("yf_ready"), o)
                for k in range(8):
                    part, kt, half = k // 4, (k // 2) % 2, k % 2
                    act.wait_ge(sem("uf_ready"), 8 * o + k + 1)
                    act.activation((u_re, u_im)[part][:, kt, half * 512:half * 512 + 512], ps[:, k % 4, :], ACT.Copy)\
                       .then_inc(sem("uf_copied"), 1)
            split(4, zz, h_hi)
            for m in range(DC):
                hi_chunk(act, FIRST["wout"] + m)
            input_norm(6, 5, 3)
            load_keys(1)
            retrieval(1)
            act.wait_ge(sem("x_ready"), 4)
            square(7, x[:, :, :], tmp)
            root(7, T)

        @block.tensor
        def _(pe):
            def sums(k, src, chunks, width):
                pe.wait_ge(sem("square_ready"), k + 1)
                if k:
                    pe.wait_ge(sem("root_ready"), k)
                for c in range(chunks):
                    last = pe.matmul(sum_bank(k)[:, 0:width], ones[:, :], src[:, c, :], start=(c == 0), stop=(c == chunks - 1))
                last.then_inc(sem("sum_ready"), 1)

            pe.wait_ge(sem("ones_ready"), 1)
            sums(0, tmp, DC, T)
            sums(1, tmp, DC, T)
            pe.wait_ge(sem("h_lo_ready"), 2)
            for m in range(DKV):
                if m >= 2:
                    pe.wait_ge(sem("lat_ready"), m - 1)
                outs = [(ps[:, 1 + m % 2, 0:T], h_hi, h_lo)]
                if m >= QC:
                    outs.append((ps[:, 3 + m % 2, 0:T], c_hi, c_lo))
                product(pe, m, outs)
            sums(2, sq_q, QC, T)
            sums(3, sq_k, KC, 512)
            pe.wait_ge(sem("attn_landed"), 64)
            pe.wait_ge(sem("cq_ready"), 1)
            for p in range(HEADS // 2):
                if p >= 2:
                    pe.wait_ge(sem("q_nope_ready"), p - 1)
                    pe.wait_ge(sem("q_rope_ready"), p - 1)
                for j in range(2):
                    for c in range(QC):
                        last = pe.matmul(ps[:, 1 + p % 2, j * T:(j + 1) * T], w_uq[:, c, 2 * p + j, :], cq[:, c, :],
                                         start=(c == 0), stop=(c == QC - 1))
                last.then_inc(sem("q_ready"), 1)
            pe.wait_ge(sem("ckv_ready"), 1)
            for k in range(8):
                if k >= 2:
                    pe.wait_ge(sem("v_keys_ready"), k - 1)
                for c in range(KC):
                    last = pe.matmul(ps[:, 3 + k % 2, :], ckv[:, c, (k // 2) * P:(k // 2 + 1) * P],
                                     w_uv[:, c, (k % 2) * 512:(k % 2 + 1) * 512], start=(c == 0), stop=(c == KC - 1))
                last.then_inc(sem("v_ready"), 1)
            pe.wait_ge(sem("v_keys_ready"), 8)
            pe.wait_ge(sem("q_nope_ready"), 8)
            pe.wait_ge(sem("q_rope_ready"), 8)
            pe.wait_ge(sem("k_rope_ready"), 1)

            def score(u):
                hh, qt = u // 2, u % 2
                pe.wait_ge(sem("k_heads_ready"), hh + 1)
                if u >= 2:
                    pe.wait_ge(sem("exp_ready"), u - 1)
                pe.matmul(ps[:, 2 + u % 2, :], q_heads[0:QK, hh, qt * P:(qt + 1) * P], k_heads[0:QK, hh % 4, :], start=True, stop=True)\
                  .then_inc(sem("scores_ready"), 1)

            def turn(u):
                pe.wait_ge(sem("probs_ready"), u + 1)
                if u >= 2:
                    pe.wait_ge(sem("probs_t_ready"), u - 1)
                for k in range(4):
                    last = pe.transpose(ps[:, 4 + u % 2, k * P:(k + 1) * P], probs[:, u % 2, k * P:(k + 1) * P], ident[:, :])
                last.then_inc(sem("turned"), 1)

            def mix(hh):
                pe.wait_ge(sem("probs_t_ready"), 2 * hh + 2)
                if hh >= 2:
                    pe.wait_ge(sem("o_lo_ready"), hh - 1)
                for k in range(4):
                    last = pe.matmul(ps[0:VD, 6 + hh % 2, 0:T], v_keys[:, k, hh * VD:(hh + 1) * VD], probs_t[:, hh % 2, k, :],
                                     start=(k == 0), stop=(k == 3))
                last.then_inc(sem("o_ready"), 1)

            pe.wait_ge(sem("table_landed"), 32)
            for p in range(HEADS // 2):
                if p:
                    pe.wait_ge(sem("k_heads_ready"), 2 * p)
                for c in range(KC):
                    last = pe.matmul(ps[:, 1, :], w_uk[:, c, p, :], ckv[:, c, :], start=(c == 0), stop=(c == KC - 1))
                last.then_inc(sem("k_ready"), 1)
                u = 4 * p
                score(u)
                score(u + 1)
                turn(u)
                score(u + 2)
                turn(u + 1)
                mix(2 * p)
                score(u + 3)
                turn(u + 2)
                turn(u + 3)
                mix(2 * p + 1)

            def residual_products(name):
                for m in range(DC):
                    if m >= 2:
                        pe.wait_ge(sem(f"{name}_added"), m - 1)
                    product(pe, FIRST[name] + m, [(ps[:, 1 + m % 2, 0:T], h_hi, h_lo)])

            pe.wait_ge(sem("o_lo_ready"), HEADS)
            residual_products("wo")

            def retrieval(l):
                n0 = FIRST[f"wq{l}"]
                for u in range(RAW):
                    product(pe, n0 + u, [(ps[:, 4 + u, 0:T], h_hi, h_lo)])
                with pe.Fori(1, HP // RAW) as i:
                    for u in range(RAW):
                        pe.wait_ge(sem(f"q_all_ready_{l}"), i * RAW + (u + 1 - RAW))
                        product(pe, n0 + u, [(ps[:, 4 + u, 0:T], h_hi, h_lo)], i)
                pe.wait_ge(sem("keys_landed"), 16 * (l + 1))
                pe.wait_ge(sem(f"q_all_ready_{l}"), HP)
                for m in range(HP):
                    if m >= 4:
                        pe.wait_ge(sem(f"scores_copied_{l}"), m - 3)
                    for tt in range(TT):
                        last = pe.matmul(ps[:, 4 + m % 4, tt * P:(tt + 1) * P], q_all[:, m, tt * P:(tt + 1) * P], keys[:, m, :],
                                         start=True, stop=True)
                    last.then_inc(sem(f"key_scores_{l}"), 1)
                n0 = FIRST[f"u{l}"]
                pe.wait_ge(sem(f"scores_copied_{l}"), HP)
                for u in range(RAW):
                    product(pe, n0 + u, [(ps[:, 4 + u, 0:T], h_hi, h_lo)])
                with pe.Fori(1, U_TOPK // RAW) as i:
                    for u in range(RAW):
                        pe.wait_ge(sem(f"acts_ready_{l}"), i * RAW + (u + 1 - RAW))
                        product(pe, n0 + u, [(ps[:, 4 + u, 0:T], h_hi, h_lo)], i)
                for u in range(RAW):
                    pe.wait_ge(sem(f"acts_ready_{l}"), U_TOPK + u + 1 - RAW)
                    product(pe, n0 + U_TOPK + u, [(ps[:, 4 + u, 0:T], h_hi, h_lo)])
                    if u == 2:
                        pe.wait_ge(sem(f"sel_ready_{l}"), 1)
                        for k, src in enumerate((fi_i, fi_j, fs)):
                            for tt in range(TT):
                                last = pe.transpose(ps[:, k, tt * P:(tt + 1) * P], src[:, tt, :], ident[:, :])
                        last.then_inc(sem(f"sel_turned_{l}"), 1)

                def gates(b, g):
                    pe.wait_ge(sem(f"onehot_ready_{l}"), g + 1)
                    for t in range(4):
                        last = pe.matmul(ps[:, b, t * P:(t + 1) * P], oh_i[:, b, t, :], oh_j[:, b, t, :], start=True, stop=True)
                    last.then_inc(sem(f"gate_ready_{l}"), 1)

                with pe.Fori(0, GATE_STEPS) as i:
                    for u in range(RAW):
                        pe.wait_ge(sem(f"acts_ready_{l}"), i * RAW + (U_GATED + u + 1 - RAW))
                        product(pe, n0 + U_GATED + u, [(ps[:, 4 + u, 0:T], h_hi, h_lo)], i)
                        gates(u % 2, i * RAW + u)
                for g in range(GATE_STEPS * RAW, GROUPS):
                    gates(g % 2, g)
                pe.wait_ge(sem(f"zeros_ready_{l}"), 1)
                for b in range(4):
                    pe.matmul(ps[:, b, :], ones[:, :], rstd[:, :], start=True, stop=False, skip_group_check=True)
                n0 = FIRST[f"v{l}"]
                with pe.Fori(0, NK // RAW) as i:
                    for u in range(RAW):
                        n = n0 + u
                        pe.wait_ge(sem(f"g_lo_ready_{l}"), i * RAW + (u + 1))
                        for k in range(2):
                            pe.wait_ge(sem("w_lo_b_ready" if k else "w_lo_a_ready"), i * RAW + (n + 1))
                            for c in range(4 * k, 4 * k + 4):
                                o = ps[:, c // 2, (c % 2) * T:(c % 2 + 1) * T]
                                wh, wl = block_of(n, c)
                                pe.matmul(o, wh, h_hi[:, u, :], start=False, stop=False, skip_group_check=True)
                                pe.matmul(o, wh, h_lo[:, u, :], start=False, stop=False, skip_group_check=True)
                                last = pe.matmul(o, wl, h_hi[:, u, :], start=False, stop=False, skip_group_check=True)
                            last.then_inc(sem("w_used"), 1)

            sums(4, tmp, DC, T)
            pe.wait_ge(sem("h_lo_ready"), 3)
            retrieval(0)

            pe.wait_ge(sem("hyena_landed"), 16 * 7)
            pe.wait_ge(sem("x_ready"), 2)
            pe.matmul(ps[0:FFN, 4, 0:T], w1[0:EMB, :], zfeat[0:EMB, :], start=True, stop=True).then_inc(sem("ffn_ready"), 1)
            for k in range(2):
                pe.wait_ge(sem("sin_ready"), k + 1)
                pe.matmul(ps[0:FFN, 5 + k, 0:T], w23[0:FFN, k, :], arg[0:FFN, 2, :], start=True, stop=True).then_inc(sem("ffn_ready"), 1)
            pe.wait_ge(sem("sin_ready"), 3)
            for k in range(16):
                mt, blk = k // 8, k % 8
                if k >= 4:
                    pe.wait_ge(sem("hf_ready"), k - 3)
                pe.matmul(ps[:, 4 + k % 4, :], arg[0:FFN, 2, mt * P:(mt + 1) * P], w4[0:FFN, blk * 512:(blk + 1) * 512], start=True, stop=True)\
                  .then_inc(sem("hf_prod"), 1)
            pe.wait_ge(sem("hf_abs_ready"), 1)
            for o in range(ORDER):
                for c in range(DC):
                    for k in range(4):
                        last = pe.matmul(ps[:, 0, o * DC + c:o * DC + c + 1], hf_abs5[:, k // 2, o, k % 2, c * P:(c + 1) * P], ones[:, 0:1],
                                         start=(k == 0), stop=(k == 3))
            last.then_inc(sem("norm_sum"), 1)
            pe.wait_ge(sem("hf_mixed"), 1)
            for k in range(16):
                part, kt, o, half = k // 8, (k // 4) % 2, (k // 2) % 2, k % 2
                if k >= 4:
                    pe.wait_ge(sem("kf_copied"), k - 3)
                src = hf_diff if part else hf_sum
                for mt in range(TT):
                    last = pe.matmul(ps[:, 4 + k % 4, :], dft[:, part, mt, kt * P:(kt + 1) * P], src[:, mt, o, half * 512:half * 512 + 512],
                                     start=(mt == 0), stop=(mt == TT - 1))
                last.then_inc(sem("kf_ready"), 1)
            pe.wait_ge(sem("inv_norm_ready"), 1)
            sums(5, tmp, DC, T)
            pe.wait_ge(sem("h_lo_ready"), 4)
            for m in range(3 * DC):
                if m >= 4:
                    pe.wait_ge(sem("p_copied"), m - 3)
                product(pe, FIRST["win"] + m, [(ps[:, 4 + m % 4, 0:T], h_hi, h_lo)])
            for o in range(ORDER):
                if o == 0:
                    pe.wait_ge(sem("conv_done"), DC)
                    pe.wait_ge(sem("p_copied"), 3 * DC)
                    src = conv
                else:
                    pe.wait_ge(sem("z_ready"), DC)
                    src = zz
                for k in range(4):
                    for j in range(4):
                        last = pe.transpose(ps[:, 4 + k, j * P:(j + 1) * P], src[:, (k % 2) * 4 + j, (k // 2) * P:(k // 2 + 1) * P], ident[:, :])
                    last.then_inc(sem("z_turned"), 1)
                pe.wait_ge(sem("tr_z_ready"), 4 * (o + 1))
                for k in range(8):
                    part, kt, half = k // 4, (k // 2) % 2, k % 2
                    if k >= 4:
                        pe.wait_ge(sem("uf_copied"), 8 * o + k - 3)
                    for mt in range(TT):
                        last = pe.matmul(ps[:, k % 4, :], dft[:, part, mt, kt * P:(kt + 1) * P], tr_z[:, mt, half * 512:half * 512 + 512],
                                         start=(mt == 0), stop=(mt == TT - 1))
                    last.then_inc(sem("uf_ready"), 1)
                pe.wait_ge(sem("yf_ready"), o + 1)
                for c in range(DC):
                    if c >= 4:
                        pe.wait_ge(sem("z_ready"), DC * o + c - 3)
                    for k in range(4):
                        part, kt = k // 2, k % 2
                        last = pe.matmul(ps[:, 4 + c % 4, 0:T], (y_re, y_im)[part][:, kt, c * P:(c + 1) * P], dft[:, 2 + part, kt, :],
                                         start=(k == 0), stop=(k == 3))
                    last.then_inc(sem("yt_ready"), 1)
            pe.wait_ge(sem("h_lo_ready"), 5)
            residual_products("wout")
            sums(6, tmp, DC, T)
            pe.wait_ge(sem("h_lo_ready"), 6)
            retrieval(1)
            sums(7, tmp, DC, T)

        @block.vector
        def _(dve):
            ch = Chain(dve, sem("dve_chain"))
            link = ch.link

            def b_cols(name, k, n):
                return cols[:, COLS[name][0] + k:COLS[name][0] + k + n]

            def gain_of(g, m, name, k):
                link(dve.scalar_tensor_tensor(out=gain[:, g * DC:(g + 1) * DC], in0=m, scalar=1.0, in1=b_cols(name, k, DC),
                                              op0=ALU.add, op1=ALU.mult))

            def normalise(k, src, dst, width, chunks, features=D):
                dve.wait_ge(sem("root_ready"), k + 1)
                r, e = rstd[:, 0:width], newton[:, 0:width]
                link(dve.reciprocal(r, r))
                link(dve.tensor_tensor(e, r, r, ALU.mult))
                total = sum_bank(k)[:, 0:width]
                link(dve.scalar_tensor_tensor(out=total, in0=total, scalar=features * EPS, in1=e, op0=ALU.add, op1=ALU.mult))
                link(dve.tensor_scalar(e, total, -0.5 / features, 1.5, ALU.mult, ALU.add))
                link(dve.tensor_tensor(r, r, e, ALU.mult))
                link(dve.tensor_tensor(dst, src, rstd[:, 0:width].unsqueeze(1).broadcast_to([P, chunks, width]), ALU.mult))

            def modulated(k, s, src, g, shift, hi, lo):
                normalise(k, src, tmp, T, DC)
                for c in range(DC):
                    last = dve.tensor_scalar(tmp[:, c, :], tmp[:, c, :], gain[:, g * DC + c:g * DC + c + 1], shift(c), ALU.mult, ALU.add)
                last.then_inc(sem("to_split"), 1)
                dve.wait_ge(sem("to_split"), s + 1)
                low(s, tmp, hi, lo)

            def low(s, src, hi, lo):
                dve.wait_ge(sem("h_hi_ready"), s + 1)
                dve.tensor_tensor(lo[:, :, :], src, hi[:, :, :], ALU.subtract).then_inc(sem("h_lo_ready"), 1)

            link(dve.memset(zero[:, :], 0.0))
            link(dve.memset(zero[:, 1:2], EPS))
            dve.wait_ge(sem("c_exp"), 2)
            link(dve.tensor_scalar(tmp_flat, tmp_flat, 1.0, None, ALU.add))
            link(dve.reciprocal(tmp_flat, tmp_flat))
            link(dve.tensor_tensor(silu[:, :], silu[:, :], tmp_flat[:, 0:D], ALU.mult))
            dve.tensor_tensor(silu_c, silu_c, tmp_flat[:, D:2 * D], ALU.mult).then_inc(sem("silu_ready"), 1)
            dve.wait_ge(sem("silu_ready"), 1)
            dve.wait_ge(sem("cols_landed"), 16)

            def dot(k, slot, dst):
                dve.tensor_tensor_reduce(mod_raw[:, slot, :], mod_raw[:, slot, :], silu[:, :], 1.0, 0.0, ALU.mult, ALU.add, dst)\
                   .then_inc(sem("mod_used"), 1)

            for k in range(2 * DC):
                dve.wait_ge(sem(f"mod_landed_{k % 2}"), 16 * (k // 2 + 1))
                link(dve.tensor_tensor_reduce(junk, mod_raw[:, k % 2, :], silu_c, 1.0, 0.0, ALU.mult, ALU.add, modc[:, k:k + 1]))
                dot(k, k % 2, mod[:, k:k + 1])
            dve.wait_ge(sem("mod_used"), 2 * DC)
            link(dve.tensor_tensor(mod[:, 0:2 * DC], mod[:, 0:2 * DC], b_cols("mod_b", 0, 2 * DC), ALU.add))
            link(dve.tensor_tensor(modc[:, :], modc[:, :], b_cols("mod_b", 0, 2 * DC), ALU.add))
            gain_of(0, mod[:, DC:2 * DC], "mix_g", 0)
            gain_of(1, modc[:, DC:2 * DC], "mix_g", 0)
            modulated(0, 0, x[:, :, :], 0, lambda c: mod[:, c:c + 1], h_hi, h_lo)
            modulated(1, 1, cx, 1, lambda c: modc[:, c:c + 1], c_hi, c_lo)
            for m in range(DKV):
                lo_chunk(dve, m)
            normalise(2, lat[:, 0:QC, 0:T], cq, T, QC, QL)
            for c in range(QC):
                last = dve.tensor_scalar(cq[:, c, :], cq[:, c, :], col("q_g", c), None, ALU.mult)
            last.then_inc(sem("cq_ready"), 1)
            normalise(3, lat[:, QC:QC + KC, :], ckv, 512, KC, KVL)
            for c in range(KC):
                last = dve.tensor_scalar(ckv[:, c, :], ckv[:, c, :], col("kv_g", c), None, ALU.mult)
            last.then_inc(sem("ckv_ready"), 1)
            dve.wait_ge(sem("attn_landed"), 64)
            lr = lat[:, DKV - 1, :]
            link(dve.tensor_tensor(rope_s[NOPE:QK, 0, :], lr[QK:P, 0:T], rope[QK:P, :], ALU.mult))
            link(dve.tensor_tensor(rope_c[NOPE:QK, 0, :], lr[NOPE:QK, 0:T], rope[NOPE:QK, :], ALU.mult))
            for s in range(4):
                dve.tensor_tensor(k_heads[NOPE:QK, s, 0:T], rope_s[NOPE:QK, 0, :], rope_c[NOPE:QK, 0, :], ALU.add)
                last = dve.tensor_copy(k_heads[NOPE:QK, s, T:2 * T], lr[NOPE:QK, T:2 * T])
            last.then_inc(sem("k_rope_ready"), 1)
            dve.wait_ge(sem("k_rope_ready"), 1)
            for p in range(HEADS // 2):
                dve.wait_ge(sem("q_ready"), p + 1)
                bank = ps[:, 1 + p % 2, :].rearrange("p (a b) -> p a b", a=2)
                link(dve.tensor_tensor(rope_s[NOPE:QK, :, :], bank[QK:P, :, :], rope[QK:P, :].unsqueeze(1).broadcast_to([ROPE, 2, T]), ALU.mult))
                link(dve.tensor_tensor(rope_c[NOPE:QK, :, :], bank[NOPE:QK, :, :], rope[NOPE:QK, :].unsqueeze(1).broadcast_to([ROPE, 2, T]), ALU.mult))
                dve.tensor_tensor(q_heads[NOPE:QK, 2 * p:2 * p + 2, :], rope_s[NOPE:QK, :, :], rope_c[NOPE:QK, :, :], ALU.add)\
                   .then_inc(sem("q_rope_ready"), 1)
                dve.wait_ge(sem("q_rope_ready"), p + 1)

            def row_max(u):
                dve.wait_ge(sem("scores_ready"), u + 1)
                k = u % 8
                if u >= 8:
                    dve.wait_ge(sem("exp_ready"), u - 7)
                link(dve.tensor_reduce(smax[:, 24 + k:25 + k], ps[:, 2 + u % 2, :], AX.X, ALU.max))
                dve.tensor_scalar(smax[:, k:k + 1], smax[:, 24 + k:25 + k], -SCALE, None, ALU.mult).then_inc(sem("max_ready"), 1)

            def norm_probs(u):
                dve.wait_ge(sem("exp_ready"), u + 1)
                k = u % 8
                link(dve.reciprocal(smax[:, 16 + k:17 + k], smax[:, 8 + k:9 + k]))
                dve.tensor_scalar(probs[:, u % 2, :], probs[:, u % 2, :], smax[:, 16 + k:17 + k], None, ALU.mult).then_inc(sem("probs_ready"), 1)

            def copy_turned(u):
                dve.wait_ge(sem("turned"), u + 1)
                hh = u // 2
                if hh >= 2:
                    dve.wait_ge(sem("o_ready"), hh - 1)
                dve.tensor_copy(probs_t[:, hh % 2, :, (u % 2) * P:(u % 2 + 1) * P], ps[:, 4 + u % 2, :].rearrange("p (a b) -> p a b", a=4))\
                   .then_inc(sem("probs_t_ready"), 1)

            for p in range(HEADS // 2):
                u = 4 * p
                row_max(u)
                row_max(u + 1)
                norm_probs(u)
                copy_turned(u)
                row_max(u + 2)
                norm_probs(u + 1)
                copy_turned(u + 1)
                row_max(u + 3)
                norm_probs(u + 2)
                copy_turned(u + 2)
                norm_probs(u + 3)
                copy_turned(u + 3)
                for hh in (2 * p, 2 * p + 1):
                    o = (hh % 2) * VD
                    dve.wait_ge(sem("o_hi_ready"), hh + 1)
                    dve.tensor_tensor(h_lo[o:o + VD, p, :], ps[0:VD, 6 + hh % 2, 0:T], h_hi[o:o + VD, p, :], ALU.subtract)\
                       .then_inc(sem("o_lo_ready"), 1)
                for k in range(2 * DC + 4 * p, 2 * DC + 4 * p + 4):
                    dve.wait_ge(sem(f"mod_landed_{k % 2}"), 16 * (k // 2 + 1))
                    dot(k, k % 2, mod[:, k:k + 1])
            dve.wait_ge(sem("mod_used"), MODS)
            link(dve.tensor_tensor(mod[:, 2 * DC:MODS], mod[:, 2 * DC:MODS], b_cols("mod_b", 2 * DC, MODS - 2 * DC), ALU.add))
            gain_of(2, mod[:, 4 * DC:5 * DC], "ffn_g", 0)

            def add_residual(m, bank, l, part):
                return dve.scalar_tensor_tensor(out=x[:, m, :], in0=bank, scalar=mod_col(l, part, m), in1=x[:, m, :], op0=ALU.mult, op1=ALU.add)

            def residual(name, l):
                for m in range(DC):
                    lo_chunk(dve, FIRST[name] + m)
                    if m:
                        multiplied(dve, FIRST[name] + m - 1)
                        add_residual(m - 1, ps[:, 1 + (m - 1) % 2, 0:T], l, 2).then_inc(sem(f"{name}_added"), 1)
                multiplied(dve, FIRST[name] + DC - 1)
                add_residual(DC - 1, ps[:, 1 + (DC - 1) % 2, 0:T], l, 2).then_inc(sem("x_ready"), 1)

            residual("wo", 0)
            dve.wait_ge(sem("x_ready"), 1)
            modulated(4, 2, x[:, :, :], 2, lambda c: mod_col(0, 3, c), h_hi, h_lo)

            def top16(rows):
                dve.drain()
                for v, rest, o, x in rows:
                    dve.max(o[:, 0:8], v)
                dve.drain()
                for v, rest, o, x in rows:
                    dve.max_index(x[:, 0:8], o[:, 0:8], v)
                    dve.match_replace(rest, o[:, 0:8], v, LOWEST)
                dve.drain()
                for v, rest, o, x in rows:
                    dve.max(o[:, 8:16], rest)
                dve.drain()
                for v, rest, o, x in rows:
                    dve.max_index(x[:, 8:16], o[:, 8:16], rest)

            iota16 = iota[:, 0:TOPK].unsqueeze(1).unsqueeze(1).broadcast_to([P, 2, TOPK, TOPK])

            def retrieval(l):
                n0 = FIRST[f"wq{l}"]
                with dve.Fori(0, HP // RAW) as i:
                    for u in range(RAW):
                        lo_chunk(dve, n0 + u, i)
                n0 = FIRST[f"u{l}"]
                lo_chunk(dve, n0)
                dve.wait_ge(sem(f"scores_copied_{l}"), HP)
                with ch.loop(TT * PH, 7) as i:
                    lo_chunk(dve, n0 + 1, i)
                    dve.tensor_copy(pair, scores_v[:, bass.ds(i, 1), :].rearrange("p o (a b) -> p (o a) b", a=2))
                    top16([(pair[:, p, :], rest[:, p, :], sv[:, p, :], si_u[:, p, :]) for p in range(2)])
                    lo_chunk(dve, n0 + 2, i)
                    dve.drain()
                    dve.tensor_copy(si_f, si_u)
                    dve.tensor_tensor(cand, sv[:, 0, :].unsqueeze(2).broadcast_to([P, TOPK, TOPK]),
                                      sv[:, 1, :].unsqueeze(1).broadcast_to([P, TOPK, TOPK]), ALU.add)
                    top16([(cand_flat, rest_flat, fs_one, fi_u)])
                    lo_chunk(dve, n0 + 3, i)
                    dve.drain()
                    dve.tensor_scalar(fa_u[:, 0, :], fi_u, 4, None, ALU.logical_shift_right)
                    link(dve.tensor_scalar(fa_u[:, 1, :], fi_u, TOPK - 1, None, ALU.bitwise_and))
                    link(dve.tensor_copy(fa_f, fa_u))
                    link(dve.tensor_tensor(eq, fa_f.unsqueeze(3).broadcast_to([P, 2, TOPK, TOPK]), iota16, ALU.is_equal))
                    link(dve.tensor_tensor(eq, eq, si_f.unsqueeze(2).broadcast_to([P, 2, TOPK, TOPK]), ALU.mult))
                    lo_chunk(dve, n0 + 4, i)
                    link(dve.tensor_reduce(keys_of, eq, AX.X, ALU.add))
                    dve.tensor_copy(fi_i_v[:, bass.ds(i, 1), :].rearrange("p o k -> p (o k)"), keys_of[:, 0, :])
                    link(dve.tensor_copy(fi_j_v[:, bass.ds(i, 1), :].rearrange("p o k -> p (o k)"), keys_of[:, 1, :]))
                    link(dve.tensor_scalar(fs_v[:, bass.ds(i, 1), :].rearrange("p o k -> p (o k)"), fs_one, fs_one[:, 0:1], None, ALU.subtract))
                dve.tensor_copy(got[:, 0:1], fs_one[:, 0:1]).then_inc(sem(f"topk_done_{l}"), 1)
                lo_chunk(dve, n0 + U_TOPK + 1)
                lo_chunk(dve, n0 + U_TOPK + 2)
                dve.wait_ge(sem(f"fs_exp_{l}"), 1)
                link(dve.tensor_reduce(fsum, fs_v, AX.X, ALU.add))
                link(dve.reciprocal(fsum, fsum))
                dve.tensor_tensor(fs_v, fs_v, fsum.unsqueeze(2).broadcast_to([P, TT * PH, TOPK]), ALU.mult).then_inc(sem(f"sel_ready_{l}"), 1)
                lo_chunk(dve, n0 + U_TOPK + 3)
                lo_chunk(dve, n0 + U_GATED)
                dve.wait_ge(sem(f"sel_turned_{l}"), 1)
                link(dve.tensor_copy(sel_g[:, :], ps[:, 2, 0:T]))
                for k, dst in enumerate((sel_i, sel_j)):
                    dve.tensor_copy(dst[:, :], ps[:, k, 0:T]).then_inc(sem(f"gelu_slots_{l}"), 1)

                def onehots(b, g):
                    four = bass.ds(g * 4, 4)
                    dve.tensor_tensor(oh_i[:, b, :, :], iota[:, :].unsqueeze(1).broadcast_to([P, 4, P]),
                                      sel_i[:, four].unsqueeze(2).broadcast_to([P, 4, P]), ALU.is_equal)
                    for t in range(4):
                        c = bass.ds(g * 4 + t, 1)
                        last = dve.tensor_scalar(oh_j[:, b, t, :], iota[:, :], sel_j[:, c], sel_g[:, c], ALU.is_equal, ALU.mult)
                    last.then_inc(sem(f"onehot_ready_{l}"), 1)

                def place_gates(b, g):
                    dve.wait_ge(sem(f"gate_ready_{l}"), g + 1)
                    some = acts[:, :, bass.ds(g * 4, 4)]
                    return dve.tensor_tensor(some, ps[:, b, :].rearrange("p (t j) -> p j t", t=4), some, ALU.mult)

                def place_acts(u, i):
                    dve.wait_ge(sem(f"acts_ready_{l}"), i * RAW + (U_GATED + u + 1))
                    some = acts[:, bass.ds(i * RAW + (U_GATED + u), 1), :].rearrange("p o t -> p (o t)")
                    dve.tensor_tensor(some, some, gelu_out[:, u % 2, :], ALU.mult).then_inc(sem(f"gelu_slots_{l}"), 1)
                    dve.wait_ge(sem(f"gelu_slots_{l}"), i * RAW + (u + 3))

                dve.wait_ge(sem(f"ones_in_place_{l}"), RAW)
                dve.wait_ge(sem(f"acts_ready_{l}"), U_GATED)
                dve.wait_ge(sem(f"gelu_slots_{l}"), 2)
                onehots(0, 0)
                with ch.loop(GATE_STEPS - 1, RAW) as i:
                    for u in range(RAW):
                        lo_chunk(dve, n0 + U_GATED + u + 1, i)
                        onehots((u + 1) % 2, i * RAW + (u + 1))
                        place_acts(u, i)
                        link(place_gates(u % 2, i * RAW + u))
                for u in range(RAW):
                    i = GATE_STEPS - 1
                    if u < RAW - 1:
                        lo_chunk(dve, n0 + NK - RAW + 1 + u)
                    onehots((u + 1) % 2, i * RAW + (u + 1))
                    place_acts(u, i)
                    link(place_gates(u % 2, i * RAW + u))
                for g in range(GATE_STEPS * RAW, GROUPS - 1):
                    onehots((g + 1) % 2, g + 1)
                    link(place_gates(g % 2, g))
                place_gates((GROUPS - 1) % 2, GROUPS - 1).then_inc(sem(f"gates_done_{l}"), 1)
                dve.memset(rstd[:, :], 0.0).then_inc(sem(f"zeros_ready_{l}"), 1)
                n0 = FIRST[f"v{l}"]

                def g_low(i, u, step):
                    dve.wait_ge(sem(f"g_hi_ready_{l}"), i * step + (u + 1))
                    dve.tensor_tensor(h_lo[:, u % RAW, :], acts[:, bass.ds(i * step + u, 1), :].rearrange("p o t -> p (o t)"), h_hi[:, u % RAW, :], ALU.subtract)\
                       .then_inc(sem(f"g_lo_ready_{l}"), 1)

                if l == 0:
                    with dve.Fori(0, 8) as i:
                        for u in range(16):
                            s, part = half_of(n0 + u, 0)
                            dve.wait_ge(sem("w_hi_ready"), i * 32 + (2 * (n0 + u) + 1))
                            dve.tensor_tensor(w_lo[:, s, :], raw[:, (n0 + u) % RAW, part], w_hi[:, s, :], ALU.subtract)\
                               .then_inc(sem("w_lo_a_ready"), 1)
                            g_low(i, u, 16)
                            if u in MOD_BESIDE:
                                m = MOD_BESIDE.index(u)
                                dve.wait_ge(sem(f"mod_landed_{m % 2}"), i * 48 + 16 * ((MODS + m) // 2 + 1))
                                dot(m, m % 2, got[:, m:m + 1])
                        dve.wait_ge(sem("mod_used"), i * 6 + (MODS + 6))
                        dve.tensor_copy(mod[:, bass.ds(i * 6 + MODS, 6)], got[:, 0:6]).then_inc(sem("mod_copied"), 1)
                        dve.wait_ge(sem("mod_copied"), i + 1)
                else:
                    with dve.Fori(0, NK // RAW) as i:
                        for u in range(RAW):
                            lo_chunk(dve, n0 + u, i)
                            g_low(i, u, RAW)
                multiplied(dve, n0 + NK - 1)
                for c in range(DC):
                    last = add_residual(c, ps[:, c // 2, (c % 2) * T:(c % 2 + 1) * T], l, 5)
                last.then_inc(sem("x_ready"), 1)
                dve.wait_ge(sem("x_ready"), 2 + 2 * l)

            retrieval(0)
            link(dve.tensor_tensor(mod[:, MODS:2 * MODS], mod[:, MODS:2 * MODS], b_cols("mod_b", MODS, MODS), ALU.add))
            gain_of(3, mod[:, MODS + DC:MODS + 2 * DC], "mix_g", DC)
            gain_of(4, mod[:, MODS + 4 * DC:MODS + 5 * DC], "ffn_g", DC)

            dve.wait_ge(sem("hyena_landed"), 16 * 7)
            dve.memset(pad[:, :, :], 0.0).then_inc(sem("pad_ready"), 1)
            r, t1 = arg[0:FFN, 0, :], arg[0:FFN, 1, :]
            for k in range(3):
                dve.wait_ge(sem("ffn_ready"), k + 1)
                link(dve.tensor_scalar(r, ps[0:FFN, 4 + k, 0:T], fcol[0:FFN, k:k + 1], fcol[0:FFN, 3:4], ALU.add, ALU.mult))
                link(dve.tensor_scalar(t1, r, 1 / (2 * math.pi), MAGIC, ALU.mult, ALU.add))
                link(dve.tensor_scalar(t1, t1, MAGIC, None, ALU.subtract))
                for part in (TWO_PI_1, TWO_PI_2, TWO_PI_3):
                    link(dve.scalar_tensor_tensor(out=r, in0=t1, scalar=-part, in1=r, op0=ALU.mult, op1=ALU.add))
                dve.tensor_scalar(r, r, 3.1415925, -3.1415925, ALU.min, ALU.max).then_inc(sem("arg_ready"), 1)
            for k in range(16):
                mt, blk = k // 8, k % 8
                dve.wait_ge(sem("decay_ready"), mt + 1)
                dve.wait_ge(sem("hf_prod"), k + 1)
                o, fb, half = blk // 4, (blk // 2) % 2, blk % 2
                dve.tensor_tensor(hf[:, mt, o, fb, half * 512:half * 512 + 512], ps[:, 4 + k % 4, :], decay[:, o, half * 512:half * 512 + 512], ALU.mult)\
                   .then_inc(sem("hf_ready"), 1)
            dve.wait_ge(sem("hf_ready"), 16)
            for o in range(ORDER):
                last = dve.memset(hf[0:1, 0, o, 1, :], 0.0)
            last.then_inc(sem("hf_zeroed"), 1)
            dve.wait_ge(sem("hf_zeroed"), 1)
            dve.wait_ge(sem("hf_abs_ready"), 1)
            for mt in range(TT):
                dve.tensor_tensor(hf_diff[:, mt, :, :], hf[:, mt, :, 0, :], hf[:, mt, :, 1, :], ALU.subtract)
            for mt in range(TT):
                last = dve.tensor_tensor(hf_sum[:, mt, :, :], hf[:, mt, :, 0, :], hf[:, mt, :, 1, :], ALU.add)
            last.then_inc(sem("hf_mixed"), 1)
            dve.wait_ge(sem("norm_sum"), 1)
            dve.reciprocal(inv_norm, ps[:, 0, 0:ORDER * DC]).then_inc(sem("inv_norm_ready"), 1)
            modulated(5, 3, x[:, :, :], 3, lambda c: mod_col(1, 0, c), h_hi, h_lo)
            n0 = FIRST["win"]

            def short_conv(m):
                dve.wait_ge(sem("p_copied"), m + 1)
                b = pad[:, m % 2, :]
                link(dve.tensor_scalar(conv[:, m, :], b[:, 0:T], col("conv_w", m), col("conv_b", m), ALU.mult, ALU.add))
                link(dve.scalar_tensor_tensor(out=conv[:, m, :], in0=b[:, 1:T + 1], scalar=col("conv_w", 3 * DC + m), in1=conv[:, m, :], op0=ALU.mult, op1=ALU.add))
                dve.scalar_tensor_tensor(out=conv[:, m, :], in0=b[:, 2:T + 2], scalar=col("conv_w", 6 * DC + m), in1=conv[:, m, :], op0=ALU.mult, op1=ALU.add)\
                   .then_inc(sem("conv_done"), 1)

            for m in range(3 * DC):
                lo_chunk(dve, n0 + m)
                if m >= 2:
                    short_conv(m - 2)
            short_conv(3 * DC - 2)
            short_conv(3 * DC - 1)
            dve.wait_ge(sem("conv_done"), 3 * DC)
            for o in range(ORDER):
                dve.wait_ge(sem("uf_copied"), 8 * (o + 1))
                for sign, ka, kb, dst in ((ALU.subtract, k_re, k_im, y_re), (ALU.add, k_im, k_re, y_im)):
                    link(dve.tensor_tensor(ctmp, u_im, kb[:, :, o, :], ALU.mult))
                    link(dve.tensor_tensor(dst, u_re, ka[:, :, o, :], ALU.mult))
                    last = dve.tensor_tensor(dst, dst, ctmp, sign)
                    if dst is y_re:
                        link(last)
                last.then_inc(sem("yf_ready"), 1)
                z = conv if o == 0 else zz
                for c in range(DC):
                    dve.wait_ge(sem("yt_ready"), DC * o + c + 1)
                    t = hrt[:, c % 2, :]
                    link(dve.tensor_scalar(t, z[:, c, :], col("hy_bias", o * DC + c), None, ALU.mult))
                    link(dve.scalar_tensor_tensor(out=t, in0=ps[:, 4 + c % 4, 0:T], scalar=inv_norm[:, o * DC + c:o * DC + c + 1], in1=t, op0=ALU.mult, op1=ALU.add))
                    dve.tensor_tensor(zz[:, c, :], t, conv[:, DC * (o + 1) + c, :], ALU.mult).then_inc(sem("z_ready"), 1)
                dve.wait_ge(sem("z_ready"), DC * (o + 1))
            dve.tensor_copy(got[:, 0:1], zz[:, 0, 0:1]).then_inc(sem("to_split"), 1)
            low(4, zz, h_hi, h_lo)
            residual("wout", 1)
            dve.wait_ge(sem("x_ready"), 3)
            modulated(6, 5, x[:, :, :], 4, lambda c: mod_col(1, 3, c), h_hi, h_lo)
            retrieval(1)
            normalise(7, x[:, :, :], x[:, :, :], T, DC)
            for c in range(DC):
                last = dve.tensor_scalar(x[:, c, :], x[:, c, :], col("final_g", c), None, ALU.mult)
            last.then_inc(sem("result_ready"), 1)


def tables():
    f = np.float32
    inv = (10000.0 ** (-np.arange(ROPE // 4, dtype=f) / f(ROPE // 4))).astype(f)
    t = np.arange(T)
    row, colu = (t // 64).astype(f), (t % 64).astype(f)
    ang = np.concatenate([row[:, None] * inv, row[:, None] * inv, colu[:, None] * inv, colu[:, None] * inv], 1).T
    sign = np.where(np.arange(ROPE) % 16 < 8, -1.0, 1.0)[:, None]
    rope = np.zeros((P, T), f)
    rope[NOPE:QK] = np.cos(ang)
    rope[QK:] = np.sin(ang) * sign
    k = np.arange(T)
    ang = 2 * np.pi * np.outer(k, k + 0.5) / (2 * T)
    def tiles(m):
        return m.reshape(TT, P, T).transpose(1, 0, 2)
    dft = np.stack([tiles(np.cos(ang)), tiles(np.sin(ang)), tiles(np.cos(ang).T / T), tiles(np.sin(ang).T / T)], 1).astype(f)
    bands = (EMB - 1) // 2
    lin = np.linspace(0.0, 1.0, T, dtype=f)
    w = (f(2.0 * math.pi / T) * np.arange(T, dtype=f))[None, :]
    fr = np.linspace(1e-4, bands - 1, bands, dtype=f)[:, None]
    zfeat = np.concatenate([lin[None, :], np.cos(fr * w), -np.sin(fr * w)], 0).astype(f)
    return dict(rope=rope, dft=dft, zfeat=zfeat, ident=np.eye(P, dtype=f), iota=np.broadcast_to(np.arange(P, dtype=f), (P, P)),
                neg_t=-lin.reshape(TT, P).T)


def kernel(**inputs):
    import concourse.bacc as _bacc
    from concourse.bass_utils import run_bass_kernel_spmd as _run

    g = {k: np.asarray(v) for k, v in inputs.items()}
    tab = tables()

    def by_feature(v):
        return v.reshape(-1, P).T

    def by_chunk(w):
        return w.reshape(DC, P, -1, P).transpose(2, 1, 0, 3).reshape(-1, P, D)

    swap = np.concatenate([np.arange(8, 16), np.arange(0, 8), np.arange(24, 32), np.arange(16, 24)])
    ar = {}
    for name in ("x", "ctx"):
        ar[name] = g[name][0].T.reshape(DC, P, T).transpose(1, 0, 2)
    ar["c"] = np.broadcast_to(g["c"][0], (P, D))
    ar["c_ctx"] = np.broadcast_to(g["c_ctx"], (P, D))
    ar["mod_w"] = g["mod_w"].reshape(2, D, MODS, P).transpose(0, 2, 3, 1).reshape(2 * MODS, P, D)
    parts = {"mix_g": g["norm_mix_g"], "ffn_g": g["norm_ffn_g"], "final_g": g["final_g"], "q_g": g["mla_q_norm_g"][0],
             "kv_g": g["mla_kv_norm_g"][0], "conv_w": g["hy_conv_w"][0], "conv_b": g["hy_conv_b"][0], "hy_bias": g["hy_bias"][0],
             "mod_b": g["mod_b"]}
    ar["cols"] = np.concatenate([by_feature(parts[n]) if n in parts else tab[n] for n in COLS], 1)
    dkv = g["mla_w_dkv"][0]
    key = dkv[:, QL + KVL:]
    dkv = np.concatenate([dkv[:, :QL + KVL], np.zeros((D, NOPE), np.float32), key, key[:, swap]], 1)
    ar["dkv"] = by_chunk(dkv)
    uq = g["mla_w_uq"][0].reshape(QL, HEADS, QK)
    uq = np.concatenate([uq, uq[:, :, NOPE + swap]], 2)
    ar["w_uq"] = uq.reshape(QC, P, HEADS, P).transpose(1, 0, 2, 3)
    ukv = g["mla_w_ukv"][0].reshape(KC, P, HEADS, NOPE + VD).transpose(1, 0, 2, 3)
    ar["w_uk"] = ukv[..., :NOPE].reshape(P, KC, HEADS // 2, P)
    ar["w_uv"] = ukv[..., NOPE:].reshape(P, KC, D)
    ar["wo"], ar["win"], ar["wout"] = by_chunk(g["mla_w_o"][0]), by_chunk(g["hy_w_in"][0]), by_chunk(g["hy_w_out"][0])
    for l in range(2):
        ar[f"wq{l}"] = by_chunk(g["peer_wq"][l])
        ar[f"u{l}"] = g["peer_u"][l].reshape(NK, NK, DC, P).transpose(1, 3, 2, 0).reshape(NK, P, D)
        ar[f"v{l}"] = g["peer_v"][l].reshape(NK, NK, D).transpose(1, 0, 2)
    ar["keys"] = g["peer_keys"].reshape(2, HP, NK, P).transpose(0, 3, 1, 2)
    ar["w4"] = g["hy_w4"][0]
    ar["delta"] = np.broadcast_to(g["hy_deltas"][0], (P, ORDER, D))
    ar["w1"] = g["hy_w1"][0]
    ar["w23"] = np.stack([g["hy_w2"][0], g["hy_w3"][0]], 1)
    ar["fcol"] = np.stack([g["hy_b1"][0], g["hy_b2"][0], g["hy_b3"][0], g["hy_sin_freq"][0]], 1)
    for n in ("rope", "dft", "zfeat", "ident", "iota"):
        ar[n] = tab[n]

    nc = _bacc.Bacc("TRN2", target_bir_lowering=False, num_devices=1)
    arrays, aps = {}, {}
    for name, v in ar.items():
        arrays[f"in_{name}"] = np.ascontiguousarray(v)
        aps[name] = nc.dram_tensor(f"in_{name}", v.shape, F32, kind="ExternalInput").ap()
    out = nc.dram_tensor("out_x", (P, DC, T), F32, kind="ExternalOutput").ap()
    build(nc, aps, out)
    r = _run(nc, [arrays], core_ids=[0])
    y = r.results[0]["out_x"]
    return np.ascontiguousarray(np.asarray(y).transpose(2, 1, 0).reshape(1, T, D))
```

```python
from contextlib import ExitStack, contextmanager
import math

import numpy as np
import concourse.bass as bass
from concourse import mybir
from concourse.alu_op_type import AluOpType as ALU

ACT = mybir.ActivationFunctionType
F32 = mybir.dt.float32
F32R = mybir.dt.float32r
U32 = mybir.dt.uint32
AX = mybir.AxisListType

P = 128
D = 1024
DC = D // P
T = 256
TT = T // P
EPS = 1e-6
HEADS, NOPE, ROPE, VD = 16, 64, 32, 64
QK = NOPE + ROPE
QL, KVL = 384, 256
QC, KC = QL // P, KVL // P
DKV = QC + KC + 1
PH, NK, TOPK = 8, 128, 16
HP = 2 * PH
STEPS = HEADS * TT
ORDER, FFN, EMB = 2, 64, 33
RAW, SPLIT = 4, 4
MODS = 6 * DC
SCALE = QK ** -0.5
LOWEST = -3.4028234663852886e38
MAGIC = 12582912.0
TWO_PI_1, TWO_PI_2 = 6.28125, 0.0019340515136718750
TWO_PI_3 = 2 * math.pi - TWO_PI_1 - TWO_PI_2

COLS = {}
_at = 0
for _n, _w in (("mix_g", 2 * DC), ("ffn_g", 2 * DC), ("final_g", DC), ("q_g", QC), ("kv_g", KC), ("conv_w", 9 * DC),
               ("conv_b", 3 * DC), ("hy_bias", ORDER * DC), ("mod_b", 2 * MODS), ("neg_t", TT)):
    COLS[_n] = (_at, _at + _w)
    _at += _w
NCOLS = _at

STREAM = [("dkv", DKV), ("wo", DC), ("wq0", HP), ("u0", NK), ("v0", NK), ("win", 3 * DC), ("wout", DC),
          ("wq1", HP), ("u1", NK), ("v1", NK)]
FIRST = {}
_at = 0
for _n, _w in STREAM:
    FIRST[_n] = _at
    _at += _w

MODS_FIRST, MODS_PE = 2 * DC, 7
PE_GROUPS = ((0, 3), (3, 6), (6, 7))
DVE_GROUPS = ((7, 11), (11, 13), (13, 16))
FILTER_GROUPS = 2 * ORDER
MOD_BESIDE = (1, 4, 6, 9, 12, 14)
U_TOPK = TT * PH * RAW
U_GATED = U_TOPK + RAW
VECTOR_BLOCKS, VECTOR_BLOCKS_TOPK, VECTOR_BLOCKS_GATES = 4, 1, 1
ONES_BESIDE, SCORES_AT = 3, 112
ONES_FIRST = SCORES_AT - ONES_BESIDE * (TT * PH - 1)
GROUPS = T // 4
GATE_STEPS = (NK - U_GATED) // RAW


SPECTRUM = [("turn", h, None, tt) if kind == "turn" else ("transform", h, part, tt)
            for h in range(2) for kind, part in (("turn", None), ("transform", 0), ("transform", 1)) for tt in range(TT)]
SP_HALF = len(SPECTRUM) // 2
WIN_SPECTRUM, WIN_PRODUCTS = 10, 17
RENEWED_BY = {"wo": 0, "v0": 1, "wout": 2, "v1": 3}
EPS_COLUMN = {D: slice(1, 2), QL: slice(2, 3), KVL: slice(3, 4)}
SQUARES_BEFORE = [0, 1, 2, 3, 4, 4 + DC, 4 + 2 * DC, 4 + 3 * DC]


class Chain:

    def __init__(self, eng, sem):
        self.eng, self.sem, self.n, self.i, self.per, self.k = eng, sem, 0, None, 0, 0

    def link(self, ins):
        ins.then_inc(self.sem, 1)
        if self.i is None:
            self.n += 1
            self.eng.wait_ge(self.sem, self.n)
        else:
            self.k += 1
            self.eng.wait_ge(self.sem, self.i * self.per + (self.n + self.k))

    @contextmanager
    def loop(self, count, per):
        with self.eng.Fori(0, count) as i:
            self.i, self.per, self.k = i, per, 0
            yield i
            assert self.k == per, (self.k, per)
        self.i = None
        self.n += count * per


def build(nc, a, spectra, out):
    with ExitStack() as ctx:
        def sb(name, shape, dt=F32):
            return ctx.enter_context(nc.sbuf_tensor(name, shape, dt))

        sems = {}

        def sem(name):
            if name not in sems:
                sems[name] = ctx.enter_context(nc.semaphore(name))
            return sems[name]

        x = sb("x", [P, DC, T])
        h_hi = sb("h_hi", [P, DC, T], F32R)
        h_lo = sb("h_lo", [P, DC, T], F32R)
        raw = sb("raw", [P, RAW, D])
        w_hi = sb("w_hi", [P, SPLIT, D // 2], F32R)
        w_lo = sb("w_lo", [P, SPLIT, D // 2], F32R)
        w_hi_flat = w_hi[:, :, :].rearrange("p a b -> p (a b)")
        w_lo_flat = w_lo[:, :, :].rearrange("p a b -> p (a b)")
        small = sb("small", [P, 2048])
        silu = sb("silu", [P, D])
        cols = sb("cols", [P, NCOLS])
        mod = sb("mod", [P, 2 * MODS])
        modc = sb("modc", [P, 2 * DC])
        c_pair = sb("c_pair", [P, DC, 2])
        c_pair_exp = sb("c_pair_exp", [P, DC, 2])
        inv_norm = sb("inv_norm", [P, ORDER * DC])
        gain = sb("gain", [P, 5 * DC])
        sel_i = sb("sel_i", [P, T])
        sel_j = sb("sel_j", [P, T])
        sel_g = sb("sel_g", [P, T])
        ident = sb("ident", [P, P])
        iota = sb("iota", [P, P])
        ones = sb("ones", [P, P])
        zero = sb("zero", [P, 8])
        zeros = sb("zeros", [P, 512])
        root_tok = sb("root_tok", [P, 8, 4])
        root_tmp = sb("root_tmp", [P, 4])
        arena_off = (nc.sbuf_base + 31) // 32 * 32
        arena = sb("arena", [P, NK * T])
        ps = ctx.enter_context(nc.psum_tensor("ps", [P, 8, 512], F32))

        def shaped(buffer, at, shape):
            v = buffer[:, at:at + int(np.prod(shape))]
            if len(shape) == 1:
                return v
            names = "abcde"[:len(shape)]
            return v.rearrange(f"p ({' '.join(names)}) -> p {' '.join(names)}", **dict(zip(names[1:], shape[1:])))

        def cut(at, *shape):
            return shaped(arena, at, shape)

        def scut(at, *shape):
            return shaped(small, at, shape)

        def col(name, k, rows=P):
            return cols[0:rows, COLS[name][0] + k:COLS[name][0] + k + 1]

        at = 0
        def take(*shape):
            nonlocal at
            v = cut(at, *shape)
            at += int(np.prod(shape))
            return v
        cx = take(DC, T)
        tmp = take(DC, T)
        f_hf = take(TT, 2, 512)
        f_hf_flat = f_hf.rearrange("p a b c -> p (a b c)")
        silu_c, products = f_hf_flat[:, 0:D], f_hf_flat[:, D:2 * D]
        q_heads = cut(0, HEADS, T)
        lat_flat = take(DKV * 512)
        lat = lat_flat.rearrange("p (a b) -> p a b", a=DKV)
        f_abs = lat_flat[:, 0:4 * 512].rearrange("p (a b c) -> p a b c", a=TT, b=2)
        f_diff = lat_flat[:, 4 * 512:6 * 512].rearrange("p (a b) -> p a b", a=TT)
        w_uq = take(QC, HEADS, P)
        w_uq_flat = w_uq.rearrange("p a b c -> p (a b c)")
        v_keys = w_uq_flat[:, 0:4 * D].rearrange("p (a b) -> p a b", a=4)
        f_out = w_uq_flat[:, 4 * D:6 * D].rearrange("p (a b) -> p a b", a=4)
        w_uk = take(KC, HEADS // 2, P)
        w_uv = take(KC, D)
        f_w4 = w_uv.rearrange("p a (b c) -> p a b c", b=2)
        cq = take(QC, T)
        zfeat, w1 = (cq.rearrange("p a b -> p (a b)")[:, o:o + n] for o, n in ((0, T), (T, FFN)))
        ckv = take(KC, 512)
        rope = take(T)
        rope_s = take(2, T)
        rope_c = take(2, T)
        k_heads = take(4, 512)
        c_at = at
        probs = take(2, 512)
        probs_t = take(2, 4, T)
        decay = take(TT, 512)
        smax = take(64)
        delta = take(ORDER, D)
        f_dft = take(2, TT, T)
        w23 = take(2 * FFN)
        fcol = take(4)
        arg = take(3, T)
        assert at <= NK * T, at
        c_hi = nc.alloc_sbuf_tensor_at("c_hi", [P, DC, T], F32R, offset=arena_off + 4 * c_at)
        c_lo = nc.alloc_sbuf_tensor_at("c_lo", [P, DC, T], F32R, offset=arena_off + 4 * (c_at + DC * T))

        tmp_flat = tmp.rearrange("p a b -> p (a b)")
        tmp_c = k_heads.rearrange("p a b -> p (a b)").rearrange("p (a b) -> p a b", a=DC)
        w_uq_chunks = w_uq_flat.rearrange("p (a b) -> p a b", a=6)
        c_chunks = cut(c_at, 4, D)
        pe_places = (w_uq_chunks[:, 0:3, :], w_uq_chunks[:, 3:6, :], c_chunks[:, 0:1, :])
        dve_places = (raw[:, :, :], scut(0, 2, D), c_chunks[:, 1:4, :])
        sq_q = tmp[:, 0:QC, :]
        sq_k = tmp_flat[:, QC * T:QC * T + KC * 512].rearrange("p (a b) -> p a b", a=KC)

        at = 0
        conv = take(3 * DC, T)
        hrt = take(2, T)
        k_both = take(2, TT * ORDER * D)
        k_re, k_im = (k_both[:, part, :].rearrange("p (a b c) -> p a b c", a=TT, b=ORDER) for part in range(2))
        u_re, u_im = take(TT, D), take(TT, D)
        y_re, y_im = take(TT, D), take(TT, D)
        tr_z = take(TT, D)
        zz = take(DC, T)
        dft = take(4, TT, T)
        ctmp = take(TT, 512)
        pad = take(2, 258)
        assert at <= NK * T, at

        acts = cut(0, NK, T)
        q_all = cut(86 * T, HP, T)
        keys = cut(102 * T, HP, P)
        scores = cut(SCORES_AT * T, TT, HP, P)
        pair_work = sb("pair_work", [P, 2 * T])
        eq = pair_work[:, :].rearrange("p (a b c) -> p a b c", a=2, b=TOPK)
        gelu_out = pair_work[:, :].rearrange("p (a b) -> p a b", a=2)
        fs = scut(0, TT, PH * TOPK)
        fi_i = scut(256, TT, PH * TOPK)
        fi_j = scut(512, TT, PH * TOPK)
        sv = scut(768, 2, TOPK)
        si_u = scut(800, 2, TOPK).bitcast(U32)
        si_f = scut(832, 2, TOPK)
        cand = scut(864, TOPK, TOPK)
        cand_flat = scut(864, TOPK * TOPK)
        rest = scut(1120, 2, P)
        rest_flat = scut(1120, TOPK * TOPK)
        keys_of = scut(1376, 2, TOPK)
        fi_u = scut(1632, TOPK).bitcast(U32)
        fa_u = scut(1648, 2, TOPK).bitcast(U32)
        fa_f = scut(1680, 2, TOPK)
        fsum = scut(1712, TT * PH)
        fs_one = scut(1984, TOPK)
        pair = scut(1728, 2, P)
        oh_i = scut(0, 2, 4, P)
        oh_j = scut(1024, 2, 4, P)
        mod_raw = scut(0, 2, D)
        scores_v = cut(SCORES_AT * T, TT * PH, 2 * P)
        fs_v = scut(0, TT * PH, TOPK)
        fi_both = scut(256, 2, TT * PH, TOPK)
        got = sb("got", [P, 8])

        block = ctx.enter_context(nc.Block())

        def raw_sem(n):
            return sem(f"raw_landed_{n % RAW}")

        def load_chunk(sp, name, index, n, i=0):
            if n >= RAW:
                sp.wait_ge(sem("w_lo_a_ready"), i * RAW + (n - RAW + 1))
                sp.wait_ge(sem("w_lo_b_ready"), i * RAW + (n - RAW + 1))
            sp.dma_start(raw[:, n % RAW, :], a[name][bass.ds(index, 1), :, :].rearrange("o p n -> p (o n)")).then_inc(raw_sem(n), 16)

        def half_of(n, k):
            return (2 * n + k) % SPLIT, slice(k * D // 2, (k + 1) * D // 2)

        def hi_chunk(act, n, i=0):
            act.wait_ge(raw_sem(n), i * 16 + 16 * (n // RAW + 1))
            for k in range(2):
                s, part = half_of(n, k)
                if 2 * n + k >= SPLIT:
                    act.wait_ge(sem("w_used"), i * 2 * RAW + (2 * n + k - SPLIT + 1))
                act.activation(w_hi[:, s, :], raw[:, n % RAW, part], ACT.Copy).then_inc(sem("w_hi_ready"), 1)

        def vector_blocks(n):
            for l in range(2):
                first = FIRST[f"u{l}"]
                if first <= n < first + U_GATED:
                    return VECTOR_BLOCKS_TOPK
                if first + U_GATED <= n < first + NK:
                    return VECTOR_BLOCKS_GATES
            return VECTOR_BLOCKS

        def lower(eng, n, first, end):
            at = n % 2 * D
            cols_of = slice(at + first * P, at + end * P)
            return eng.tensor_tensor(w_lo_flat[:, cols_of], raw[:, n % RAW, first * P:end * P], w_hi_flat[:, cols_of], ALU.subtract)

        def lo_chunk(dve, n, i=0, step=RAW):
            dve.wait_ge(sem("w_hi_ready"), i * 2 * step + (2 * n + 1))
            lower(dve, n, 0, vector_blocks(n)).then_inc(sem("w_lo_a_ready"), 1)

        def mid_count(n, i=0):
            l = 0 if n < FIRST["v0"] else 1
            return i * RAW + (n - FIRST[f"u{l}"] + NK * l + 1)

        def lo_chunk_b(pool, n, i=0):
            if vector_blocks(n) < DC // 2:
                pool.wait_ge(sem("w_hi_ready"), i * 2 * RAW + (2 * n + 1))
                lower(pool, n, vector_blocks(n), DC // 2).then_inc(sem("w_lo_mid_ready"), 1)
            pool.wait_ge(sem("w_hi_ready"), i * 2 * RAW + (2 * n + 2))
            lower(pool, n, DC // 2, DC).then_inc(sem("w_lo_b_ready"), 1)

        def block_of(n, c):
            s = (2 * n + c // 4) % SPLIT
            return w_hi[:, s, (c % 4) * P:(c % 4 + 1) * P], w_lo[:, s, (c % 4) * P:(c % 4 + 1) * P]

        def spans(cut_at):
            ends = sorted({0, cut_at, DC // 2, DC})
            return list(zip(ends, ends[1:]))

        def product(pe, n, outs, i=0, fresh=None):
            cut_at = vector_blocks(n)
            for first, end in spans(cut_at):
                if first == 0:
                    pe.wait_ge(sem("w_lo_a_ready"), i * RAW + (n + 1))
                if first == cut_at < DC // 2:
                    pe.wait_ge(sem("w_lo_mid_ready"), mid_count(n, i))
                if first == DC // 2:
                    pe.wait_ge(sem("w_lo_b_ready"), i * RAW + (n + 1))
                for o, rh, rl in outs:
                    for c in range(first, end):
                        if fresh is not None:
                            pe.wait_ge(sem("h_lo_ready"), DC * fresh + c + 1)
                        wh, wl = block_of(n, c)
                        pe.matmul(o, wh, rh[:, c, :], start=(c == 0), stop=False)
                        pe.matmul(o, wh, rl[:, c, :], start=False, stop=False)
                        last = pe.matmul(o, wl, rh[:, c, :], start=False, stop=(c == DC - 1))
                if end % (DC // 2) == 0:
                    last.then_inc(sem("w_used"), 1)

        def multiplied(eng, n, i=0):
            eng.wait_ge(sem("w_used"), i * 2 * RAW + (2 * n + 2))

        def sum_view(k, width):
            if k in (4, 6):
                return ps[:, 0:4:3, 0]
            if k in (5, 7):
                return ps[:, 4:6, 0]
            return ps[:, spread_bank(k), 0:width // P]

        def spread_bank(k):
            return 5 if k in (1, 3) else 0

        def roots(k, width=T):
            return ps[:, spread_bank(k), 0:width]

        def renewed(eng, name, chunks):
            eng.wait_ge(sem("x_renewed"), RENEWED_BY[name] * DC + chunks)

        def mod_col(l, part, c):
            k = l * MODS + part * DC + c
            return mod[:, k:k + 1]

        @block.sync
        def _(sp):
            def load_mod(k, i=None):
                k -= MODS_FIRST
                if i is None:
                    if k >= 2:
                        sp.wait_ge(sem("mod_used"), k - 1)
                    src = a["mod_w"][k]
                else:
                    sp.wait_ge(sem("mod_used"), i * 6 + (k - 1))
                    src = a["mod_w"][bass.ds(i * 6 + k, 1), :, :].rearrange("o p n -> p (o n)")
                sp.dma_start(mod_raw[:, k % 2, :], src).then_inc(sem(f"mod_landed_{k % 2}"), 16)

            def load_all(name, first=0):
                count, n0 = dict(STREAM)[name], FIRST[name]
                with sp.Fori(0, (count - first) // RAW) as i:
                    for u in range(RAW):
                        load_chunk(sp, name, i * RAW + (first + u), n0 + first + u, i)

            sp.dma_start(c_pair[:, :, :], a["c_pair"]).then_inc(sem("c_pair_landed"), 16)
            for j in range(3):
                first, end = PE_GROUPS[j]
                sp.dma_start(pe_places[j], a["mod_first_pe"][:, first:end, :]).then_inc(sem(f"mod_pe_landed_{j}"), 16)
                first, end = DVE_GROUPS[j]
                sp.dma_start(dve_places[j], a["mod_first_dve"][:, first - MODS_PE:end - MODS_PE, :]).then_inc(sem(f"mod_dve_landed_{j}"), 16)
            sp.wait_ge(sem("mod_dve_used"), 1)
            for k in range(DKV):
                load_chunk(sp, "dkv", k, k)
            sp.wait_ge(sem("mod_dve_used"), 2)
            load_mod(2 * DC)
            load_mod(2 * DC + 1)
            for k in range(RAW):
                load_chunk(sp, "wo", k, FIRST["wo"] + k)
            for k in range(2 * DC + 2, MODS):
                load_mod(k)
            load_all("wo", RAW)
            for l in range(2):
                load_all(f"wq{l}", 0)
                load_all(f"u{l}")
                if l == 1:
                    load_all("v1")
                    break
                n0 = FIRST["v0"]

                def load_v0(i, u):
                    n = n0 + u
                    sp.wait_ge(sem("w_lo_a_ready"), i * 16 + (n - RAW + 1))
                    sp.wait_ge(sem("w_lo_b_ready"), i * 16 + (n - RAW + 1))
                    sp.dma_start(raw[:, n % RAW, :], a["v0"][bass.ds(i * 16 + u, 1), :, :].rearrange("o p n -> p (o n)"))\
                      .then_inc(raw_sem(n), 16)

                def load_beside(i, u):
                    if u in MOD_BESIDE:
                        load_mod(MODS + MOD_BESIDE.index(u), i=i)

                for u in range(RAW):
                    load_v0(0, u)
                sp.wait_ge(sem("gates_done_0"), 1)
                for u in range(RAW):
                    load_beside(0, u)
                for u in range(RAW, 16):
                    load_v0(0, u)
                    load_beside(0, u)
                with sp.Fori(1, NK // 16) as i:
                    for u in range(16):
                        load_v0(i, u)
                        load_beside(i, u)
                for k in range(RAW):
                    load_chunk(sp, "win", k, FIRST["win"] + k)
                renewed(sp, "v0", 1)
                sp.dma_start(dft, a["dft"]).then_inc(sem("dft_landed"), 16)
                sp.wait_ge(sem("spectra_stored"), 16 * FILTER_GROUPS)
                sp.dma_start(k_both, spectra.rearrange("p a b c d -> p a (b c d)")).then_inc(sem("spectra_landed"), 16)
                load_all("win", RAW)
                load_all("wout")
            for half in range(2):
                part = slice(half * DC // 2, (half + 1) * DC // 2)
                sp.wait_ge(sem("result_ready"), half + 1)
                sp.dma_start(out[:, part, :], x[:, part, :]).then_inc(sem("stored"), 16)
            sp.wait_ge(sem("stored"), 32)

        @block.gpsimd
        def _(pool):
            pool.dma_start(ident[:, :], a["ident"]).then_inc(sem("ident_landed"), 16)
            pool.memset(ones[:, :], 1.0).then_inc(sem("ones_ready"), 1)
            pool.dma_start(cols[:, :], a["cols"]).then_inc(sem("cols_landed"), 16)
            for dst, src in ((zfeat[0:EMB, :], "zfeat"), (w1[0:EMB, :], "w1"), (w23[0:FFN, :], "w23"), (fcol[0:FFN, :], "fcol")):
                pool.dma_start(dst, a[src]).then_inc(sem("mlp_landed"), 16)
            pool.dma_start(iota[:, :], a["iota"]).then_inc(sem("iota_landed"), 16)
            pool.wait_ge(sem("mod_dve_used"), 1)
            pool.dma_start(rope, a["rope"]).then_inc(sem("attn_landed"), 16)
            pool.dma_start(w_uk, a["w_uk"]).then_inc(sem("attn_landed"), 16)
            pool.dma_start(w_uv, a["w_uv"]).then_inc(sem("attn_landed"), 16)
            pool.dma_start(delta, a["delta"]).then_inc(sem("filter_landed"), 16)
            pool.dma_start(f_dft, a["dft"][:, 0:2, :, :]).then_inc(sem("filter_landed"), 16)
            pool.wait_ge(sem("mod_pe_used"), 2)
            pool.dma_start(w_uq, a["w_uq"]).then_inc(sem("attn_landed"), 16)
            for k in range(DKV):
                lo_chunk_b(pool, k)

            def load_w4(g):
                pool.dma_start(f_w4[0:FFN, g % 2, :, :], a["w4"][:, g // 2, :, g % 2, :]).then_inc(sem(f"w4_landed_{g % 2}"), 16)

            pool.wait_ge(sem("v_ready"), 8)
            load_w4(0)
            load_w4(1)
            for g in range(FILTER_GROUPS):
                if g + 2 < FILTER_GROUPS:
                    pool.wait_ge(sem("hf_prod"), 4 * (g + 1))
                    load_w4(g + 2)
                pool.wait_ge(sem("kf_copied"), 4 * (g + 1))
                pool.dma_start(spectra[:, :, :, g // 2, (g % 2) * 512:(g % 2 + 1) * 512], f_out.rearrange("p (a b) n -> p a b n", a=2))\
                    .then_inc(sem("spectra_stored"), 16)
            for name, count in STREAM[1:]:
                n0 = FIRST[name]
                if name[0] == "u":
                    l = name[1]
                    with pool.Fori(0, U_TOPK // RAW) as i:
                        for u in range(RAW):
                            lo_chunk_b(pool, n0 + u, i)
                    for u in range(RAW):
                        lo_chunk_b(pool, n0 + U_TOPK + u)
                        if u == 0:
                            pool.wait_ge(sem(f"topk_done_{l}"), 1)
                        step = (NK - SCORES_AT) // RAW
                        j = SCORES_AT + u * step
                        pool.memset(acts[:, j:j + step, :], 1.0).then_inc(sem(f"ones_in_place_{l}"), 1)
                    with pool.Fori(0, GATE_STEPS) as i:
                        for u in range(RAW):
                            lo_chunk_b(pool, n0 + U_GATED + u, i)
                elif count % RAW:
                    for k in range(count):
                        lo_chunk_b(pool, n0 + k)
                else:
                    with pool.Fori(0, count // RAW) as i:
                        for u in range(RAW):
                            lo_chunk_b(pool, n0 + u, i)

        @block.scalar
        def _(act):
            def square(k, src, dst):
                act.activation(dst, src, ACT.Square).then_inc(sem("square_ready"), 1)

            def root(k, width, features=D):
                act.wait_ge(sem("sum_ready"), k + 1)
                act.activation(root_tok[:, k, 0:width // P], sum_view(k, width), ACT.Sqrt, bias=zero[:, EPS_COLUMN[features]], scale=1.0).then_inc(sem("root_ready"), 1)

            def square_chunk(name, c):
                renewed(act, name, c + 1)
                act.activation(tmp[:, c, :], x[:, c, :], ACT.Square).then_inc(sem("square_ready"), 1)

            def split(s, t, shift, hi, beside=None):
                for c in range(DC):
                    if c == DC // 2 and beside is not None:
                        hi_chunk(act, beside)
                    act.wait_ge(sem("to_split"), DC * (s - (s > 4)) + c + 1)
                    act.activation(hi[:, c, :], t[:, c, :], ACT.Identity, bias=shift(c)).then_inc(sem("h_hi_ready"), 1)

            act.dma_start(x[:, :, :], a["x"]).then_inc(sem("x_landed"), 16)
            act.dma_start(cx, a["ctx"]).then_inc(sem("cx_landed"), 16)
            act.wait_ge(sem("c_pair_landed"), 16)
            act.activation(c_pair_exp[:, :, :], c_pair[:, :, :], ACT.Exp, scale=-1.0).then_inc(sem("c_pair_exp_ready"), 1)
            for k, dst in enumerate((silu, silu_c)):
                act.wait_ge(sem("silu_spread"), k + 1)
                act.activation(dst[:, 0:D], ps[:, 1 + 2 * k:3 + 2 * k, :].rearrange("p a b -> p (a b)"), ACT.Copy).then_inc(sem("silu_ready"), 1)

            act.wait_ge(sem("x_landed"), 16)
            square(0, x[:, :, :], tmp)
            act.wait_ge(sem("cx_landed"), 16)
            square(1, cx, tmp_c)
            root(0, T)
            root(1, T)
            hi_chunk(act, 0)
            hi_chunk(act, 1)
            split(0, tmp, lambda c: mod[:, c:c + 1], h_hi)
            def lat_copy(m):
                multiplied(act, m)
                last = act.activation(lat[:, m, 0:T], ps[:, 1 + m % 2, 0:T], ACT.Copy)
                if m >= QC:
                    last = act.activation(lat[:, m, T:2 * T], ps[:, 3 + m % 2, 0:T], ACT.Copy)
                last.then_inc(sem("lat_ready"), 1)

            def sine(k):
                act.wait_ge(sem("arg_ready"), k + 1)
                act.activation(arg[0:FFN, 2, :], arg[0:FFN, 0, :], ACT.Sin).then_inc(sem("sin_ready"), 1)

            for m in range(DKV):
                if m >= 3:
                    hi_chunk(act, m)
                if m:
                    lat_copy(m - 1)
                if m == 1:
                    split(1, tmp_c, lambda c: modc[:, c:c + 1], c_hi, beside=2)
                if m == QC:
                    act.wait_ge(sem("lat_ready"), QC)
                    square(2, lat[:, 0:QC, 0:T], sq_q)
                if m == QC + KC:
                    act.wait_ge(sem("lat_ready"), QC + KC)
                    square(3, lat[:, QC:QC + KC, :], sq_k)
                if m in (1, 3):
                    sine(m // 2)
            lat_copy(DKV - 1)
            root(2, T, QL)
            root(3, 512, KVL)
            sine(2)
            for p in range(HEADS // 2):
                act.wait_ge(sem("q_ready"), p + 1)
                act.activation(q_heads[0:NOPE, 2 * p:2 * p + 2, :], ps[0:NOPE, 1 + p % 2, :].rearrange("p (a b) -> p a b", a=2),
                               ACT.Copy).then_inc(sem("q_nope_ready"), 1)
            for k in range(8):
                act.wait_ge(sem("v_ready"), k + 1)
                act.activation(v_keys[:, k // 2, (k % 2) * 512:(k % 2 + 1) * 512], ps[:, 3 + k % 2, :], ACT.Copy)\
                   .then_inc(sem("v_keys_ready"), 1)

            act.wait_ge(sem("filter_landed"), 32)
            act.activation(delta, delta, ACT.Abs).then_inc(sem("delta_abs"), 1)
            def decays(g):
                if g:
                    act.wait_ge(sem("hf_ready"), 4 * g)
                for mt in range(TT):
                    last = act.activation(decay[:, mt, :], delta[:, g // 2, (g % 2) * 512:(g % 2 + 1) * 512], ACT.Exp, scale=col("neg_t", mt))
                last.then_inc(sem("decay_ready"), 1)

            def magnitudes(g, mt):
                act.wait_ge(sem("hf_zeroed"), g + 1)
                act.wait_ge(sem("hf_ready"), 4 * g + 2 * (mt + 1))
                if g:
                    act.wait_ge(sem("norm_sum"), g)
                act.activation(f_abs[:, mt, :, :], f_hf[:, mt, :, :], ACT.Abs).then_inc(sem("hf_abs_ready"), 1)

            def spectrum_copy(g, j):
                act.wait_ge(sem("kf_ready"), 4 * g + j + 1)
                if g:
                    act.wait_ge(sem("spectra_stored"), 16 * g)
                act.activation(f_out[:, j, :], ps[:, 0, :], ACT.Copy).then_inc(sem("kf_copied"), 1)

            def keys_copy(p):
                act.wait_ge(sem("k_ready"), p + 1)
                if p >= 2:
                    act.wait_ge(sem("scores_ready"), 4 * (p - 1))
                for j in range(2):
                    act.activation(k_heads[0:NOPE, (2 * p + j) % 4, :], ps[j * NOPE:(j + 1) * NOPE, 1, :], ACT.Copy)\
                       .then_inc(sem("k_heads_ready"), 1)

            def exponentials(u):
                act.wait_ge(sem("max_ready"), u + 1)
                if u >= 2:
                    act.wait_ge(sem("turned"), u - 1)
                act.activation(probs[:, u % 2, :], ps[:, 2 + u % 2, :], ACT.Exp, bias=smax[:, u % 8:u % 8 + 1],
                               scale=SCALE, accum_out=smax[:, 8 + u % 8:9 + u % 8]).then_inc(sem("exp_ready"), 1)

            def copy_turned(u):
                act.wait_ge(sem("turned"), u + 1)
                hh = u // 2
                if hh >= 2:
                    act.wait_ge(sem("o_ready"), hh - 1)
                act.activation(probs_t[:, hh % 2, :, (u % 2) * P:(u % 2 + 1) * P], ps[:, 4 + u % 2, :].rearrange("p (a b) -> p a b", a=4), ACT.Copy)\
                   .then_inc(sem("probs_t_ready"), 1)

            def output_copy(hh):
                o = (hh % 2) * VD
                act.wait_ge(sem("o_ready"), hh + 1)
                act.activation(h_hi[o:o + VD, hh // 2, :], ps[0:VD, 6 + hh % 2, 0:T], ACT.Copy).then_inc(sem("o_hi_ready"), 1)

            act.wait_ge(sem("delta_abs"), 1)
            keys_copy(0)
            decays(0)
            exponentials(0)
            for u in range(STEPS):
                p, j = u // 4, u % 4
                if u + 1 < STEPS:
                    exponentials(u + 1)
                if p % 2 and j:
                    spectrum_copy(p // 2, j - 1)
                copy_turned(u)
                if j == 1 and p + 1 < HEADS // 2:
                    keys_copy(p + 1)
                if u % 2 == 0 and u:
                    output_copy(u // 2 - 1)
                if p % 2 == 0 and j >= 2:
                    magnitudes(p // 2, j - 2)
                if j == 3:
                    if p % 2:
                        spectrum_copy(p // 2, 3)
                        if p + 1 < HEADS // 2:
                            decays((p + 1) // 2)
            output_copy(HEADS - 1)
            def residual(name, after):
                for m in range(DC):
                    if m or name == "wo":
                        hi_chunk(act, FIRST[name] + m)
                    if m >= 2:
                        square_chunk(name, m - 2)
                for m in range(DC - 2, DC):
                    square_chunk(name, m)
                root({"wo": 4, "wout": 6}[name], T)
                hi_chunk(act, FIRST[after])

            residual("wo", "wq0")

            def retrieval(l):
                n0 = FIRST[f"wq{l}"]

                def q_copy(i, u):
                    multiplied(act, n0 + u, i)
                    act.activation(q_all[:, bass.ds(i * RAW + u, 1), :], ps[:, 4 + u, 0:T].unsqueeze(1), ACT.Copy)\
                       .then_inc(sem(f"q_all_ready_{l}"), 1)

                with act.Fori(0, HP // RAW - 1) as i:
                    for u in range(RAW):
                        hi_chunk(act, n0 + u + 1, i)
                        q_copy(i, u)
                for u in range(RAW):
                    if u < RAW - 1:
                        hi_chunk(act, n0 + HP - RAW + u + 1)
                    q_copy(HP // RAW - 1, u)
                for m in range(HP):
                    act.wait_ge(sem(f"key_scores_{l}"), m + 1)
                    act.activation(scores[:, :, m, :], ps[:, 4 + m % 4, 0:T].rearrange("p (a b) -> p a b", a=TT), ACT.Copy)\
                       .then_inc(sem(f"scores_copied_{l}"), 1)
                n0 = FIRST[f"u{l}"]

                def gelu(i, u):
                    multiplied(act, n0 + u, i)
                    act.activation(acts[:, bass.ds(i * RAW + u, 1), :], ps[:, 4 + u, 0:T].unsqueeze(1), ACT.Gelu)\
                       .then_inc(sem(f"acts_ready_{l}"), 1)

                def gelu_beside(i, u):
                    act.wait_ge(sem(f"gelu_slots_{l}"), i * RAW + (u + 1))
                    multiplied(act, n0 + U_GATED + u, i)
                    act.activation(gelu_out[:, u % 2, :], ps[:, 4 + u, 0:T], ACT.Gelu).then_inc(sem(f"acts_ready_{l}"), 1)

                def pair_copy(i):
                    act.activation(pair, scores_v[:, bass.ds(i, 1), :].rearrange("p o (a b) -> p (o a) b", a=2), ACT.Copy)\
                       .then_inc(sem(f"pair_ready_{l}"), 1)

                hi_chunk(act, n0)
                act.activation(got[:, 7:8], zero[:, 0:1], ACT.Gelu)
                act.wait_ge(sem(f"scores_copied_{l}"), HP)
                pair_copy(0)
                with act.Fori(0, U_TOPK // RAW - 1) as i:
                    for u in range(RAW):
                        hi_chunk(act, n0 + u + 1, i)
                        gelu(i, u)
                        if u < ONES_BESIDE:
                            act.activation(acts[:, bass.ds(i * ONES_BESIDE + (ONES_FIRST + u), 1), :], ones[:, :].unsqueeze(1).broadcast_to([P, 2, P]),
                                           ACT.Copy).then_inc(sem(f"ones_behind_{l}"), 1)
                        if u == 2:
                            act.wait_ge(sem(f"pair_used_{l}"), i + 1)
                            pair_copy(i + 1)
                for u in range(RAW):
                    hi_chunk(act, n0 + U_TOPK - RAW + u + 1)
                    gelu(U_TOPK // RAW - 1, u)
                for u in range(RAW):
                    hi_chunk(act, n0 + U_TOPK + u + 1)
                    gelu(U_TOPK // RAW, u)
                    if u == 0:
                        act.wait_ge(sem(f"topk_done_{l}"), 1)
                        act.activation(fs_v, fs_v, ACT.Exp).then_inc(sem(f"fs_exp_{l}"), 1)
                with act.Fori(0, GATE_STEPS - 1) as i:
                    for u in range(RAW):
                        hi_chunk(act, n0 + U_GATED + u + 1, i)
                        gelu_beside(i, u)
                for u in range(RAW):
                    if u < RAW - 1:
                        hi_chunk(act, n0 + NK - RAW + u + 1)
                    gelu_beside(GATE_STEPS - 1, u)
                n0 = FIRST[f"v{l}"]

                def gated_high(i, u):
                    act.activation(h_hi[:, u, :], acts[:, bass.ds(i * RAW + u, 1), :].rearrange("p o t -> p (o t)"), ACT.Copy)\
                       .then_inc(sem(f"g_hi_ready_{l}"), 1)

                hi_chunk(act, n0)
                act.wait_ge(sem(f"gates_done_{l}"), 1)
                with act.Fori(0, NK // RAW - 1) as i:
                    for u in range(RAW):
                        gated_high(i, u)
                        hi_chunk(act, n0 + u + 1, i)
                for u in range(RAW):
                    gated_high(NK // RAW - 1, u)
                    if u < RAW - 1:
                        hi_chunk(act, n0 + NK - RAW + u + 1)

            def load_keys(l):
                act.dma_start(keys, a["keys"][l]).then_inc(sem("keys_landed"), 16)

            load_keys(0)
            split(2, tmp, lambda c: mod_col(0, 3, c), h_hi)
            act.wait_ge(sem("spectra_stored"), 16 * FILTER_GROUPS)
            retrieval(0)

            for c in range(DC):
                square_chunk("v0", c)
            root(5, T)
            hi_chunk(act, FIRST["win"])
            split(3, tmp, lambda c: mod_col(1, 0, c), h_hi)
            n0 = FIRST["win"]

            def p_copy(m):
                multiplied(act, n0 + m)
                if m >= 2:
                    act.wait_ge(sem("conv_done"), m - 1)
                act.activation(pad[:, m % 2, 1:T + 1], ps[:, 4 + m % 4, 0:T], ACT.Copy).then_inc(sem("p_copied"), 1)

            act.wait_ge(sem("pad_ready"), 1)
            def spectrum_copy(o, e):
                kind, h, part, tt = SPECTRUM[e]
                act.wait_ge(sem("spectrum_ready"), len(SPECTRUM) * o + e + 1)
                if o and kind == "transform":
                    act.wait_ge(sem("yf_ready"), 2 * (o - 1) + h + 1)
                dst = tr_z if kind == "turn" else (u_re, u_im)[part]
                act.activation(dst[:, tt, h * 512:(h + 1) * 512], ps[:, e % 4, :], ACT.Copy).then_inc(sem("spectrum_copied"), 1)

            for m in range(3 * DC):
                if m:
                    hi_chunk(act, n0 + m)
                    p_copy(m - 1)
                    if 0 <= m - 1 - WIN_SPECTRUM < len(SPECTRUM):
                        spectrum_copy(0, m - 1 - WIN_SPECTRUM)
            p_copy(3 * DC - 1)
            for o in range(1, ORDER):
                for e in range(len(SPECTRUM)):
                    spectrum_copy(o, e)
            hi_chunk(act, FIRST["wout"])
            for c in range(DC):
                act.wait_ge(sem("z_ready"), DC * (ORDER - 1) + c + 1)
                act.activation(h_hi[:, c, :], zz[:, c, :], ACT.Copy).then_inc(sem("h_hi_ready"), 1)
            residual("wout", "wq1")
            load_keys(1)
            split(5, tmp, lambda c: mod_col(1, 3, c), h_hi)
            retrieval(1)
            for c in range(DC):
                square_chunk("v1", c)
            root(7, T)

        @block.tensor
        def _(pe):
            def sums(k, src, chunks, width):
                pe.wait_ge(sem("square_ready"), SQUARES_BEFORE[k] + 1)
                for tt in range(width // P):
                    for c in range(chunks):
                        last = pe.matmul(sum_view(k, width)[:, tt:tt + 1], src[:, c, tt * P:(tt + 1) * P], ones[:, 0:1],
                                         start=(c == 0), stop=(c == chunks - 1))
                last.then_inc(sem("sum_ready"), 1)

            def sum_chunk(k, c):
                pe.wait_ge(sem("square_ready"), SQUARES_BEFORE[k] + c + 1)
                for tt in range(TT):
                    add = pe.matmul(sum_view(k, T)[:, tt:tt + 1], tmp[:, c, tt * P:(tt + 1) * P], ones[:, 0:1], start=(c == 0), stop=(c == DC - 1))
                if c == DC - 1:
                    add.then_inc(sem("sum_ready"), 1)

            def spread_root(k, width=T):
                pe.wait_ge(sem("root_tok_ready"), k + 1)
                for tt in range(width // P):
                    last = pe.matmul(roots(k, width)[:, tt * P:(tt + 1) * P], root_tok[:, k, tt:tt + 1].broadcast_to([P, P]), ident[:, :],
                                     start=True, stop=True)
                last.then_inc(sem("root_spread"), 1)

            def first_mods(j):
                pe.wait_ge(sem(f"mod_pe_landed_{j}"), 16)
                first, end = PE_GROUPS[j]
                for m in range(first, end):
                    for c in range(DC):
                        last = pe.matmul(ps[:, 7, 2 * m:2 * m + 2], pe_places[j][:, m - first, c * P:(c + 1) * P], c_pair[:, c, :],
                                         start=(c == 0), stop=(c == DC - 1))
                last.then_inc(sem("mod_pe_used"), 1)

            def network(k):
                if k == 0:
                    pe.wait_ge(sem("mlp_landed"), 16 * 4)
                    w, src = w1[0:EMB, :], zfeat[0:EMB, :]
                else:
                    pe.wait_ge(sem("sin_ready"), k)
                    w, src = w23[0:FFN, (k - 1) * FFN:k * FFN], arg[0:FFN, 2, :]
                pe.matmul(ps[0:FFN, 6, k % 2 * T:(k % 2 + 1) * T], w, src, start=True, stop=True).then_inc(sem("ffn_ready"), 1)

            pe.wait_ge(sem("silu_pair_ready"), 1)
            pe.wait_ge(sem("ident_landed"), 16)
            for k in range(2):
                for c in range(DC):
                    last = pe.matmul(ps[:, 1 + 2 * k + c // 4, (c % 4) * P:(c % 4 + 1) * P], c_pair[:, c, k:k + 1].broadcast_to([P, P]), ident[:, :],
                                     start=True, stop=True)
                last.then_inc(sem("silu_spread"), 1)
            first_mods(0)
            pe.wait_ge(sem("ones_ready"), 1)
            sums(0, tmp, DC, T)
            first_mods(1)
            spread_root(0)
            first_mods(2)
            sums(1, tmp_c, DC, T)
            spread_root(1)
            for m in range(DKV):
                if m in (0, 3, 5):
                    network({0: 0, 3: 1, 5: 2}[m])
                if m >= 2:
                    pe.wait_ge(sem("lat_ready"), m - 1)
                outs = [(ps[:, 1 + m % 2, 0:T], h_hi, h_lo)]
                if m == QC:
                    pe.wait_ge(sem("h_lo_ready"), 2 * DC)
                if m >= QC:
                    outs.append((ps[:, 3 + m % 2, 0:T], c_hi, c_lo))
                product(pe, m, outs, fresh=0 if m == 0 else None)
                if m == QC + 1:
                    sums(2, sq_q, QC, T)
            spread_root(2)
            sums(3, sq_k, KC, 512)
            pe.wait_ge(sem("attn_landed"), 64)
            pe.wait_ge(sem("cq_ready"), 1)
            for p in range(HEADS // 2):
                if p >= 2:
                    pe.wait_ge(sem("q_nope_ready"), p - 1)
                    pe.wait_ge(sem("q_rope_ready"), p - 1)
                for j in range(2):
                    for c in range(QC):
                        last = pe.matmul(ps[:, 1 + p % 2, j * T:(j + 1) * T], w_uq[:, c, 2 * p + j, :], cq[:, c, :],
                                         start=(c == 0), stop=(c == QC - 1))
                last.then_inc(sem("q_ready"), 1)
                if p == 0:
                    spread_root(3, 512)
            pe.wait_ge(sem("ckv_ready"), 1)
            for k in range(8):
                if k >= 2:
                    pe.wait_ge(sem("v_keys_ready"), k - 1)
                for c in range(KC):
                    last = pe.matmul(ps[:, 3 + k % 2, :], ckv[:, c, (k // 2) * P:(k // 2 + 1) * P],
                                     w_uv[:, c, (k % 2) * 512:(k % 2 + 1) * 512], start=(c == 0), stop=(c == KC - 1))
                last.then_inc(sem("v_ready"), 1)
            pe.wait_ge(sem("v_keys_ready"), 8)
            pe.wait_ge(sem("q_nope_ready"), 8)
            pe.wait_ge(sem("q_rope_ready"), 8)
            pe.wait_ge(sem("k_rope_ready"), 1)

            def score(u):
                hh, qt = u // 2, u % 2
                pe.wait_ge(sem("k_heads_ready"), hh + 1)
                if u >= 2:
                    pe.wait_ge(sem("exp_ready"), u - 1)
                pe.matmul(ps[:, 2 + u % 2, :], q_heads[0:QK, hh, qt * P:(qt + 1) * P], k_heads[0:QK, hh % 4, :], start=True, stop=True)\
                  .then_inc(sem("scores_ready"), 1)

            def turn(u):
                pe.wait_ge(sem("probs_ready"), u + 1)
                if u >= 2:
                    pe.wait_ge(sem("probs_t_ready"), u - 1)
                for k in range(4):
                    last = pe.transpose(ps[:, 4 + u % 2, k * P:(k + 1) * P], probs[:, u % 2, k * P:(k + 1) * P], ident[:, :])
                last.then_inc(sem("turned"), 1)

            def mix(hh):
                pe.wait_ge(sem("probs_t_ready"), 2 * hh + 2)
                if hh >= 2:
                    pe.wait_ge(sem("o_lo_ready"), hh - 1)
                for k in range(4):
                    last = pe.matmul(ps[0:VD, 6 + hh % 2, 0:T], v_keys[:, k, hh * VD:(hh + 1) * VD], probs_t[:, hh % 2, k, :],
                                     start=(k == 0), stop=(k == 3))
                last.then_inc(sem("o_ready"), 1)

            def filter_product(g, j):
                if j == 0:
                    pe.wait_ge(sem(f"w4_landed_{g % 2}"), 16 * (g // 2 + 1))
                    if g:
                        pe.wait_ge(sem("kf_copied"), 4 * g)
                    else:
                        pe.wait_ge(sem("sin_ready"), 3)
                else:
                    pe.wait_ge(sem("hf_ready"), 4 * g + j)
                mt, fb = j // 2, j % 2
                pe.matmul(ps[:, 0, :], arg[0:FFN, 2, mt * P:(mt + 1) * P], f_w4[0:FFN, g % 2, fb, :], start=True, stop=True)\
                  .then_inc(sem("hf_prod"), 1)

            def filter_norms(g):
                pe.wait_ge(sem("hf_abs_ready"), TT * (g + 1))
                for c in range(DC // 2):
                    for k in range(4):
                        last = pe.matmul(ps[:, 0, c:c + 1], f_abs[:, k // 2, k % 2, c * P:(c + 1) * P], ones[:, 0:1],
                                         start=(k == 0), stop=(k == 3))
                last.then_inc(sem("norm_sum"), 1)

            def filter_spectrum(g, j):
                if j == 0:
                    pe.wait_ge(sem("hf_mixed"), g + 1)
                    pe.wait_ge(sem("inv_norm_ready"), g + 1)
                else:
                    pe.wait_ge(sem("kf_copied"), 4 * g + j)
                part, kt = j // 2, j % 2
                for mt in range(TT):
                    last = pe.matmul(ps[:, 0, :], f_dft[:, part, mt, kt * P:(kt + 1) * P], f_diff[:, mt, :] if part else f_hf[:, mt, 0, :],
                                     start=(mt == 0), stop=(mt == TT - 1))
                last.then_inc(sem("kf_ready"), 1)

            def filter_step(p, j):
                if p % 2 == 0:
                    filter_product(p // 2, j)
                elif j == 0:
                    filter_norms(p // 2)
                else:
                    filter_spectrum(p // 2, j - 1)

            pe.wait_ge(sem("filter_landed"), 32)
            def key_products(p):
                if p:
                    pe.wait_ge(sem("k_heads_ready"), 2 * p)
                for c in range(KC):
                    last = pe.matmul(ps[:, 1, :], w_uk[:, c, p, :], ckv[:, c, :], start=(c == 0), stop=(c == KC - 1))
                last.then_inc(sem("k_ready"), 1)

            key_products(0)
            score(0)
            for u in range(STEPS):
                p, j = u // 4, u % 4
                if u + 1 < STEPS:
                    score(u + 1)
                filter_step(p, j)
                turn(u)
                if j == 1 and p + 1 < HEADS // 2:
                    key_products(p + 1)
                if u % 2 == 0 and u:
                    mix(u // 2 - 1)
                if p % 2 and j == 3:
                    filter_spectrum(p // 2, 3)
            mix(HEADS - 1)

            def residual_products(name, k, fresh=None):
                for m in range(DC):
                    if m >= 2:
                        renewed(pe, name, m - 1)
                    product(pe, FIRST[name] + m, [(ps[:, 1 + m % 2, 0:T], h_hi, h_lo)], fresh=fresh if m == 0 else None)
                    if m >= 2:
                        sum_chunk(k, m - 2)
                for m in range(DC - 2, DC):
                    sum_chunk(k, m)
                spread_root(k)

            pe.wait_ge(sem("o_lo_ready"), HEADS)
            residual_products("wo", 4)

            def retrieval(l):
                n0 = FIRST[f"wq{l}"]
                for u in range(RAW):
                    product(pe, n0 + u, [(ps[:, 4 + u, 0:T], h_hi, h_lo)], fresh=(2, 5)[l] if u == 0 else None)
                with pe.Fori(1, HP // RAW) as i:
                    for u in range(RAW):
                        pe.wait_ge(sem(f"q_all_ready_{l}"), i * RAW + (u + 1 - RAW))
                        product(pe, n0 + u, [(ps[:, 4 + u, 0:T], h_hi, h_lo)], i)
                pe.wait_ge(sem("keys_landed"), 16 * (l + 1))
                pe.wait_ge(sem(f"q_all_ready_{l}"), HP)
                for m in range(HP):
                    if m >= 4:
                        pe.wait_ge(sem(f"scores_copied_{l}"), m - 3)
                    for tt in range(TT):
                        last = pe.matmul(ps[:, 4 + m % 4, tt * P:(tt + 1) * P], q_all[:, m, tt * P:(tt + 1) * P], keys[:, m, :],
                                         start=True, stop=True)
                    last.then_inc(sem(f"key_scores_{l}"), 1)
                n0 = FIRST[f"u{l}"]
                pe.wait_ge(sem(f"scores_copied_{l}"), HP)
                for u in range(RAW):
                    product(pe, n0 + u, [(ps[:, 4 + u, 0:T], h_hi, h_lo)])
                with pe.Fori(1, U_TOPK // RAW) as i:
                    for u in range(RAW):
                        pe.wait_ge(sem(f"acts_ready_{l}"), i * RAW + (u + 1 - RAW))
                        product(pe, n0 + u, [(ps[:, 4 + u, 0:T], h_hi, h_lo)], i)
                for u in range(RAW):
                    pe.wait_ge(sem(f"acts_ready_{l}"), U_TOPK + u + 1 - RAW)
                    product(pe, n0 + U_TOPK + u, [(ps[:, 4 + u, 0:T], h_hi, h_lo)])
                    if u == 2:
                        pe.wait_ge(sem(f"sel_ready_{l}"), 1)
                        for k, src in enumerate((fi_i, fi_j, fs)):
                            for tt in range(TT):
                                last = pe.transpose(ps[:, k, tt * P:(tt + 1) * P], src[:, tt, :], ident[:, :])
                        last.then_inc(sem(f"sel_turned_{l}"), 1)

                def gates(b, g):
                    pe.wait_ge(sem(f"onehot_ready_{l}"), g + 1)
                    for t in range(4):
                        last = pe.matmul(ps[:, b, t * P:(t + 1) * P], oh_i[:, b, t, :], oh_j[:, b, t, :], start=True, stop=True)
                    last.then_inc(sem(f"gate_ready_{l}"), 1)

                with pe.Fori(0, GATE_STEPS) as i:
                    for u in range(RAW):
                        pe.wait_ge(sem(f"acts_ready_{l}"), i * RAW + (U_GATED + u + 1 - RAW))
                        product(pe, n0 + U_GATED + u, [(ps[:, 4 + u, 0:T], h_hi, h_lo)], i)
                        gates(u % 2, i * RAW + u)
                for g in range(GATE_STEPS * RAW, GROUPS):
                    gates(g % 2, g)
                pe.wait_ge(sem(f"gates_done_{l}"), 1)
                for b in range(4):
                    pe.matmul(ps[:, b, :], ones[:, :], zeros[:, :], start=True, stop=False, skip_group_check=True)
                n0 = FIRST[f"v{l}"]
                with pe.Fori(0, NK // RAW) as i:
                    for u in range(RAW):
                        n = n0 + u
                        pe.wait_ge(sem(f"g_lo_ready_{l}"), i * RAW + (u + 1))
                        for k in range(2):
                            pe.wait_ge(sem("w_lo_b_ready" if k else "w_lo_a_ready"), i * RAW + (n + 1))
                            for c in range(4 * k, 4 * k + 4):
                                o = ps[:, c // 2, (c % 2) * T:(c % 2 + 1) * T]
                                wh, wl = block_of(n, c)
                                pe.matmul(o, wh, h_hi[:, u, :], start=False, stop=False, skip_group_check=True)
                                pe.matmul(o, wh, h_lo[:, u, :], start=False, stop=False, skip_group_check=True)
                                last = pe.matmul(o, wl, h_hi[:, u, :], start=False, stop=False, skip_group_check=True)
                            last.then_inc(sem("w_used"), 1)

            retrieval(0)

            for c in range(DC):
                sum_chunk(5, c)
            spread_root(5)
            def spectrum(o, e):
                kind, h, part, tt = SPECTRUM[e]
                done = len(SPECTRUM) * o
                if o or e >= 4:
                    pe.wait_ge(sem("spectrum_copied"), done + e - 3)
                if kind == "turn":
                    if o == 0:
                        pe.wait_ge(sem("conv_done"), (h + 1) * DC // 2)
                    else:
                        pe.wait_ge(sem("z_ready"), (o - 1) * DC + (h + 1) * DC // 2)
                    src = zz if o else conv
                    for j in range(4):
                        last = pe.transpose(ps[:, e % 4, j * P:(j + 1) * P], src[:, 4 * h + j, tt * P:(tt + 1) * P], ident[:, :])
                else:
                    pe.wait_ge(sem("spectrum_copied"), done + SP_HALF * h + TT)
                    pe.wait_ge(sem("dft_landed"), 16)
                    for mt in range(TT):
                        last = pe.matmul(ps[:, e % 4, :], dft[:, part, mt, tt * P:(tt + 1) * P], tr_z[:, mt, h * 512:(h + 1) * 512],
                                         start=(mt == 0), stop=(mt == TT - 1))
                last.then_inc(sem("spectrum_ready"), 1)

            for m in range(3 * DC):
                if m >= 4:
                    pe.wait_ge(sem("p_copied"), m - 3)
                product(pe, FIRST["win"] + m, [(ps[:, 4 + m % 4, 0:T], h_hi, h_lo)], fresh=3 if m == 0 else None)
                if 0 <= m - WIN_SPECTRUM < len(SPECTRUM):
                    spectrum(0, m - WIN_SPECTRUM)
            pe.wait_ge(sem("p_copied"), 3 * DC)
            for o in range(ORDER):
                if o:
                    for e in range(len(SPECTRUM)):
                        spectrum(o, e)
                for c in range(DC):
                    pe.wait_ge(sem("yf_ready"), 2 * o + c // (DC // 2) + 1)
                    if DC * o + c >= 4:
                        pe.wait_ge(sem("z_ready"), DC * o + c - 3)
                    for k in range(4):
                        part, kt = k // 2, k % 2
                        last = pe.matmul(ps[:, 4 + c % 4, 0:T], (y_re, y_im)[part][:, kt, c * P:(c + 1) * P], dft[:, 2 + part, kt, :],
                                         start=(k == 0), stop=(k == 3))
                    last.then_inc(sem("yt_ready"), 1)
            residual_products("wout", 6, fresh=4)
            retrieval(1)
            for c in range(DC):
                sum_chunk(7, c)
            spread_root(7)

        @block.vector
        def _(dve):
            ch = Chain(dve, sem("dve_chain"))
            link = ch.link

            def b_cols(name, k, n):
                return cols[:, COLS[name][0] + k:COLS[name][0] + k + n]

            def gain_of(g, m, name, k):
                link(dve.scalar_tensor_tensor(out=gain[:, g * DC:(g + 1) * DC], in0=m, scalar=1.0, in1=b_cols(name, k, DC),
                                              op0=ALU.add, op1=ALU.mult))

            def root(k, width=T, features=D):
                r, e, total = root_tok[:, k, 0:width // P], root_tmp[:, 0:width // P], sum_view(k, width)
                dve.wait_ge(sem("root_ready"), k + 1)
                link(dve.reciprocal(r, r))
                link(dve.tensor_tensor(e, r, r, ALU.mult))
                link(dve.scalar_tensor_tensor(out=e, in0=total, scalar=features * EPS, in1=e, op0=ALU.add, op1=ALU.mult))
                scale = math.sqrt(features)
                link(dve.tensor_scalar(e, e, -0.5 * scale, 1.5 * scale, ALU.mult, ALU.add))
                dve.tensor_tensor(r, r, e, ALU.mult).then_inc(sem("root_tok_ready"), 1)

            def normalise(k, src, dst, width, name):
                dve.wait_ge(sem("root_spread"), k + 1)
                for c in range(src.shape[1]):
                    last = dve.scalar_tensor_tensor(out=dst[:, c, :], in0=src[:, c, :], scalar=col(name, c), in1=roots(k, width),
                                                    op0=ALU.mult, op1=ALU.mult)
                return last

            def modulated(k, s, src, g, shift, hi, lo, t=tmp, beside=None):
                def scaled(c):
                    dve.scalar_tensor_tensor(out=t[:, c, :], in0=src[:, c, :], scalar=gain[:, g * DC + c:g * DC + c + 1],
                                             in1=roots(k), op0=ALU.mult, op1=ALU.mult).then_inc(sem("to_split"), 1)
                dve.wait_ge(sem("root_spread"), k + 1)
                scaled(0)
                for c in range(DC):
                    if c + 1 < DC:
                        scaled(c + 1)
                    if c == DC // 2 and beside is not None:
                        lo_chunk(dve, beside)
                    dve.wait_ge(sem("h_hi_ready"), DC * s + c + 1)
                    dve.scalar_tensor_tensor(out=lo[:, c, :], in0=t[:, c, :], scalar=shift(c), in1=hi[:, c, :],
                                             op0=ALU.add, op1=ALU.subtract).then_inc(sem("h_lo_ready"), 1)

            link(dve.memset(zero[:, :], 0.0))
            dve.memset(zeros[:, :], 0.0)
            for features, column in EPS_COLUMN.items():
                last = dve.memset(zero[:, column], features * EPS)
            link(last)
            dve.wait_ge(sem("c_pair_exp_ready"), 1)
            link(dve.tensor_scalar(c_pair_exp[:, :, :], c_pair_exp[:, :, :], 1.0, None, ALU.add))
            link(dve.reciprocal(c_pair_exp[:, :, :], c_pair_exp[:, :, :]))
            dve.tensor_tensor(c_pair[:, :, :], c_pair[:, :, :], c_pair_exp[:, :, :], ALU.mult).then_inc(sem("silu_pair_ready"), 1)
            def network(k):
                r, t1 = arg[0:FFN, 0, :], arg[0:FFN, 1, :]
                dve.wait_ge(sem("mlp_landed"), 16 * 4)
                dve.wait_ge(sem("ffn_ready"), k + 1)
                link(dve.tensor_scalar(r, ps[0:FFN, 6, k % 2 * T:(k % 2 + 1) * T], fcol[0:FFN, k:k + 1], fcol[0:FFN, 3:4], ALU.add, ALU.mult))
                link(dve.tensor_scalar(t1, r, 1 / (2 * math.pi), MAGIC, ALU.mult, ALU.add))
                link(dve.tensor_scalar(t1, t1, MAGIC, None, ALU.subtract))
                for part in (TWO_PI_1, TWO_PI_2, TWO_PI_3):
                    link(dve.scalar_tensor_tensor(out=r, in0=t1, scalar=-part, in1=r, op0=ALU.mult, op1=ALU.add))
                dve.tensor_scalar(r, r, 3.1415925, -3.1415925, ALU.min, ALU.max).then_inc(sem("arg_ready"), 1)

            def dot(k, slot, dst):
                dve.tensor_tensor_reduce(mod_raw[:, slot, :], mod_raw[:, slot, :], silu[:, :], 1.0, 0.0, ALU.mult, ALU.add, dst)\
                   .then_inc(sem("mod_used"), 1)

            dve.wait_ge(sem("silu_ready"), 2)
            for j in range(3):
                if j == 2:
                    root(0, T)
                dve.wait_ge(sem(f"mod_dve_landed_{j}"), 16)
                first, end = DVE_GROUPS[j]
                for m in range(first, end):
                    w = dve_places[j][:, m - first, :]
                    link(dve.tensor_tensor_reduce(products, w, silu_c, 1.0, 0.0, ALU.mult, ALU.add, modc[:, m:m + 1]))
                    last = dve.tensor_tensor_reduce(w, w, silu[:, :], 1.0, 0.0, ALU.mult, ALU.add, mod[:, m:m + 1])
                last.then_inc(sem("mod_dve_used"), 1)
            root(1, T)
            dve.wait_ge(sem("mod_dve_used"), 3)
            dve.wait_ge(sem("mod_pe_used"), 3)
            dve.wait_ge(sem("cols_landed"), 16)
            both = ps[:, 7, 0:2 * MODS_PE].rearrange("p (a b) -> p a b", b=2)
            dve.tensor_tensor(mod[:, 0:MODS_PE], both[:, :, 0], b_cols("mod_b", 0, MODS_PE), ALU.add)
            dve.tensor_tensor(modc[:, 0:MODS_PE], both[:, :, 1], b_cols("mod_b", 0, MODS_PE), ALU.add)
            late = slice(MODS_PE, MODS_FIRST)
            dve.tensor_tensor(mod[:, late], mod[:, late], b_cols("mod_b", MODS_PE, MODS_FIRST - MODS_PE), ALU.add)
            link(dve.tensor_tensor(modc[:, late], modc[:, late], b_cols("mod_b", MODS_PE, MODS_FIRST - MODS_PE), ALU.add))
            gain_of(0, mod[:, DC:2 * DC], "mix_g", 0)
            gain_of(1, modc[:, DC:2 * DC], "mix_g", 0)
            lo_chunk(dve, 0)
            lo_chunk(dve, 1)
            modulated(0, 0, x[:, :, :], 0, lambda c: mod[:, c:c + 1], h_hi, h_lo)
            for m in range(DKV):
                if m >= 3:
                    lo_chunk(dve, m)
                if m == 1:
                    modulated(1, 1, cx, 1, lambda c: modc[:, c:c + 1], c_hi, c_lo, tmp_c, beside=2)
                if m in (1, 3):
                    network(m // 2)
            root(2, T, QL)
            normalise(2, lat[:, 0:QC, 0:T], cq, T, "q_g").then_inc(sem("cq_ready"), 1)
            network(2)
            root(3, 512, KVL)
            normalise(3, lat[:, QC:QC + KC, :], ckv, 512, "kv_g").then_inc(sem("ckv_ready"), 1)
            dve.wait_ge(sem("attn_landed"), 64)
            lr = lat[:, DKV - 1, :]
            link(dve.tensor_tensor(rope_s[NOPE:QK, 0, :], lr[QK:P, 0:T], rope[QK:P, :], ALU.mult))
            link(dve.tensor_tensor(rope_c[NOPE:QK, 0, :], lr[NOPE:QK, 0:T], rope[NOPE:QK, :], ALU.mult))
            for s in range(4):
                dve.tensor_tensor(k_heads[NOPE:QK, s, 0:T], rope_s[NOPE:QK, 0, :], rope_c[NOPE:QK, 0, :], ALU.add)
                last = dve.tensor_copy(k_heads[NOPE:QK, s, T:2 * T], lr[NOPE:QK, T:2 * T])
            last.then_inc(sem("k_rope_ready"), 1)
            dve.wait_ge(sem("k_rope_ready"), 1)
            for p in range(HEADS // 2):
                dve.wait_ge(sem("q_ready"), p + 1)
                bank = ps[:, 1 + p % 2, :].rearrange("p (a b) -> p a b", a=2)
                link(dve.tensor_tensor(rope_s[NOPE:QK, :, :], bank[QK:P, :, :], rope[QK:P, :].unsqueeze(1).broadcast_to([ROPE, 2, T]), ALU.mult))
                link(dve.tensor_tensor(rope_c[NOPE:QK, :, :], bank[NOPE:QK, :, :], rope[NOPE:QK, :].unsqueeze(1).broadcast_to([ROPE, 2, T]), ALU.mult))
                dve.tensor_tensor(q_heads[NOPE:QK, 2 * p:2 * p + 2, :], rope_s[NOPE:QK, :, :], rope_c[NOPE:QK, :, :], ALU.add)\
                   .then_inc(sem("q_rope_ready"), 1)
                dve.wait_ge(sem("q_rope_ready"), p + 1)

            def row_max(u):
                dve.wait_ge(sem("scores_ready"), u + 1)
                k = u % 8
                if u >= 8:
                    dve.wait_ge(sem("exp_ready"), u - 7)
                link(dve.tensor_reduce(smax[:, 24 + k:25 + k], ps[:, 2 + u % 2, :], AX.X, ALU.max))
                dve.tensor_scalar(smax[:, k:k + 1], smax[:, 24 + k:25 + k], -SCALE, None, ALU.mult).then_inc(sem("max_ready"), 1)

            def norm_probs(u):
                dve.wait_ge(sem("exp_ready"), u + 1)
                k = u % 8
                link(dve.reciprocal(smax[:, 16 + k:17 + k], smax[:, 8 + k:9 + k]))
                dve.tensor_scalar(probs[:, u % 2, :], probs[:, u % 2, :], smax[:, 16 + k:17 + k], None, ALU.mult).then_inc(sem("probs_ready"), 1)

            def filter_step(p, j):
                g = p // 2
                if p % 2 == 0:
                    mt, fb = j // 2, j % 2
                    if j == 0:
                        dve.wait_ge(sem("decay_ready"), g + 1)
                        if g:
                            dve.wait_ge(sem("kf_ready"), 4 * g)
                    dve.wait_ge(sem("hf_prod"), 4 * g + j + 1)
                    dve.tensor_tensor(f_hf[:, mt, fb, :], ps[:, 0, :], decay[:, mt, :], ALU.mult).then_inc(sem("hf_ready"), 1)
                    if j == 1:
                        dve.wait_ge(sem("hf_ready"), 4 * g + 2)
                        dve.memset(f_hf[0:1, 0, 1, :], 0.0).then_inc(sem("hf_zeroed"), 1)
                elif j == 0:
                    dve.wait_ge(sem("hf_abs_ready"), TT * (g + 1))
                    link(dve.tensor_tensor(f_diff, f_hf[:, :, 0, :], f_hf[:, :, 1, :], ALU.subtract))
                    dve.tensor_tensor(f_hf[:, :, 0, :], f_hf[:, :, 0, :], f_hf[:, :, 1, :], ALU.add).then_inc(sem("hf_mixed"), 1)
                    dve.wait_ge(sem("norm_sum"), g + 1)
                    at = g // 2 * DC + g % 2 * (DC // 2)
                    dve.reciprocal(inv_norm[:, at:at + DC // 2], ps[:, 0, 0:DC // 2]).then_inc(sem("inv_norm_ready"), 1)

            def beside(p, j):
                filter_step(p, j)
                k = MODS_FIRST + 4 * p + j
                dve.wait_ge(sem(f"mod_landed_{k % 2}"), 16 * ((k - MODS_FIRST) // 2 + 1))
                dot(k, k % 2, mod[:, k:k + 1])

            def output_low(hh):
                o = (hh % 2) * VD
                dve.wait_ge(sem("o_hi_ready"), hh + 1)
                dve.tensor_tensor(h_lo[o:o + VD, hh // 2, :], ps[0:VD, 6 + hh % 2, 0:T], h_hi[o:o + VD, hh // 2, :], ALU.subtract)\
                   .then_inc(sem("o_lo_ready"), 1)

            row_max(0)
            for u in range(STEPS):
                norm_probs(u)
                if u + 1 < STEPS:
                    row_max(u + 1)
                beside(u // 4, u % 4)
                if u % 2 and u >= 3:
                    output_low(u // 2 - 1)
            output_low(HEADS - 1)
            dve.wait_ge(sem("mod_used"), MODS - MODS_FIRST)
            link(dve.tensor_tensor(mod[:, 2 * DC:MODS], mod[:, 2 * DC:MODS], b_cols("mod_b", 2 * DC, MODS - 2 * DC), ALU.add))
            gain_of(2, mod[:, 4 * DC:5 * DC], "ffn_g", 0)

            def add_residual(m, bank, l, part):
                return dve.scalar_tensor_tensor(out=x[:, m, :], in0=bank, scalar=mod_col(l, part, m), in1=x[:, m, :], op0=ALU.mult, op1=ALU.add)

            def residual(name, l):
                for m in range(DC):
                    if m or name == "wo":
                        lo_chunk(dve, FIRST[name] + m)
                    if m:
                        multiplied(dve, FIRST[name] + m - 1)
                        add_residual(m - 1, ps[:, 1 + (m - 1) % 2, 0:T], l, 2).then_inc(sem("x_renewed"), 1)
                multiplied(dve, FIRST[name] + DC - 1)
                add_residual(DC - 1, ps[:, 1 + (DC - 1) % 2, 0:T], l, 2).then_inc(sem("x_renewed"), 1)

            residual("wo", 0)
            root(4, T)
            lo_chunk(dve, FIRST["wq0"])
            modulated(4, 2, x[:, :, :], 2, lambda c: mod_col(0, 3, c), h_hi, h_lo)

            def top16(rows):
                dve.drain()
                for v, rest, o, x in rows:
                    dve.max(o[:, 0:8], v)
                dve.drain()
                for v, rest, o, x in rows:
                    dve.max_index(x[:, 0:8], o[:, 0:8], v)
                    dve.match_replace(rest, o[:, 0:8], v, LOWEST)
                dve.drain()
                for v, rest, o, x in rows:
                    dve.max(o[:, 8:16], rest)
                dve.drain()
                for v, rest, o, x in rows:
                    dve.max_index(x[:, 8:16], o[:, 8:16], rest)

            iota16 = iota[:, 0:TOPK].unsqueeze(1).unsqueeze(1).broadcast_to([P, 2, TOPK, TOPK])

            def retrieval(l):
                n0 = FIRST[f"wq{l}"]
                dve.wait_ge(sem("iota_landed"), 16)
                with dve.Fori(0, HP // RAW - 1) as i:
                    for u in range(RAW):
                        lo_chunk(dve, n0 + 1 + u, i)
                for u in range(1, RAW):
                    lo_chunk(dve, n0 + HP - RAW + u)
                n0 = FIRST[f"u{l}"]
                lo_chunk(dve, n0)
                dve.wait_ge(sem(f"scores_copied_{l}"), HP)
                with ch.loop(TT * PH, 5) as i:
                    dve.wait_ge(sem(f"pair_ready_{l}"), i + 1)
                    lo_chunk(dve, n0 + 1, i)
                    top16([(pair[:, p, :], rest[:, p, :], sv[:, p, :], si_u[:, p, :]) for p in range(2)])
                    lo_chunk(dve, n0 + 2, i)
                    dve.drain()
                    dve.tensor_copy(si_f, si_u).then_inc(sem(f"pair_used_{l}"), 1)
                    dve.tensor_tensor(cand, sv[:, 0, :].unsqueeze(2).broadcast_to([P, TOPK, TOPK]),
                                      sv[:, 1, :].unsqueeze(1).broadcast_to([P, TOPK, TOPK]), ALU.add)
                    top16([(cand_flat, rest_flat, fs_one, fi_u)])
                    lo_chunk(dve, n0 + 3, i)
                    dve.drain()
                    dve.tensor_scalar(fa_u[:, 0, :], fi_u, 4, None, ALU.logical_shift_right)
                    link(dve.tensor_scalar(fa_u[:, 1, :], fi_u, TOPK - 1, None, ALU.bitwise_and))
                    link(dve.tensor_copy(fa_f, fa_u))
                    link(dve.tensor_tensor(eq, fa_f.unsqueeze(3).broadcast_to([P, 2, TOPK, TOPK]), iota16, ALU.is_equal))
                    link(dve.tensor_tensor(eq, eq, si_f.unsqueeze(2).broadcast_to([P, 2, TOPK, TOPK]), ALU.mult))
                    lo_chunk(dve, n0 + 4, i)
                    link(dve.tensor_reduce(keys_of, eq, AX.X, ALU.add))
                    dve.tensor_copy(fi_both[:, :, bass.ds(i, 1), :].rearrange("p a o k -> p a (o k)"), keys_of)
                    dve.tensor_scalar(fs_v[:, bass.ds(i, 1), :].rearrange("p o k -> p (o k)"), fs_one, fs_one[:, 0:1], None, ALU.subtract)
                dve.tensor_copy(got[:, 0:1], fs_one[:, 0:1]).then_inc(sem(f"topk_done_{l}"), 1)
                lo_chunk(dve, n0 + U_TOPK + 1)
                lo_chunk(dve, n0 + U_TOPK + 2)
                dve.wait_ge(sem(f"fs_exp_{l}"), 1)
                link(dve.tensor_reduce(fsum, fs_v, AX.X, ALU.add))
                link(dve.reciprocal(fsum, fsum))
                dve.tensor_tensor(fs_v, fs_v, fsum.unsqueeze(2).broadcast_to([P, TT * PH, TOPK]), ALU.mult).then_inc(sem(f"sel_ready_{l}"), 1)
                lo_chunk(dve, n0 + U_TOPK + 3)
                lo_chunk(dve, n0 + U_GATED)
                dve.wait_ge(sem(f"sel_turned_{l}"), 1)
                link(dve.tensor_copy(sel_g[:, :], ps[:, 2, 0:T]))
                for k, dst in enumerate((sel_i, sel_j)):
                    dve.tensor_copy(dst[:, :], ps[:, k, 0:T]).then_inc(sem(f"gelu_slots_{l}"), 1)

                def onehots(b, g):
                    four = bass.ds(g * 4, 4)
                    dve.tensor_tensor(oh_i[:, b, :, :], iota[:, :].unsqueeze(1).broadcast_to([P, 4, P]),
                                      sel_i[:, four].unsqueeze(2).broadcast_to([P, 4, P]), ALU.is_equal)
                    for t in range(4):
                        c = bass.ds(g * 4 + t, 1)
                        last = dve.tensor_scalar(oh_j[:, b, t, :], iota[:, :], sel_j[:, c], sel_g[:, c], ALU.is_equal, ALU.mult)
                    last.then_inc(sem(f"onehot_ready_{l}"), 1)

                def place_gates(b, g):
                    dve.wait_ge(sem(f"gate_ready_{l}"), g + 1)
                    some = acts[:, :, bass.ds(g * 4, 4)]
                    return dve.tensor_tensor(some, ps[:, b, :].rearrange("p (t j) -> p j t", t=4), some, ALU.mult)

                def place_acts(u, i):
                    dve.wait_ge(sem(f"acts_ready_{l}"), i * RAW + (U_GATED + u + 1))
                    some = acts[:, bass.ds(i * RAW + (U_GATED + u), 1), :].rearrange("p o t -> p (o t)")
                    dve.tensor_tensor(some, some, gelu_out[:, u % 2, :], ALU.mult).then_inc(sem(f"gelu_slots_{l}"), 1)
                    dve.wait_ge(sem(f"gelu_slots_{l}"), i * RAW + (u + 3))

                dve.wait_ge(sem(f"ones_in_place_{l}"), RAW)
                dve.wait_ge(sem(f"ones_behind_{l}"), ONES_BESIDE * (TT * PH - 1))
                dve.wait_ge(sem(f"acts_ready_{l}"), U_GATED)
                dve.wait_ge(sem(f"gelu_slots_{l}"), 2)
                onehots(0, 0)
                with ch.loop(GATE_STEPS - 1, RAW) as i:
                    for u in range(RAW):
                        lo_chunk(dve, n0 + U_GATED + u + 1, i)
                        onehots((u + 1) % 2, i * RAW + (u + 1))
                        place_acts(u, i)
                        link(place_gates(u % 2, i * RAW + u))
                for u in range(RAW):
                    i = GATE_STEPS - 1
                    if u < RAW - 1:
                        lo_chunk(dve, n0 + NK - RAW + 1 + u)
                    onehots((u + 1) % 2, i * RAW + (u + 1))
                    place_acts(u, i)
                    link(place_gates(u % 2, i * RAW + u))
                for g in range(GATE_STEPS * RAW, GROUPS - 1):
                    onehots((g + 1) % 2, g + 1)
                    link(place_gates(g % 2, g))
                lo_chunk(dve, FIRST[f"v{l}"])
                place_gates((GROUPS - 1) % 2, GROUPS - 1).then_inc(sem(f"gates_done_{l}"), 1)
                n0 = FIRST[f"v{l}"]

                def g_low(i, u, step):
                    dve.wait_ge(sem(f"g_hi_ready_{l}"), i * step + (u + 1))
                    dve.tensor_tensor(h_lo[:, u % RAW, :], acts[:, bass.ds(i * step + u, 1), :].rearrange("p o t -> p (o t)"), h_hi[:, u % RAW, :], ALU.subtract)\
                       .then_inc(sem(f"g_lo_ready_{l}"), 1)

                if l == 0:
                    def values_step(i, last=False):
                        for u in range(16):
                            g_low(i, u, 16)
                            if not (last and u == 15):
                                lo_chunk(dve, n0 + u + 1, i, 16)
                            if u in MOD_BESIDE:
                                m = MOD_BESIDE.index(u)
                                dve.wait_ge(sem(f"mod_landed_{m % 2}"), i * 48 + 16 * ((MODS - MODS_FIRST + m) // 2 + 1))
                                dot(m, m % 2, got[:, m:m + 1])
                        dve.wait_ge(sem("mod_used"), i * 6 + (MODS - MODS_FIRST + 6))
                        dve.tensor_copy(mod[:, bass.ds(i * 6 + MODS, 6)], got[:, 0:6]).then_inc(sem("mod_copied"), 1)
                        dve.wait_ge(sem("mod_copied"), i + 1)

                    with dve.Fori(0, NK // 16 - 1) as i:
                        values_step(i)
                    values_step(NK // 16 - 1, last=True)
                else:
                    with dve.Fori(0, NK // RAW - 1) as i:
                        for u in range(RAW):
                            g_low(i, u, RAW)
                            lo_chunk(dve, n0 + u + 1, i)
                    for u in range(RAW):
                        g_low(NK // RAW - 1, u, RAW)
                        if u < RAW - 1:
                            lo_chunk(dve, n0 + NK - RAW + u + 1)
                multiplied(dve, n0 + NK - 1)
                for c in range(DC):
                    add_residual(c, ps[:, c // 2, (c % 2) * T:(c % 2 + 1) * T], l, 5).then_inc(sem("x_renewed"), 1)

            retrieval(0)
            link(dve.tensor_tensor(mod[:, MODS:2 * MODS], mod[:, MODS:2 * MODS], b_cols("mod_b", MODS, MODS), ALU.add))
            gain_of(3, mod[:, MODS + DC:MODS + 2 * DC], "mix_g", DC)
            gain_of(4, mod[:, MODS + 4 * DC:MODS + 5 * DC], "ffn_g", DC)

            dve.memset(pad[:, :, :], 0.0).then_inc(sem("pad_ready"), 1)
            root(5, T)
            lo_chunk(dve, FIRST["win"])
            modulated(5, 3, x[:, :, :], 3, lambda c: mod_col(1, 0, c), h_hi, h_lo)
            n0 = FIRST["win"]

            def short_conv(m):
                dve.wait_ge(sem("p_copied"), m + 1)
                b = pad[:, m % 2, :]
                link(dve.tensor_scalar(conv[:, m, :], b[:, 0:T], col("conv_w", m), col("conv_b", m), ALU.mult, ALU.add))
                link(dve.scalar_tensor_tensor(out=conv[:, m, :], in0=b[:, 1:T + 1], scalar=col("conv_w", 3 * DC + m), in1=conv[:, m, :], op0=ALU.mult, op1=ALU.add))
                dve.scalar_tensor_tensor(out=conv[:, m, :], in0=b[:, 2:T + 2], scalar=col("conv_w", 6 * DC + m), in1=conv[:, m, :], op0=ALU.mult, op1=ALU.add)\
                   .then_inc(sem("conv_done"), 1)

            def multiply(o, h, step):
                part = slice(h * 512, (h + 1) * 512)
                sign, ka, kb, dst = ((ALU.subtract, k_re, k_im, y_re), (ALU.add, k_im, k_re, y_im))[step // 3]
                dst = dst[:, :, part]
                if step == 0:
                    dve.wait_ge(sem("spectra_landed"), 16)
                    dve.wait_ge(sem("spectrum_copied"), len(SPECTRUM) * o + SP_HALF * (h + 1))
                if step % 3 == 0:
                    link(dve.tensor_tensor(ctmp, u_im[:, :, part], kb[:, :, o, part], ALU.mult))
                elif step % 3 == 1:
                    link(dve.tensor_tensor(dst, u_re[:, :, part], ka[:, :, o, part], ALU.mult))
                else:
                    last = dve.tensor_tensor(dst, dst, ctmp, sign)
                    if step == 5:
                        last.then_inc(sem("yf_ready"), 1)
                        dve.wait_ge(sem("yf_ready"), 2 * o + h + 1)
                    else:
                        link(last)

            for m in range(3 * DC):
                if m:
                    lo_chunk(dve, n0 + m)
                if m >= 2:
                    short_conv(m - 2)
                if 0 <= m - WIN_PRODUCTS < 6:
                    multiply(0, 0, m - WIN_PRODUCTS)
            short_conv(3 * DC - 2)
            short_conv(3 * DC - 1)
            dve.wait_ge(sem("conv_done"), 3 * DC)
            def z_low(c):
                dve.wait_ge(sem("h_hi_ready"), 4 * DC + c + 1)
                dve.tensor_tensor(h_lo[:, c, :], zz[:, c, :], h_hi[:, c, :], ALU.subtract).then_inc(sem("h_lo_ready"), 1)

            for o in range(ORDER):
                for h in range(0 if o else 1, 2):
                    for step in range(6):
                        multiply(o, h, step)
                z = conv if o == 0 else zz
                if o == ORDER - 1:
                    lo_chunk(dve, FIRST["wout"])
                for c in range(DC):
                    dve.wait_ge(sem("yt_ready"), DC * o + c + 1)
                    t = hrt[:, c % 2, :]
                    link(dve.tensor_scalar(t, z[:, c, :], col("hy_bias", o * DC + c), None, ALU.mult))
                    link(dve.scalar_tensor_tensor(out=t, in0=ps[:, 4 + c % 4, 0:T], scalar=inv_norm[:, o * DC + c:o * DC + c + 1], in1=t, op0=ALU.mult, op1=ALU.add))
                    dve.tensor_tensor(zz[:, c, :], t, conv[:, DC * (o + 1) + c, :], ALU.mult).then_inc(sem("z_ready"), 1)
                    if o == ORDER - 1 and c:
                        z_low(c - 1)
                dve.wait_ge(sem("z_ready"), DC * (o + 1))
            z_low(DC - 1)
            residual("wout", 1)
            root(6, T)
            lo_chunk(dve, FIRST["wq1"])
            modulated(6, 5, x[:, :, :], 4, lambda c: mod_col(1, 3, c), h_hi, h_lo)
            retrieval(1)
            root(7, T)
            dve.wait_ge(sem("root_spread"), 8)
            for c in range(DC):
                last = dve.scalar_tensor_tensor(out=x[:, c, :], in0=x[:, c, :], scalar=col("final_g", c), in1=roots(7),
                                                op0=ALU.mult, op1=ALU.mult)
                if c % (DC // 2) == DC // 2 - 1:
                    last.then_inc(sem("result_ready"), 1)


def tables():
    f = np.float32
    inv = (10000.0 ** (-np.arange(ROPE // 4, dtype=f) / f(ROPE // 4))).astype(f)
    t = np.arange(T)
    row, colu = (t // 64).astype(f), (t % 64).astype(f)
    ang = np.concatenate([row[:, None] * inv, row[:, None] * inv, colu[:, None] * inv, colu[:, None] * inv], 1).T
    sign = np.where(np.arange(ROPE) % 16 < 8, -1.0, 1.0)[:, None]
    rope = np.zeros((P, T), f)
    rope[NOPE:QK] = np.cos(ang)
    rope[QK:] = np.sin(ang) * sign
    k = np.arange(T)
    ang = 2 * np.pi * np.outer(k, k + 0.5) / (2 * T)
    def tiles(m):
        return m.reshape(TT, P, T).transpose(1, 0, 2)
    dft = np.stack([tiles(np.cos(ang)), tiles(np.sin(ang)), tiles(np.cos(ang).T / T), tiles(np.sin(ang).T / T)], 1).astype(f)
    bands = (EMB - 1) // 2
    lin = np.linspace(0.0, 1.0, T, dtype=f)
    w = (f(2.0 * math.pi / T) * np.arange(T, dtype=f))[None, :]
    fr = np.linspace(1e-4, bands - 1, bands, dtype=f)[:, None]
    zfeat = np.concatenate([lin[None, :], np.cos(fr * w), -np.sin(fr * w)], 0).astype(f)
    return dict(rope=rope, dft=dft, zfeat=zfeat, ident=np.eye(P, dtype=f), iota=np.broadcast_to(np.arange(P, dtype=f), (P, P)),
                neg_t=-lin.reshape(TT, P).T)


def kernel(**inputs):
    import concourse.bacc as _bacc
    from concourse.bass_utils import run_bass_kernel_spmd as _run

    g = {k: np.asarray(v) for k, v in inputs.items()}
    tab = tables()

    def by_feature(v):
        return v.reshape(-1, P).T

    def by_chunk(w):
        return w.reshape(DC, P, -1, P).transpose(2, 1, 0, 3).reshape(-1, P, D)

    swap = np.concatenate([np.arange(8, 16), np.arange(0, 8), np.arange(24, 32), np.arange(16, 24)])
    ar = {}
    for name in ("x", "ctx"):
        ar[name] = g[name][0].T.reshape(DC, P, T).transpose(1, 0, 2)
    ar["c_pair"] = np.stack([g["c"][0].reshape(DC, P).T, g["c_ctx"].reshape(DC, P).T], 2)
    first = g["mod_w"][0][:, :MODS_FIRST * P].reshape(DC, P, MODS_FIRST, P)
    ar["mod_first_pe"] = first[:, :, :MODS_PE].transpose(1, 2, 0, 3).reshape(P, MODS_PE, D)
    ar["mod_first_dve"] = first[:, :, MODS_PE:].transpose(3, 2, 0, 1).reshape(P, MODS_FIRST - MODS_PE, D)
    ar["mod_w"] = g["mod_w"].reshape(2, D, MODS, P).transpose(0, 2, 3, 1).reshape(2 * MODS, P, D)[MODS_FIRST:]
    parts = {"mix_g": g["norm_mix_g"], "ffn_g": g["norm_ffn_g"], "final_g": g["final_g"], "q_g": g["mla_q_norm_g"][0],
             "kv_g": g["mla_kv_norm_g"][0], "conv_w": g["hy_conv_w"][0], "conv_b": g["hy_conv_b"][0], "hy_bias": g["hy_bias"][0],
             "mod_b": g["mod_b"]}
    ar["cols"] = np.concatenate([by_feature(parts[n]) if n in parts else tab[n] for n in COLS], 1)
    dkv = g["mla_w_dkv"][0]
    key = dkv[:, QL + KVL:]
    dkv = np.concatenate([dkv[:, :QL + KVL], np.zeros((D, NOPE), np.float32), key, key[:, swap]], 1)
    ar["dkv"] = by_chunk(dkv)
    uq = g["mla_w_uq"][0].reshape(QL, HEADS, QK)
    uq = np.concatenate([uq, uq[:, :, NOPE + swap]], 2)
    ar["w_uq"] = uq.reshape(QC, P, HEADS, P).transpose(1, 0, 2, 3)
    ukv = g["mla_w_ukv"][0].reshape(KC, P, HEADS, NOPE + VD).transpose(1, 0, 2, 3)
    ar["w_uk"] = ukv[..., :NOPE].reshape(P, KC, HEADS // 2, P)
    ar["w_uv"] = ukv[..., NOPE:].reshape(P, KC, D)
    ar["wo"], ar["win"], ar["wout"] = by_chunk(g["mla_w_o"][0]), by_chunk(g["hy_w_in"][0]), by_chunk(g["hy_w_out"][0])
    for l in range(2):
        ar[f"wq{l}"] = by_chunk(g["peer_wq"][l])
        ar[f"u{l}"] = g["peer_u"][l].reshape(NK, NK, DC, P).transpose(1, 3, 2, 0).reshape(NK, P, D)
        ar[f"v{l}"] = g["peer_v"][l].reshape(NK, NK, D).transpose(1, 0, 2)
    ar["keys"] = g["peer_keys"].reshape(2, HP, NK, P).transpose(0, 3, 1, 2)
    ar["w4"] = g["hy_w4"][0].reshape(FFN, ORDER, 2, 2, 512)
    ar["delta"] = np.broadcast_to(g["hy_deltas"][0], (P, ORDER, D))
    ar["w1"] = g["hy_w1"][0]
    ar["w23"] = np.concatenate([g["hy_w2"][0], g["hy_w3"][0]], 1)
    ar["fcol"] = np.stack([g["hy_b1"][0], g["hy_b2"][0], g["hy_b3"][0], g["hy_sin_freq"][0]], 1)
    for n in ("rope", "dft", "zfeat", "ident", "iota"):
        ar[n] = tab[n]

    nc = _bacc.Bacc("TRN2", target_bir_lowering=False, num_devices=1)
    arrays, aps = {}, {}
    for name, v in ar.items():
        arrays[f"in_{name}"] = np.ascontiguousarray(v)
        aps[name] = nc.dram_tensor(f"in_{name}", v.shape, F32, kind="ExternalInput").ap()
    out = nc.dram_tensor("out_x", (P, DC, T), F32, kind="ExternalOutput").ap()
    spectra = nc.dram_tensor("spectra", (P, 2, TT, ORDER, D), F32).ap()
    build(nc, aps, spectra, out)
    r = _run(nc, [arrays], core_ids=[0])
    y = r.results[0]["out_x"]
    return np.ascontiguousarray(np.asarray(y).transpose(2, 1, 0).reshape(1, T, D))
```
